# Optimizing a Trainium2 kernel written in Bass

```python
import math
import jax, jax.numpy as jnp
from jax import lax
import numpy as np

D_MODEL = 1024
BATCH = 1
SEQ = 512
DEPTH = 2

GRID_W = 64
CTX_LEN = 256
N_AB = (DEPTH + 1) // 2
N_C = DEPTH // 2
A_HEADS = 8
A_KV_HEADS = 2
A_HEAD_DIM = 64
A_WIDTH = A_HEADS * A_HEAD_DIM
A_KV_WIDTH = A_KV_HEADS * A_HEAD_DIM
WINDOW = 128
Q_BLOCK = WINDOW
ROPE_BASE = 10000.0
B_WIDTH = D_MODEL // 2
CONV_W = 3
AB_IN_WIDTH = 2 * A_WIDTH + 2 * A_KV_WIDTH + 4 * B_WIDTH
AB_OUT_WIDTH = A_WIDTH + B_WIDTH
C_HEADS = 8
C_KEY_DIM = 128
C_VAL_DIM = D_MODEL // C_HEADS
C_F_WIDTH = C_HEADS * C_KEY_DIM
C_I_WIDTH = C_HEADS * C_VAL_DIM
C_IN_WIDTH = 3 * C_F_WIDTH + 2 * C_I_WIDTH
CHUNK = 32
DEEPNORM_ALPHA = (2 * DEPTH) ** 0.25
DEEPNORM_BETA = (8 * DEPTH) ** -0.25
LN_EPS = 1e-5
RMS_EPS = 1e-6


def split_cols(p, widths):
    idx = [int(v) for v in np.cumsum(widths)[:-1]]
    return jnp.split(p, idx, axis=-1)

def layer_norm(x, g, b):
    xf = x.astype(jnp.float32)
    mu = xf.mean(-1, keepdims=True)
    var = jnp.square(xf - mu).mean(-1, keepdims=True)
    return ((xf - mu) * lax.rsqrt(var + LN_EPS) * g + b).astype(x.dtype)

def modulate(h, shift, scale):
    return h * (1 + scale) + shift

def rope_1d(x, pos):
    half = x.shape[-1] // 2
    freqs = ROPE_BASE ** (-jnp.arange(half, dtype=jnp.float32) / half)
    ang = pos.astype(jnp.float32)[:, None] * freqs[None, :]
    cos = jnp.cos(ang)[:, None, :].astype(x.dtype)
    sin = jnp.sin(ang)[:, None, :].astype(x.dtype)
    x1, x2 = x[..., :half], x[..., half:]
    return jnp.concatenate([x1 * cos - x2 * sin, x1 * sin + x2 * cos], axis=-1)

def axial_rope(x, row, col):
    half = x.shape[-1] // 2
    return jnp.concatenate([rope_1d(x[..., :half], row), rope_1d(x[..., half:], col)], axis=-1)

def heads(t, n_heads):
    return t.reshape(t.shape[0], t.shape[1], n_heads, A_HEAD_DIM)

def short_conv(u, w):
    pad = CONV_W // 2
    L = u.shape[1]
    up = jnp.pad(u, ((0, 0), (pad, pad), (0, 0)))
    y = up[:, 0:L] * w[0]
    for j in range(1, CONV_W):
        y = y + up[:, j:j + L] * w[j]
    return y

def window_attention(q, k, v, kc, vc, sink):
    B, L = q.shape[:2]
    n_blk = L // Q_BLOCK
    G = A_HEADS // A_KV_HEADS
    scale = A_HEAD_DIM ** -0.5
    lc = kc.shape[1]
    span = Q_BLOCK + 2 * WINDOW
    qb = q.reshape(B, n_blk, Q_BLOCK, A_KV_HEADS, G, A_HEAD_DIM).swapaxes(0, 1)
    kp = jnp.pad(k, ((0, 0), (WINDOW, WINDOW), (0, 0), (0, 0)))
    vp = jnp.pad(v, ((0, 0), (WINDOW, WINDOW), (0, 0), (0, 0)))
    rel = jnp.arange(span)[None, :] - WINDOW - jnp.arange(Q_BLOCK)[:, None]
    in_win = jnp.abs(rel) <= WINDOW
    sink_l = jnp.broadcast_to(sink.astype(jnp.float32).reshape(1, A_KV_HEADS, G, 1, 1),
                              (B, A_KV_HEADS, G, Q_BLOCK, 1))

    def one_block(args):
        n, q_n = args
        start = n * Q_BLOCK
        k_n = lax.dynamic_slice_in_dim(kp, start, span, axis=1)
        v_n = lax.dynamic_slice_in_dim(vp, start, span, axis=1)
        key_pos = start - WINDOW + jnp.arange(span)
        valid = in_win & ((key_pos >= 0) & (key_pos < L))[None, :]
        s_loc = jnp.einsum('bikgd,bjkd->bkgij', q_n, k_n).astype(jnp.float32) * scale
        s_loc = jnp.where(valid, s_loc, -jnp.inf)
        s_ctx = jnp.einsum('bikgd,bjkd->bkgij', q_n, kc).astype(jnp.float32) * scale
        p = jax.nn.softmax(jnp.concatenate([sink_l, s_ctx, s_loc], axis=-1), axis=-1).astype(v.dtype)
        return (jnp.einsum('bkgij,bjkd->bikgd', p[..., 1:1 + lc], vc)
                + jnp.einsum('bkgij,bjkd->bikgd', p[..., 1 + lc:], v_n))

    out = lax.map(one_block, (jnp.arange(n_blk), qb))
    return out.swapaxes(0, 1).reshape(B, L, A_WIDTH)

def context_attention(qc, kc, vc, sink):
    B, lc = qc.shape[:2]
    G = A_HEADS // A_KV_HEADS
    q = qc.reshape(B, lc, A_KV_HEADS, G, A_HEAD_DIM)
    s = jnp.einsum('bikgd,bjkd->bkgij', q, kc).astype(jnp.float32) * (A_HEAD_DIM ** -0.5)
    sink_l = jnp.broadcast_to(sink.astype(jnp.float32).reshape(1, A_KV_HEADS, G, 1, 1),
                              (B, A_KV_HEADS, G, lc, 1))
    p = jax.nn.softmax(jnp.concatenate([sink_l, s], axis=-1), axis=-1).astype(vc.dtype)
    return jnp.einsum('bkgij,bjkd->bikgd', p[..., 1:], vc).reshape(B, lc, A_WIDTH)

def ab_layer(x, xc, mod, mod_c, w_in, w_out, sink, conv_w, ln_g, ln_b, row, col, ctx_out):
    shift, scale, gate = jnp.split(mod, 3, axis=-1)
    shift_c, scale_c, gate_c = jnp.split(mod_c, 3, axis=-1)
    widths = (A_WIDTH, A_KV_WIDTH, A_KV_WIDTH, A_WIDTH, B_WIDTH, B_WIDTH, B_WIDTH, B_WIDTH)
    q, k, v, g_a, xb, b_g, c_g, g_b = split_cols(modulate(x, shift, scale) @ w_in, widths)
    hc = modulate(xc, shift_c, scale_c)
    if ctx_out:
        qc, kc, vc, g_ac, xbc, b_gc, c_gc, g_bc = split_cols(hc @ w_in, widths)
    else:
        kc, vc = split_cols(hc @ w_in[:, A_WIDTH:A_WIDTH + 2 * A_KV_WIDTH], (A_KV_WIDTH, A_KV_WIDTH))
    kc, vc = heads(kc, A_KV_HEADS), heads(vc, A_KV_HEADS)
    q = axial_rope(heads(q, A_HEADS), row, col)
    k = axial_rope(heads(k, A_KV_HEADS), row, col)
    o_a = window_attention(q, k, heads(v, A_KV_HEADS), kc, vc, sink)
    o_b = b_g * short_conv(c_g * xb, conv_w)
    y = jnp.concatenate([o_a * jax.nn.silu(g_a), o_b * jax.nn.silu(g_b)], axis=-1) @ w_out
    x_new = layer_norm(DEEPNORM_ALPHA * x + gate * y, ln_g, ln_b)
    if not ctx_out:
        return x_new, None
    o_ac = context_attention(heads(qc, A_HEADS), kc, vc, sink)
    o_bc = b_gc * short_conv(c_gc * xbc, conv_w)
    yc = jnp.concatenate([o_ac * jax.nn.silu(g_ac), o_bc * jax.nn.silu(g_bc)], axis=-1) @ w_out
    xc_new = layer_norm(DEEPNORM_ALPHA * xc + gate_c * yc, ln_g, ln_b)
    return x_new, xc_new

def to_heads(t, d):
    B, L, _ = t.shape
    return t.reshape(B, L, -1, d).transpose(0, 2, 1, 3).astype(jnp.float32)

def forget_terms(z, lb):
    lb = jnp.clip(lb.astype(jnp.float32), 0.0, 1.0).reshape(C_HEADS, 1, C_KEY_DIM)
    log_f = jnp.logaddexp(jnp.log(lb), jnp.log1p(-lb) + jax.nn.log_sigmoid(z))
    k = (1 - lb) * jax.nn.sigmoid(-z)
    return k, log_f

def hgrn2_scan(q, k, v, log_f, s0, with_outputs):
    B, H, L, dk = k.shape
    n = L // CHUNK
    chunks = lambda t: t.reshape(B, H, n, CHUNK, t.shape[-1])
    to_scan = lambda t: jnp.moveaxis(t, 2, 0)
    k, v, log_f = chunks(k), chunks(v), chunks(log_f)
    b = jnp.cumsum(log_f, axis=3)
    b_last = b[:, :, :, -1:, :]
    k_state = k * jnp.exp(b_last - b)
    decay = jnp.exp(b_last[:, :, :, 0, :])
    if with_outputs:
        q = chunks(q)
        q_inter = q * jnp.exp(b)
        tri = jnp.tril(jnp.ones((CHUNK, CHUNK), dtype=bool))[:, :, None]

        def step(s, xs):
            q_n, k_n, v_n, b_n, qi_n, ks_n, d_n = xs
            o_inter = jnp.einsum('bhcd,bhde->bhce', qi_n, s)
            diff = b_n[:, :, :, None, :] - b_n[:, :, None, :, :]
            w = jnp.exp(jnp.where(tri, diff, -jnp.inf))
            scores = jnp.einsum('bhcd,bhsd,bhcsd->bhcs', q_n, k_n, w)
            o_n = o_inter + jnp.einsum('bhcs,bhse->bhce', scores, v_n)
            return d_n[..., None] * s + jnp.einsum('bhcd,bhce->bhde', ks_n, v_n), o_n

        s_final, o = lax.scan(step, s0, (to_scan(q), to_scan(k), to_scan(v), to_scan(b),
                                         to_scan(q_inter), to_scan(k_state), to_scan(decay)))
        o = jnp.moveaxis(o, 0, 2).reshape(B, H, L, v.shape[-1])
        return o, s_final

    def step_state(s, xs):
        k_n, v_n, d_n = xs
        return d_n[..., None] * s + jnp.einsum('bhcd,bhce->bhde', k_n, v_n), None

    s_final, _ = lax.scan(step_state, s0, (to_scan(k_state), to_scan(v), to_scan(decay)))
    return None, s_final

def hgrn2_direction(q, i, z, lb, qc, ic, zc, ctx_out, reverse):
    flip = (lambda t: jnp.flip(t, axis=2)) if reverse else (lambda t: t)
    B = i.shape[0]
    kc, lfc = forget_terms(zc, lb)
    s0 = jnp.zeros((B, C_HEADS, C_KEY_DIM, C_VAL_DIM), jnp.float32)
    oc, s_ctx = hgrn2_scan(flip(qc) if ctx_out else None, flip(kc), flip(ic), flip(lfc), s0, ctx_out)
    k, lf = forget_terms(z, lb)
    o, _ = hgrn2_scan(flip(q), flip(k), flip(i), flip(lf), s_ctx, True)
    return flip(o), (flip(oc) if ctx_out else None)

def hgrn2_readout(o, g, g_norm, w_out):
    on = o * lax.rsqrt(jnp.mean(o * o, axis=-1, keepdims=True) + RMS_EPS) * g_norm
    B, H, L, dv = on.shape
    return (on.transpose(0, 2, 1, 3).reshape(B, L, H * dv).astype(g.dtype) * jax.nn.silu(g)) @ w_out

def c_layer(x, xc, mod, mod_c, w_in, w_out, lb_f, lb_b, g_norm, ln_g, ln_b, ctx_out):
    shift, scale, gate = jnp.split(mod, 3, axis=-1)
    shift_c, scale_c, gate_c = jnp.split(mod_c, 3, axis=-1)
    widths = (C_F_WIDTH, C_F_WIDTH, C_F_WIDTH, C_I_WIDTH, C_I_WIDTH)
    q, zf, zb, i, g = split_cols(modulate(x, shift, scale) @ w_in, widths)
    hc = modulate(xc, shift_c, scale_c)
    if ctx_out:
        qc, zfc, zbc, ic, gc = split_cols(hc @ w_in, widths)
        qc = jax.nn.silu(to_heads(qc, C_KEY_DIM)) * (C_KEY_DIM ** -0.5)
    else:
        zfc, zbc, ic = split_cols(hc @ w_in[:, C_F_WIDTH:3 * C_F_WIDTH + C_I_WIDTH],
                                  (C_F_WIDTH, C_F_WIDTH, C_I_WIDTH))
        qc = None
    q = jax.nn.silu(to_heads(q, C_KEY_DIM)) * (C_KEY_DIM ** -0.5)
    i, zf, zb = to_heads(i, C_VAL_DIM), to_heads(zf, C_KEY_DIM), to_heads(zb, C_KEY_DIM)
    ic, zfc, zbc = to_heads(ic, C_VAL_DIM), to_heads(zfc, C_KEY_DIM), to_heads(zbc, C_KEY_DIM)
    o_f, oc_f = hgrn2_direction(q, i, zf, lb_f, qc, ic, zfc, ctx_out, reverse=False)
    o_b, oc_b = hgrn2_direction(q, i, zb, lb_b, qc, ic, zbc, ctx_out, reverse=True)
    y = hgrn2_readout(o_f + o_b, g, g_norm, w_out)
    x_new = layer_norm(DEEPNORM_ALPHA * x + gate * y, ln_g, ln_b)
    if not ctx_out:
        return x_new, None
    yc = hgrn2_readout(oc_f + oc_b, gc, g_norm, w_out)
    xc_new = layer_norm(DEEPNORM_ALPHA * xc + gate_c * yc, ln_g, ln_b)
    return x_new, xc_new

def first_inputs(seed: int = 0) -> dict:
    key = jax.random.key(seed)
    ks = jax.random.split(key, 16)
    nrm = lambda k, shape, s: jax.random.normal(k, shape, jnp.float32) * s
    ab_col_scale = jnp.concatenate([
        jnp.ones((A_WIDTH + A_KV_WIDTH,), jnp.float32),
        jnp.full((A_KV_WIDTH,), DEEPNORM_BETA, jnp.float32),
        jnp.ones((A_WIDTH + 4 * B_WIDTH,), jnp.float32)])
    c_col_scale = jnp.concatenate([
        jnp.ones((3 * C_F_WIDTH,), jnp.float32),
        jnp.full((C_I_WIDTH,), DEEPNORM_BETA, jnp.float32),
        jnp.ones((C_I_WIDTH,), jnp.float32)])
    return {
        "x": nrm(ks[0], (BATCH, SEQ, D_MODEL), 1.0),
        "c": nrm(ks[1], (BATCH, D_MODEL), 1.0),
        "ctx": nrm(ks[2], (BATCH, CTX_LEN, D_MODEL), 1.0),
        "c_ctx": nrm(ks[3], (D_MODEL,), 1.0),
        "w_ada": nrm(ks[4], (DEPTH, D_MODEL, 3 * D_MODEL), D_MODEL ** -0.5),
        "b_ada": nrm(ks[5], (DEPTH, 3 * D_MODEL), 0.02),
        "ln_g": 1.0 + nrm(ks[6], (DEPTH, D_MODEL), 0.02),
        "ln_b": nrm(ks[7], (DEPTH, D_MODEL), 0.02),
        "w_in_ab": nrm(ks[8], (N_AB, D_MODEL, AB_IN_WIDTH), D_MODEL ** -0.5) * ab_col_scale,
        "w_out_ab": nrm(ks[9], (N_AB, AB_OUT_WIDTH, D_MODEL), AB_OUT_WIDTH ** -0.5 * DEEPNORM_BETA),
        "sink_ab": nrm(ks[10], (N_AB, A_HEADS), 0.5),
        "conv_ab": nrm(ks[11], (N_AB, CONV_W, B_WIDTH), CONV_W ** -0.5),
        "w_in_c": nrm(ks[12], (N_C, D_MODEL, C_IN_WIDTH), D_MODEL ** -0.5) * c_col_scale,
        "w_out_c": nrm(ks[13], (N_C, C_I_WIDTH, D_MODEL), C_I_WIDTH ** -0.5 * DEEPNORM_BETA),
        "lb_c": nrm(ks[14], (2, N_C, C_F_WIDTH), 0.5),
        "gnorm_c": 1.0 + nrm(ks[15], (N_C, C_VAL_DIM), 0.02),
    }

def first_block(x, c, ctx, c_ctx, w_ada, b_ada, ln_g, ln_b, w_in_ab, w_out_ab, sink_ab, conv_ab,
              w_in_c, w_out_c, lb_c, gnorm_c):
    L = x.shape[1]
    rows = L // GRID_W
    row = jnp.repeat(jnp.arange(rows), GRID_W)
    col = jnp.tile(jnp.arange(GRID_W), rows)
    lb_p = jax.nn.softmax(lb_c.astype(jnp.float32), axis=1)
    lb_all = jnp.cumsum(lb_p, axis=1) - lb_p[:, :1]
    silu_c = jax.nn.silu(c)
    silu_cc = jax.nn.silu(c_ctx)
    xc = ctx
    for l in range(DEPTH):
        mod = (silu_c @ w_ada[l] + b_ada[l])[:, None, :]
        mod_c = silu_cc @ w_ada[l] + b_ada[l]
        ctx_out = l < DEPTH - 1
        j = l // 2
        if l % 2 == 0:
            x, xc = ab_layer(x, xc, mod, mod_c, w_in_ab[j], w_out_ab[j], sink_ab[j], conv_ab[j],
                             ln_g[l], ln_b[l], row, col, ctx_out)
        else:
            x, xc = c_layer(x, xc, mod, mod_c, w_in_c[j], w_out_c[j], lb_all[0, j], lb_all[1, j],
                            gnorm_c[j], ln_g[l], ln_b[l], ctx_out)
    return x


HEAD_DIM = 64
N_ATTN_HEADS = 8
N_KV_GROUPS = 2
GQA_RATIO = N_ATTN_HEADS // N_KV_GROUPS
ATTN_WIDTH = N_ATTN_HEADS * HEAD_DIM
N_MLP_GROUPS = 8
MLP_WIDTH = N_MLP_GROUPS * HEAD_DIM
MIX_WIDTH = ATTN_WIDTH + MLP_WIDTH
KV_WIDTH = N_KV_GROUPS * HEAD_DIM
N_BRANCH = 3
GATE_WIDTH = N_ATTN_HEADS * N_BRANCH
IN_SIZES = [ATTN_WIDTH] + [KV_WIDTH] * 6 + [GATE_WIDTH, MLP_WIDTH, MLP_WIDTH]
IN_WIDTH = ATTN_WIDTH + 6 * KV_WIDTH + GATE_WIDTH + 2 * MLP_WIDTH
ROT_DIM = HEAD_DIM // 4
ROPE_THETA = 500000.0
CMP_LEN = 32
CMP_STRIDE = 16
CMP_HIDDEN = 256
SEL_LEN = 64
N_SELECT = 16
WINDOW_2 = 512
Q_BLOCK_2 = 128
CHUNK_2 = 128
D_FF = 2816
CONV_WIDTH = 3
PLE_DIM = 256
NORM_EPS = 1e-6
NEG = -1e30
FORCED = 1e9


def rms_norm(x, gain):
    xf = x.astype(jnp.float32)
    y = xf * lax.rsqrt(jnp.mean(xf * xf, axis=-1, keepdims=True) + NORM_EPS)
    return (y * gain.astype(jnp.float32)).astype(x.dtype)

def layer_norm_2(x, gain, bias):
    xf = x.astype(jnp.float32)
    mu = jnp.mean(xf, axis=-1, keepdims=True)
    var = jnp.mean(jnp.square(xf - mu), axis=-1, keepdims=True)
    y = (xf - mu) * lax.rsqrt(var + NORM_EPS) * gain.astype(jnp.float32) + bias.astype(jnp.float32)
    return y.astype(x.dtype)

def rope_partial(x, pos):
    half = ROT_DIM // 2
    inv = ROPE_THETA ** (-jnp.arange(half, dtype=jnp.float32) / half)
    ang = pos.astype(jnp.float32)[:, None] * inv[None, :]
    cos = jnp.cos(ang)[:, None, :]
    sin = jnp.sin(ang)[:, None, :]
    xr = x[..., :ROT_DIM].astype(jnp.float32)
    x1, x2 = xr[..., :half], xr[..., half:]
    rot = jnp.concatenate([x1 * cos - x2 * sin, x2 * cos + x1 * sin], axis=-1).astype(x.dtype)
    return jnp.concatenate([rot, x[..., ROT_DIM:]], axis=-1)

def masked_softmax(s, mask):
    s = jnp.where(mask, s, NEG)
    m = jnp.max(s, axis=-1, keepdims=True)
    e = jnp.exp(s - m) * mask
    return e / jnp.maximum(jnp.sum(e, axis=-1, keepdims=True), 1e-30)

def compress(t, pe, w1, b1, w2, b2):
    B, S, G, D = t.shape
    r = CMP_LEN // CMP_STRIDE
    nch = S // CMP_STRIDE
    nc = nch - r + 1
    ch = t.reshape(B, nch, CMP_STRIDE, G, D)
    blocks = jnp.concatenate([ch[:, j:j + nc] for j in range(r)], axis=2)
    blocks = blocks + pe[None, None, :, None, :]
    flat = blocks.transpose(0, 1, 3, 2, 4).reshape(B, nc, G, CMP_LEN * D)
    h = jax.nn.gelu(flat @ w1 + b1)
    return h @ w2 + b2

def nsa_attention(q, kc, vc, ks, vs, kw, vw, gates):
    B, S, H, D = q.shape
    G = kc.shape[2]
    R = H // G
    nc = kc.shape[1]
    ns = S // SEL_LEN
    n_sel = min(N_SELECT, ns)
    scale = D ** -0.5
    cmp_start = jnp.arange(nc) * CMP_STRIDE
    cmp_end = cmp_start + CMP_LEN - 1
    sel_start = jnp.arange(ns) * SEL_LEN
    overlap = ((cmp_end[:, None] >= sel_start[None, :]) &
               (cmp_start[:, None] <= sel_start[None, :] + SEL_LEN - 1)).astype(jnp.float32)
    ks_blk = ks.reshape(B, ns, SEL_LEN, G, D).transpose(0, 3, 1, 2, 4)
    vs_blk = vs.reshape(B, ns, SEL_LEN, G, D).transpose(0, 3, 1, 2, 4)
    kw_pad = jnp.pad(kw, ((0, 0), (WINDOW_2, 0), (0, 0), (0, 0)))
    vw_pad = jnp.pad(vw, ((0, 0), (WINDOW_2, 0), (0, 0), (0, 0)))
    qg = q.reshape(B, S, G, R, D)
    gg = gates.reshape(B, S, G, R, N_BRANCH)
    bi = jnp.arange(B)[:, None, None, None]
    gi = jnp.arange(G)[None, :, None, None]
    blk = jnp.arange(ns)
    f32 = jnp.float32

    def block(qi):
        t0 = qi * Q_BLOCK_2
        tq = t0 + jnp.arange(Q_BLOCK_2)
        qb = lax.dynamic_slice_in_dim(qg, t0, Q_BLOCK_2, axis=1)
        gb = lax.dynamic_slice_in_dim(gg, t0, Q_BLOCK_2, axis=1)
        s_c = jnp.einsum('bqgrd,bngd->bgrqn', qb, kc, preferred_element_type=f32) * scale
        p_c = masked_softmax(s_c, cmp_end[None, :] <= tq[:, None])
        o_c = jnp.einsum('bgrqn,bngd->bqgrd', p_c.astype(vc.dtype), vc)
        imp = jnp.einsum('bgrqn,nj->bgqj', p_c, overlap)
        cur = tq // SEL_LEN
        valid = blk[None, :] <= cur[:, None]
        forced = valid & ((blk[None, :] == 0) | (blk[None, :] == cur[:, None]) | (blk[None, :] == cur[:, None] - 1))
        score = jnp.where(forced, FORCED, jnp.where(valid, imp, NEG))
        vals, idx = lax.top_k(score, n_sel)
        sel_ok = vals > NEG * 0.5
        k_g = ks_blk[bi, gi, idx].reshape(B, G, Q_BLOCK_2, n_sel * SEL_LEN, D)
        v_g = vs_blk[bi, gi, idx].reshape(B, G, Q_BLOCK_2, n_sel * SEL_LEN, D)
        kpos = idx[..., None] * SEL_LEN + jnp.arange(SEL_LEN)
        mask_s = ((kpos <= tq[:, None, None]) & sel_ok[..., None]).reshape(B, G, Q_BLOCK_2, n_sel * SEL_LEN)
        s_s = jnp.einsum('bqgrd,bgqkd->bgrqk', qb, k_g, preferred_element_type=f32) * scale
        p_s = masked_softmax(s_s, mask_s[:, :, None])
        o_s = jnp.einsum('bgrqk,bgqkd->bqgrd', p_s.astype(v_g.dtype), v_g)
        kwb = lax.dynamic_slice_in_dim(kw_pad, t0, Q_BLOCK_2 + WINDOW_2, axis=1)
        vwb = lax.dynamic_slice_in_dim(vw_pad, t0, Q_BLOCK_2 + WINDOW_2, axis=1)
        kpos_w = t0 - WINDOW_2 + jnp.arange(Q_BLOCK_2 + WINDOW_2)
        mask_w = ((kpos_w[None, :] <= tq[:, None]) & (kpos_w[None, :] > tq[:, None] - WINDOW_2)
                  & (kpos_w[None, :] >= 0))
        s_w = jnp.einsum('bqgrd,bkgd->bgrqk', qb, kwb, preferred_element_type=f32) * scale
        p_w = masked_softmax(s_w, mask_w)
        o_w = jnp.einsum('bgrqk,bkgd->bqgrd', p_w.astype(vwb.dtype), vwb)
        o = gb[..., 0:1] * o_c + gb[..., 1:2] * o_s + gb[..., 2:3] * o_w
        return o.reshape(B, Q_BLOCK_2, H * D)

    out = lax.map(block, jnp.arange(S // Q_BLOCK_2))
    return out.transpose(1, 0, 2, 3).reshape(B, S, H * D)

def spatial_gating(u, v, ln_g, ln_b, w_s, b_s):
    B, S, _ = u.shape
    u = jax.nn.gelu(u)
    v = layer_norm_2(jax.nn.gelu(v), ln_g, ln_b)
    vc = v.reshape(B, S // CHUNK_2, CHUNK_2, N_MLP_GROUPS, HEAD_DIM)
    causal = jnp.tril(jnp.ones((CHUNK_2, CHUNK_2), dtype=bool))
    ws = jnp.where(causal[None], w_s, 0)
    mixed = jnp.einsum('gts,bcsgd->bctgd', ws, vc) + b_s.T[None, None, :, :, None]
    return u * mixed.reshape(B, S, MLP_WIDTH)

def conv_ffn(x, w_up, conv_w, conv_b, w_down):
    S = x.shape[1]
    h = x @ w_up
    hp = jnp.pad(h, ((0, 0), (CONV_WIDTH - 1, 0), (0, 0)))
    hc = conv_b
    for k in range(CONV_WIDTH):
        hc = hc + hp[:, k:k + S] * conv_w[k]
    g, up = jnp.split(hc, 2, axis=-1)
    return (jax.nn.silu(g) * up) @ w_down

def second_inputs(seed: int = 0) -> dict:
    key = jax.random.key(seed)
    ks = jax.random.split(key, 32)
    L = DEPTH

    def nrm(k, shape, scale):
        return jax.random.normal(k, shape, dtype=jnp.float32) * scale

    def gain(k, shape):
        return 1.0 + nrm(k, shape, 0.05)

    return {
        "x": nrm(ks[0], (BATCH, SEQ, D_MODEL), 1.0),
        "p": nrm(ks[1], (DEPTH, BATCH, SEQ, PLE_DIM), 1.0),
        "pre_mix_g": gain(ks[2], (L, D_MODEL)),
        "w_in": nrm(ks[3], (L, D_MODEL, IN_WIDTH), D_MODEL ** -0.5),
        "cmp_pe": nrm(ks[4], (L, 2, CMP_LEN, HEAD_DIM), 0.1),
        "cmp_w1": nrm(ks[5], (L, 2, CMP_LEN * HEAD_DIM, CMP_HIDDEN), (CMP_LEN * HEAD_DIM) ** -0.5),
        "cmp_b1": nrm(ks[6], (L, 2, CMP_HIDDEN), 0.02),
        "cmp_w2": nrm(ks[7], (L, 2, CMP_HIDDEN, HEAD_DIM), CMP_HIDDEN ** -0.5),
        "cmp_b2": nrm(ks[8], (L, 2, HEAD_DIM), 0.02),
        "gmlp_ln_g": gain(ks[9], (L, MLP_WIDTH)),
        "gmlp_ln_b": nrm(ks[10], (L, MLP_WIDTH), 0.02),
        "gmlp_ws": nrm(ks[11], (L, N_MLP_GROUPS, CHUNK_2, CHUNK_2), 0.5 * CHUNK_2 ** -0.5),
        "gmlp_bs": 1.0 + nrm(ks[12], (L, N_MLP_GROUPS, CHUNK_2), 0.1),
        "attn_out_g": gain(ks[13], (L, ATTN_WIDTH)),
        "mlp_out_g": gain(ks[14], (L, MLP_WIDTH)),
        "w_o": nrm(ks[15], (L, MIX_WIDTH, D_MODEL), MIX_WIDTH ** -0.5),
        "post_mix_g": gain(ks[16], (L, D_MODEL)),
        "pre_ffn_g": gain(ks[17], (L, D_MODEL)),
        "w_up": nrm(ks[18], (L, D_MODEL, 2 * D_FF), D_MODEL ** -0.5),
        "conv_w": nrm(ks[19], (L, CONV_WIDTH, 2 * D_FF), CONV_WIDTH ** -0.5),
        "conv_b": nrm(ks[20], (L, 2 * D_FF), 0.02),
        "w_down": nrm(ks[21], (L, D_FF, D_MODEL), D_FF ** -0.5),
        "post_ffn_g": gain(ks[22], (L, D_MODEL)),
        "ple_norm_g": gain(ks[23], (L, D_MODEL)),
        "w_ple_gate": nrm(ks[24], (L, D_MODEL, D_MODEL), D_MODEL ** -0.5),
        "w_ple_proj": nrm(ks[25], (L, PLE_DIM, D_MODEL), PLE_DIM ** -0.5),
    }

def second_block(x, p, pre_mix_g, w_in, cmp_pe, cmp_w1, cmp_b1, cmp_w2, cmp_b2,
              gmlp_ln_g, gmlp_ln_b, gmlp_ws, gmlp_bs, attn_out_g, mlp_out_g, w_o,
              post_mix_g, pre_ffn_g, w_up, conv_w, conv_b, w_down, post_ffn_g,
              ple_norm_g, w_ple_gate, w_ple_proj):
    B, S, _ = x.shape
    pos = jnp.arange(S)
    split_at = [int(o) for o in np.cumsum(IN_SIZES)[:-1]]
    nc = S // CMP_STRIDE - CMP_LEN // CMP_STRIDE + 1
    cmp_pos = jnp.arange(nc) * CMP_STRIDE + CMP_LEN - 1
    h = x
    for i in range(DEPTH):
        a = rms_norm(h, pre_mix_g[i])
        z = a @ w_in[i]
        zq, zkc, zvc, zks, zvs, zkw, zvw, zg, zu, zv = jnp.split(z, split_at, axis=-1)
        kv = lambda t: t.reshape(B, S, N_KV_GROUPS, HEAD_DIM)
        q = rope_partial(zq.reshape(B, S, N_ATTN_HEADS, HEAD_DIM), pos)
        kc = compress(kv(zkc), cmp_pe[i, 0], cmp_w1[i, 0], cmp_b1[i, 0], cmp_w2[i, 0], cmp_b2[i, 0])
        vc = compress(kv(zvc), cmp_pe[i, 1], cmp_w1[i, 1], cmp_b1[i, 1], cmp_w2[i, 1], cmp_b2[i, 1])
        kc = rope_partial(kc, cmp_pos)
        k_sel = rope_partial(kv(zks), pos)
        k_win = rope_partial(kv(zkw), pos)
        gates = jax.nn.sigmoid(zg.reshape(B, S, N_ATTN_HEADS, N_BRANCH))
        attn = nsa_attention(q, kc, vc, k_sel, kv(zvs), k_win, kv(zvw), gates)
        mlp = spatial_gating(zu, zv, gmlp_ln_g[i], gmlp_ln_b[i], gmlp_ws[i], gmlp_bs[i])
        mix = jnp.concatenate([rms_norm(attn, attn_out_g[i]), rms_norm(mlp, mlp_out_g[i])], axis=-1) @ w_o[i]
        h = h + rms_norm(mix, post_mix_g[i])
        f = conv_ffn(rms_norm(h, pre_ffn_g[i]), w_up[i], conv_w[i], conv_b[i], w_down[i])
        h = h + rms_norm(f, post_ffn_g[i])
        gate = jax.nn.sigmoid(rms_norm(h, ple_norm_g[i]) @ w_ple_gate[i])
        h = h + gate * (p[i] @ w_ple_proj[i])
    return h


def setup_inputs(seed=0):
    out = dict(first_inputs(seed))
    for name, value in second_inputs(seed + 1).items():
        if name != "x":
            out[name + "_2"] = value
    return out


def reference(
    x, c, ctx, c_ctx, w_ada, b_ada, ln_g, ln_b, w_in_ab, w_out_ab, sink_ab, conv_ab, w_in_c,
    w_out_c, lb_c, gnorm_c, p_2, pre_mix_g_2, w_in_2, cmp_pe_2, cmp_w1_2, cmp_b1_2, cmp_w2_2,
    cmp_b2_2, gmlp_ln_g_2, gmlp_ln_b_2, gmlp_ws_2, gmlp_bs_2, attn_out_g_2, mlp_out_g_2, w_o_2,
    post_mix_g_2, pre_ffn_g_2, w_up_2, conv_w_2, conv_b_2, w_down_2, post_ffn_g_2, ple_norm_g_2,
    w_ple_gate_2, w_ple_proj_2,
):
    x = first_block(
        x, c, ctx, c_ctx, w_ada, b_ada, ln_g, ln_b, w_in_ab, w_out_ab, sink_ab, conv_ab, w_in_c,
        w_out_c, lb_c, gnorm_c,
    )
    return second_block(
        x, p_2, pre_mix_g_2, w_in_2, cmp_pe_2, cmp_w1_2, cmp_b1_2, cmp_w2_2, cmp_b2_2,
        gmlp_ln_g_2, gmlp_ln_b_2, gmlp_ws_2, gmlp_bs_2, attn_out_g_2, mlp_out_g_2, w_o_2,
        post_mix_g_2, pre_ffn_g_2, w_up_2, conv_w_2, conv_b_2, w_down_2, post_ffn_g_2,
        ple_norm_g_2, w_ple_gate_2, w_ple_proj_2,
    )


_drawn_inputs = setup_inputs


def setup_inputs(seed=0):
    import zlib

    import numpy as np

    out = dict(_drawn_inputs(seed))
    spreads = {}
    factors = {'ctx': 4.593,
     'sink_ab': 64.0,
     'gnorm_c': 8.0,
     'cmp_b1_2': 3.194,
     'gmlp_ln_g_2': 4.847,
     'gmlp_ln_b_2': 24.143,
     'conv_b_2': 2.672,
     'ple_norm_g_2': 7.341,
     'cmp_b2_2': 2.941}
    for name, (base, spread) in spreads.items():
        noise = np.random.default_rng([zlib.crc32(name.encode()), seed]).standard_normal(out[name].shape)
        drawn = base * np.exp(spread * noise) if base else spread * noise
        out[name] = __import__('jax').numpy.asarray(drawn.astype(out[name].dtype))
    for name, factor in factors.items():
        out[name] = (out[name] * factor).astype(out[name].dtype)
    return out
```

```python
import numpy as np
from contextlib import ExitStack
import concourse.bass as bass
from concourse import mybir

P = 128
D = 1024
L = 512
LC = 256
T = L + LC
KT = D // P
HD = 64
NH = 8
NT4 = 4
NB = L // P
CH = 8
LEV = 7
FF = 2816
FT = FF // P
NCMP = 31
UNIT = 2048
RING = 3
ALPHA = 4 ** 0.25
LN_EPS = 1e-5
RMS_EPS = 1e-6
NEG = -1e30
ASCALE = HD ** -0.5
KSCALE = P ** -0.5

SEG1 = [("ada0", 12), ("ab_in", 13), ("ab_out", 4), ("ada1", 12), ("c_in", 20), ("c_out", 4)]
SEG2 = [("in2", 9), ("cmp1", 4), ("wo", 4), ("up", FT), ("down", 12), ("pleg", 4), ("plep", 1)]


def first_units(seg):
    at, out = 0, {}
    for name, n in seg:
        out[name] = at
        at += n
    return out, at


U1, NU1 = first_units(SEG1)
U2, NU2 = first_units(SEG2)


def columns(parts):
    at, out = 0, {}
    for name, n in parts:
        out[name] = (at, at + n)
        at += n
    return out, at


V1, NV1 = columns([("c", 8), ("cc", 8), ("b_ada0", 24), ("b_ada1", 24), ("ln_g0", 8), ("ln_b0", 8), ("ln_g1", 8),
                   ("ln_b1", 8), ("conv", 12), ("gnorm", 1)])
V2, NV2 = columns([("pre_mix", 8), ("pe", 32), ("b1", 4), ("b2k", 1), ("attn_g", 4), ("mlp_g", 4), ("post_mix", 8),
                   ("pre_ffn", 8), ("cw", 3 * 2 * FT), ("cb", 2 * FT), ("post_ffn", 8), ("ple_g", 8)])
R2, NR2 = columns([("ln_g", 512), ("ln_b", 512), ("b2v", 64), ("bs", NT4 * P), ("w2k", 2 * P), ("w2v", 2 * HD)])
CF, NCF = columns([("ident", P), ("ones", P), ("r1", P), ("r2", P), ("reset", L), ("one", LC), ("eps", 2)])
CG, NCG = columns([("tri", P), ("cos2", L), ("sin2", L), ("cosc", 64), ("sinc", 64)])
CA, NCA = columns([("cos1", L), ("sin1", L)])
CB, NCB = columns([("ident", P), ("up", P), ("low", P), ("cmp", NB * 32), ("scan", 2 * 8 * P)])


class Sems:
    def __init__(self, nc, es, tag):
        def sem(name):
            return es.enter_context(nc.semaphore(f"{name}_{tag}"))

        self.load = sem("load")
        self.load2 = sem("load2")
        self.store = sem("store")
        self.act_step = sem("act_step")
        self.dve_step = sem("dve_step")
        self.pe_tile = sem("pe_tile")
        self.act_out = sem("act_out")
        self.dve_out = sem("dve_out")
        self.scores = sem("scores")
        self.shift = sem("shift")
        self.probs = sem("probs")
        self.normed = sem("normed")
        self.flipped = sem("flipped")
        self.copied = sem("copied")
        self.mixed = sem("mixed")
        self.squares = sem("squares")
        self.sums = sem("sums")
        self.ready = sem("ready")
        self.decays = sem("decays")
        self.absolute = sem("absolute")
        self.log_k = sem("log_k")
        self.exponents = sem("exponents")
        self.weights = sem("weights")
        self.state_keys = sem("state_keys")
        self.levelled = sem("levelled")
        self.own = sem("own")
        self.products = sem("products")
        self.masked = sem("masked")
        self.summed = sem("summed")
        self.chunk_out = sem("chunk_out")
        self.head_copied = sem("head_copied")
        self.head_squared = sem("head_squared")
        self.head_sum = sem("head_sum")
        self.head_root = sem("head_root")
        self.range = range(self.load.num, self.head_root.num + 1)
        assert len(self.range) == 34


def program(nc, d):
    f32, bf16 = mybir.dt.float32, mybir.dt.bfloat16
    A = mybir.ActivationFunctionType
    O = mybir.AluOpType
    AX = mybir.AxisListType.X
    es = ExitStack()
    with es:
        def sb(name, cols, dt=f32):
            return es.enter_context(nc.sbuf_tensor(name, [P, cols], dt))

        ringb = sb("ring", RING * UNIT)
        xb_ = sb("x", KT * T)
        ab_ = sb("a", KT * T)
        cf = sb("cf", NCF)
        cb = sb("cb", NCB, bf16)
        v1 = sb("v1", NV1)
        v2 = sb("v2", NV2)
        mod = sb("mod", 2 * 48)
        NARENA = 31500
        arena = sb("arena", NARENA)
        psb = es.enter_context(nc.psum_tensor("ps", [P, 8 * 512], f32))

        X = xb_[:, :].rearrange("p (k t) -> p k t", k=KT)
        AT = ab_[:, :].rearrange("p (k t) -> p k t", k=KT)
        PS = psb[:, :].rearrange("p (b n) -> p b n", b=8)

        def const(name):
            return cf[:, CF[name][0]:CF[name][1]]

        def const2(name):
            at = NARENA - NCG
            return arena[:, at + CG[name][0]:at + CG[name][1]]

        def constb(name):
            return cb[:, CB[name][0]:CB[name][1]]

        def vec1(name, j=0):
            return v1[:, V1[name][0] + j:V1[name][0] + j + 1]

        def vec2(name, j=0):
            return v2[:, V2[name][0] + j:V2[name][0] + j + 1]

        def modv(l, part, who, j):
            c = l * 48 + (part * 8 + j) * 2 + who
            return mod[:, c:c + 1]

        ident, ones = const("ident"), const("ones")

        class Carve:
            def __init__(self, at=0):
                self.at = at

            def __call__(self, n):
                a = self.at
                self.at += n
                assert self.at <= NARENA, self.at
                return arena[:, a:a + n]

        sets = [Sems(nc, es, "a"), Sems(nc, es, "b")]
        w_arrived = [es.enter_context(nc.semaphore(f"w_arrived{i}")) for i in range(RING)]
        assert [s.num for s in w_arrived] == list(range(w_arrived[0].num, w_arrived[0].num + RING))
        turn = [0]

        def stage_sems():
            turn[0] += 1
            return sets[turn[0] % 2], sets[(turn[0] + 1) % 2]

        def unit(n):
            return ringb[:, (n % RING) * UNIT:(n % RING + 1) * UNIT]

        def issue(sp, src, a, b, total, tile_done, per_unit=1):
            for n in range(a + RING, min(b + RING, total)):
                sp.wait_ge(tile_done, (n - RING - a + 1) * per_unit)
                sp.dma_start(unit(n), src(n)).then_inc(w_arrived[n % RING], 16)

        def issue_first(sp, src):
            sp.sem_clear(range(w_arrived[0].num, w_arrived[0].num + RING))
            for n in range(RING):
                sp.dma_start(unit(n), src(n)).then_inc(w_arrived[n], 16)

        def arrived(pe, n):
            pe.wait_ge(w_arrived[n % RING], 16 * (n // RING + 1))

        def src1(n):
            return d["w1"][n]

        cond = sb("cond", 32)
        silu_c = cond[:, 16:32].rearrange("p (w k) -> p k w", w=2)

        def stage_load():
            S, N = stage_sems()
            with nc.Block() as block:
                @block.sync
                def _(sp):
                    sp.sem_clear(N.range)
                    sp.dma_start(v1[:, :], d["v1"]).then_inc(S.load, 16)
                    issue_first(sp, src1)
                    sp.dma_start(X[:, :, 0:L], d["xT"]).then_inc(S.load2, 16)
                    sp.dma_start(X[:, :, L:T], d["ctxT"]).then_inc(S.load2, 16)
                    sp.dma_start(cf[:, :], d["cf"]).then_inc(S.load2, 16)
                    sp.dma_start(arena[:, 0:NCB], d["cb"]).then_inc(S.load2, 16)
                    sp.wait_ge(S.load, 16)
                    sp.wait_ge(S.load2, 64)

                @block.scalar
                def _(act):
                    act.wait_ge(S.load, 16)
                    nc.scalar.activation(cond[:, 16:32], v1[:, 0:16], A.Silu).then_inc(S.act_out, 1)

                @block.vector
                def _(dve):
                    dve.wait_ge(S.load2, 64)
                    nc.vector.tensor_copy(cb[:, :], arena[:, 0:NCB]).then_inc(S.dve_out, 1)

        def stage_mod(l, u0):
            S, N = stage_sems()
            with nc.Block() as block:
                @block.sync
                def _(sp):
                    sp.sem_clear(N.range)
                    issue(sp, src1, u0, u0 + 12, NU1, S.pe_tile)

                @block.tensor
                def _(pe):
                    for u in range(12):
                        arrived(pe, u0 + u)
                        w = unit(u0 + u).rearrange("p (k n) -> p k n", k=KT)
                        for h in range(2):
                            j = 2 * u + h
                            for k in range(KT):
                                last = nc.tensor.matmul(PS[:, 0, 2 * j:2 * j + 2], w[:, k, h * P:(h + 1) * P],
                                                        silu_c[:, k, :], start=(k == 0), stop=(k == KT - 1))
                        last.then_inc(S.pe_tile, 1)

                @block.vector
                def _(dve):
                    b = v1[:, V1[f"b_ada{l}"][0]:V1[f"b_ada{l}"][1]]
                    m = mod[:, l * 48:(l + 1) * 48]
                    dve.wait_ge(S.pe_tile, 12)
                    nc.vector.tensor_tensor(m.rearrange("p (j w) -> p j w", w=2),
                                            PS[:, 0, 0:48].rearrange("p (j w) -> p j w", w=2),
                                            b.unsqueeze(2).to_broadcast([P, 24, 2]), O.add).then_inc(S.dve_step, 1)
                    dve.wait_ge(S.dve_step, 1)
                    nc.vector.tensor_scalar(m[:, 16:32], m[:, 16:32], 1.0, None, O.add)

        def stage_modulate(l):
            S, N = stage_sems()
            with nc.Block() as block:
                @block.sync
                def _(sp):
                    sp.sem_clear(N.range)

                @block.vector
                def _(dve):
                    for k in range(KT):
                        for who, (a, b) in enumerate(((0, L), (L, T))):
                            nc.vector.tensor_scalar(AT[:, k, a:b], X[:, k, a:b], modv(l, 1, who, k),
                                                    modv(l, 0, who, k), O.mult, O.add).then_inc(S.dve_out, 1)

                @block.scalar
                def _(act):
                    for k in range(KT):
                        act.wait_ge(S.dve_out, 2 * k + 2)
                        nc.scalar.mul(X[:, k, :], X[:, k, :], ALPHA)

        c = Carve()
        qT = c(NT4 * T).rearrange("p (j t) -> p j t", j=NT4)
        kT = c(T)
        vtok = c(6 * P).rearrange("p (i n) -> p i n", i=6)
        yin = c(KT * T).rearrange("p (j t) -> p j t", j=KT)
        ca = c(NCA)
        esink = c(16)
        nsink = esink[:, 0:8]
        ab_mark = c.at
        xbt = c(NT4 * T).rearrange("p (j t) -> p j t", j=NT4)
        UP = T + 4
        upad = c(NT4 * UP).rearrange("p (j t) -> p j t", j=NT4)
        yc = c(NT4 * UP).rearrange("p (j t) -> p j t", j=NT4)

        def stage_ab_in():
            S, N = stage_sems()
            u0 = U1["ab_in"]
            tiles = ([("q", j) for j in range(4)] + [("k", 0), ("v", 0)] + [("ga", j) for j in range(4)]
                     + [("xb", j) for j in range(4)] + [("cg", j) for j in range(4)]
                     + [("gb", j) for j in range(4)] + [("bg", j) for j in range(4)])
            index = {t: i for i, t in enumerate(tiles)}
            by_dve = ("cg", "bg")

            def count(t):
                mine = t[0] in by_dve
                return sum((x[0] in by_dve) == mine for x in tiles[:index[t] + 1])

            def wide(i):
                return PS[:, 2 * (i % 4):2 * (i % 4) + 2, :].rearrange("p b n -> p (b n)")

            with nc.Block() as block:
                @block.sync
                def _(sp):
                    sp.sem_clear(N.range)
                    sp.dma_start(ca, d["ca"]).then_inc(S.load, 16)
                    sp.dma_start(nsink, d["sink"]).then_inc(S.load, 16)
                    issue(sp, src1, u0, u0 + 13, NU1, S.pe_tile, 2)
                    sp.wait_ge(S.load, 32)

                @block.tensor
                def _(pe):
                    for i, t in enumerate(tiles):
                        if i % 2 == 0:
                            arrived(pe, u0 + i // 2)
                        if i >= 4:
                            old = tiles[i - 4]
                            pe.wait_ge(S.dve_out if old[0] in by_dve else S.act_out, count(old))
                        w = unit(u0 + i // 2).rearrange("p (k n) -> p k n", k=KT)[:, :, (i % 2) * P:(i % 2 + 1) * P]
                        ps = wide(i)
                        if t[0] == "v":
                            for m in range(6):
                                for k in range(KT):
                                    last = nc.tensor.matmul(ps[:, m * P:(m + 1) * P], AT[:, k, m * P:(m + 1) * P],
                                                            w[:, k, :], start=(k == 0), stop=(k == KT - 1))
                        else:
                            for a, b in ((0, L), (L, T)):
                                for k in range(KT):
                                    last = nc.tensor.matmul(ps[:, a:b], w[:, k, :], AT[:, k, a:b],
                                                            start=(k == 0), stop=(k == KT - 1))
                        last.then_inc(S.pe_tile, 1)

                @block.scalar
                def _(act):
                    for i, (kind, j) in enumerate(tiles):
                        if kind in by_dve:
                            continue
                        act.wait_ge(S.pe_tile, i + 1)
                        dst = {"q": qT[:, j, :], "k": kT, "v": vtok.rearrange("p i n -> p (i n)"),
                               "ga": yin[:, j, :], "xb": xbt[:, j, :], "gb": yin[:, 4 + j, :]}[kind]
                        nc.scalar.activation(dst, wide(i)[:, 0:T], A.Silu if kind in ("ga", "gb") else A.Copy)\
                            .then_inc(S.act_out, 1)

                @block.vector
                def _(dve):
                    steps = [0]

                    def link(ins):
                        steps[0] += 1
                        ins.then_inc(S.dve_step, 1)
                        dve.wait_ge(S.dve_step, steps[0])

                    link(nc.vector.memset(upad, 0.0))
                    for j in range(4):
                        i = index[("cg", j)]
                        dve.wait_ge(S.pe_tile, i + 1)
                        dve.wait_ge(S.act_out, count(("xb", j)))
                        nc.vector.tensor_tensor(upad[:, j, 1:1 + L], wide(i)[:, 0:L], xbt[:, j, 0:L], O.mult)
                        nc.vector.tensor_tensor(upad[:, j, L + 3:T + 3], wide(i)[:, L:T], xbt[:, j, L:T], O.mult)\
                            .then_inc(S.dve_out, 1)
                        dve.wait_ge(S.dve_out, j + 1)
                        y, u = yc[:, j, 1:T + 3], upad[:, j, :]
                        link(nc.vector.tensor_scalar(y, u[:, 1:T + 3], vec1("conv", 4 + j), None, O.mult))
                        link(nc.vector.scalar_tensor_tensor(y, u[:, 0:T + 2], vec1("conv", j), y, O.mult, O.add))
                        link(nc.vector.scalar_tensor_tensor(y, u[:, 2:T + 4], vec1("conv", 8 + j), y, O.mult, O.add))
                    for j in range(4):
                        i = index[("bg", j)]
                        dve.wait_ge(S.pe_tile, i + 1)
                        dve.wait_ge(S.act_out, count(("gb", j)))
                        o = yin[:, 4 + j, :]
                        nc.vector.tensor_tensor(o, o, wide(i)[:, 0:T], O.mult).then_inc(S.dve_out, 1)
                        dve.wait_ge(S.dve_out, 4 + j + 1)
                        nc.vector.tensor_tensor(o[:, 0:L], o[:, 0:L], yc[:, j, 1:1 + L], O.mult)
                        nc.vector.tensor_tensor(o[:, L:T], o[:, L:T], yc[:, j, L + 3:T + 3], O.mult)

        def stage_rope(items, rot, tmp):
            S, N = stage_sems()
            with nc.Block() as block:
                @block.sync
                def _(sp):
                    sp.sem_clear(N.range)

                @block.tensor
                def _(pe):
                    for i, (x, _c, _s, n) in enumerate(items):
                        nc.tensor.matmul(PS[:, i, 0:n], rot, x, start=True, stop=True).then_inc(S.pe_tile, 1)

                @block.vector
                def _(dve):
                    for i, (x, cos, sin, n) in enumerate(items):
                        dve.wait_ge(S.pe_tile, i + 1)
                        nc.vector.tensor_tensor(tmp[:, 0:n], PS[:, i, 0:n], sin, O.mult)
                        nc.vector.tensor_tensor(x, x, cos, O.mult).then_inc(S.dve_step, 1)
                        dve.wait_ge(S.dve_step, 2 * i + 1)
                        nc.vector.tensor_tensor(x, x, tmp[:, 0:n], O.add).then_inc(S.dve_step, 1)
                        dve.wait_ge(S.dve_step, 2 * i + 2)

        def stage_ab_attention():
            S, N = stage_sems()
            cc = Carve(ab_mark)
            pr = cc(3 * 640).rearrange("p (b n) -> p b n", b=3)
            pt = cc(2 * 640).rearrange("p (b n) -> p b n", b=2)
            st = cc(3 * 8).rearrange("p (b n) -> p b n", b=3)
            jobs = []
            for n in range(NB):
                lo, hi = max(0, n - 1), min(NB - 1, n + 1)
                for h in range(NH):
                    jobs.append((n * P, list(range(lo, hi + 1)), n, h))
            for n in range(LC // P):
                for h in range(NH):
                    jobs.append((L + n * P, [], None, h))
            NJ = len(jobs)

            def region(j):
                return PS[:, 2 * (j % 2):2 * (j % 2) + 2, :].rearrange("p b n -> p (b n)")

            flips = PS[:, 4:6, :].rearrange("p b n -> p (b n)")

            def half(h):
                g = h // 4
                return slice(HD * g, HD * g + HD)

            with nc.Block() as block:
                @block.sync
                def _(sp):
                    sp.sem_clear(N.range)

                @block.tensor
                def _(pe):
                    def scores(j):
                        q0, loc, n, h = jobs[j]
                        nl = len(loc)
                        hs = half(h)
                        q = qT[hs, h % 4, q0:q0 + P]
                        if j >= 2:
                            pe.wait_ge(S.probs, j - 1)
                        r = region(j)
                        if nl:
                            nc.tensor.matmul(r[:, L - P * nl:L], q, kT[hs, loc[0] * P:(loc[-1] + 1) * P],
                                             start=True, stop=False)
                            edges = [m for m in loc if m != n]
                            for m in edges:
                                a = L - P * nl + (m - loc[0]) * P
                                nc.tensor.matmul(r[:, a:a + P], constb("ident"), constb("low" if m < n else "up"),
                                                 start=False, stop=(m == edges[-1]))
                        nc.tensor.matmul(r[:, L:L + LC], q, kT[hs, L:T], start=True, stop=True)\
                            .then_inc(S.scores, 1)

                    def flip(j):
                        pe.wait_ge(S.normed, j + 1)
                        if j >= 1:
                            pe.wait_ge(S.copied, j)
                        for i in range(len(jobs[j][1]) + 2):
                            last = nc.tensor.transpose(flips[:, i * P:(i + 1) * P],
                                                       pr[:, j % 3, i * P:(i + 1) * P], ident)
                        last.then_inc(S.flipped, 1)

                    def mix(j):
                        q0, loc, n, h = jobs[j]
                        hs = half(h)
                        pe.wait_ge(S.copied, j + 1)
                        if j >= 2:
                            pe.wait_ge(S.dve_out, j - 1)
                        keys = loc + [4, 5]
                        for i, m in enumerate(keys):
                            last = nc.tensor.matmul(PS[hs, 6 + j % 2, 0:P], vtok[:, m, hs],
                                                    pt[:, j % 2, i * P:(i + 1) * P], start=(i == 0),
                                                    stop=(i == len(keys) - 1))
                        last.then_inc(S.mixed, 1)

                    for s in range(NJ + 3):
                        if s < NJ:
                            scores(s)
                        if 2 <= s < NJ + 2:
                            flip(s - 2)
                        if s >= 3:
                            mix(s - 3)

                @block.scalar
                def _(act):
                    def exps(j):
                        nl = len(jobs[j][1])
                        act.wait_ge(S.shift, j + 1)
                        if j >= 3:
                            act.wait_ge(S.flipped, j - 2)
                        b = st[:, j % 3, :]
                        nc.scalar.activation(b[:, 3:4], b[:, 6:7], A.Exp)
                        nc.scalar.activation(pr[:, j % 3, 0:P * (nl + 2)], region(j)[:, L - P * nl:L + LC], A.Exp,
                                             bias=b[:, 1:2], scale=ASCALE, accum_out=b[:, 2:3]).then_inc(S.probs, 1)

                    def copy(j):
                        nk = len(jobs[j][1]) + 2
                        act.wait_ge(S.flipped, j + 1)
                        if j >= 2:
                            act.wait_ge(S.mixed, j - 1)
                        nc.scalar.activation(pt[:, j % 2, 0:nk * P], flips[:, 0:nk * P], A.Copy)\
                            .then_inc(S.copied, 1)

                    for s in range(NJ + 2):
                        if s < NJ:
                            exps(s)
                        if s >= 2:
                            copy(s - 2)

                @block.vector
                def _(dve):
                    steps = [0]

                    def link(ins):
                        steps[0] += 1
                        ins.then_inc(S.dve_step, 1)
                        dve.wait_ge(S.dve_step, steps[0])

                    def shift(j):
                        h, nl = jobs[j][3], len(jobs[j][1])
                        dve.wait_ge(S.scores, j + 1)
                        if j >= 3:
                            dve.wait_ge(S.normed, j - 2)
                        b = st[:, j % 3, :]
                        link(nc.vector.tensor_reduce(b[:, 0:1], region(j)[:, L - P * nl:L + LC], AX, O.max))
                        link(nc.vector.tensor_scalar(b[:, 1:2], b[:, 0:1], -ASCALE, esink[:, 8 + h:9 + h],
                                                     O.mult, O.min))
                        nc.vector.tensor_tensor(b[:, 6:7], b[:, 1:2], nsink[:, h:h + 1], O.add).then_inc(S.shift, 1)

                    def norm(j):
                        nk = len(jobs[j][1]) + 2
                        dve.wait_ge(S.probs, j + 1)
                        b = st[:, j % 3, :]
                        link(nc.vector.tensor_tensor(b[:, 4:5], b[:, 2:3], b[:, 3:4], O.add))
                        link(nc.vector.reciprocal(b[:, 5:6], b[:, 4:5]))
                        p_ = pr[:, j % 3, 0:nk * P]
                        nc.vector.tensor_scalar(p_, p_, b[:, 5:6], None, O.mult).then_inc(S.normed, 1)

                    def out(j):
                        q0, loc, n, h = jobs[j]
                        hs = half(h)
                        dve.wait_ge(S.mixed, j + 1)
                        y = yin[hs, h % 4, q0:q0 + P]
                        nc.vector.tensor_tensor(y, y, PS[hs, 6 + j % 2, 0:P], O.mult)\
                            .then_inc(S.dve_out, 1)

                    link(nc.vector.tensor_scalar(esink[:, 8:16], nsink, -1.0, None, O.mult))
                    for s in range(NJ + 3):
                        if s < NJ:
                            shift(s)
                        if 1 <= s < NJ + 1:
                            norm(s - 1)
                        if s >= 3:
                            out(s - 3)

        def stage_out1(l, u0, y, W):
            S, N = stage_sems()

            def wide(i):
                return PS[:, 2 * (i % 4):2 * (i % 4) + 2, :].rearrange("p b n -> p (b n)")

            parts = [(0, L)] + ([(L, T)] if W > L else [])
            with nc.Block() as block:
                @block.sync
                def _(sp):
                    sp.sem_clear(N.range)
                    issue(sp, src1, u0, u0 + 4, NU1, S.pe_tile, 2)

                @block.tensor
                def _(pe):
                    for i in range(KT):
                        if i % 2 == 0:
                            arrived(pe, u0 + i // 2)
                        if i >= 4:
                            pe.wait_ge(S.dve_out, i - 3)
                        w = unit(u0 + i // 2).rearrange("p (k n) -> p k n", k=KT)[:, :, (i % 2) * P:(i % 2 + 1) * P]
                        for a, b in parts:
                            for k in range(KT):
                                last = nc.tensor.matmul(wide(i)[:, a:b], w[:, k, :], y[:, k, a:b],
                                                        start=(k == 0), stop=(k == KT - 1))
                        last.then_inc(S.pe_tile, 1)

                @block.vector
                def _(dve):
                    for i in range(KT):
                        dve.wait_ge(S.pe_tile, i + 1)
                        for who, (a, b) in enumerate(parts):
                            last = nc.vector.scalar_tensor_tensor(X[:, i, a:b], wide(i)[:, a:b], modv(l, 2, who, i),
                                                                  X[:, i, a:b], O.mult, O.add)
                        last.then_inc(S.dve_out, 1)

        def stage_layer_norm(l, W, sq, tmp):
            S, N = stage_sems()
            parts = [(0, L)] + ([(L, T)] if W > L else [])
            mean = PS[:, 0:2, :].rearrange("p b n -> p (b n)")
            var = PS[:, 2:4, :].rearrange("p b n -> p (b n)")
            with nc.Block() as block:
                @block.sync
                def _(sp):
                    sp.sem_clear(N.range)

                @block.tensor
                def _(pe):
                    for a, b in parts:
                        for k in range(KT):
                            last = nc.tensor.matmul(mean[:, a:b], ones, X[:, k, a:b], start=(k == 0),
                                                    stop=(k == KT - 1))
                    last.then_inc(S.sums, 1)
                    for k in range(KT):
                        pe.wait_ge(S.squares, k + 1)
                        for a, b in parts:
                            last = nc.tensor.matmul(var[:, a:b], ones, sq[:, k, a:b], start=(k == 0),
                                                    stop=(k == KT - 1))
                    last.then_inc(S.sums, 1)

                @block.scalar
                def _(act):
                    for k in range(KT):
                        act.wait_ge(S.dve_out, k + 1)
                        nc.scalar.activation(sq[:, k, 0:W], X[:, k, 0:W], A.Square).then_inc(S.squares, 1)
                    act.wait_ge(S.sums, 2)
                    nc.scalar.activation(tmp[:, 0:W], var[:, 0:W], A.Sqrt, bias=const("eps")[:, 0:1], scale=1.0 / D)\
                        .then_inc(S.act_out, 1)
                    for k in range(KT):
                        act.wait_ge(S.normed, k + 1)
                        nc.scalar.activation(X[:, k, 0:W], X[:, k, 0:W], A.Identity, bias=vec1(f"ln_b{l}", k),
                                             scale=vec1(f"ln_g{l}", k))

                @block.vector
                def _(dve):
                    dve.wait_ge(S.sums, 1)
                    for k in range(KT):
                        nc.vector.scalar_tensor_tensor(X[:, k, 0:W], mean[:, 0:W], -1.0 / D, X[:, k, 0:W],
                                                       O.mult, O.add).then_inc(S.dve_out, 1)
                    dve.wait_ge(S.act_out, 1)
                    dve.wait_ge(S.dve_out, KT)
                    nc.vector.reciprocal(tmp[:, 0:W], tmp[:, 0:W]).then_inc(S.dve_step, 1)
                    dve.wait_ge(S.dve_step, 1)
                    dve.wait_ge(S.squares, KT)
                    for k in range(KT):
                        nc.vector.tensor_tensor(X[:, k, 0:W], X[:, k, 0:W], tmp[:, 0:W], O.mult)\
                            .then_inc(S.normed, 1)

        c = Carve()
        yh = c(CH * L).rearrange("p (j t) -> p j t", j=CH)
        hq = [c(2 * L).rearrange("p (j t) -> p j t", j=2) for _ in range(2)]
        hz = [c(4 * T).rearrange("p (d j t) -> p d j t", d=2, j=2) for _ in range(2)]
        hi = [c(6 * 256).rearrange("p (i n) -> p i n", i=6), X[:, 0:6, L:T]]
        buf_t1 = [c(T), c(T)]
        buf_lf = [c(T), c(T)]
        buf_k = [c(T), c(T)]
        buf_b = [c(T), c(T)]
        buf_eb = [c(L), c(L)]
        buf_x = [c(LEV * L), c(LEV * L)]
        buf_kt = c(5 * P)
        buf_s = [c(4 * P), c(4 * P)]
        prod = c(1024)
        am = [c(P), c(P)]

        C_TILES = [("q", 0, 0), ("q", 1, 0), ("z", 0, 1), ("z", 1, 1), ("z", 2, 2), ("z", 3, 2), ("i", 0, 3),
                   ("i", 1, 3), ("g", 0, 4), ("g", 1, 4)]

        def stage_c(step):
            S, N = stage_sems()
            u0 = U1["c_in"] + 5 * step
            projects, scans = step < CH // 2, step > 0
            qn, zn, iv = hq[step % 2], hz[step % 2], hi[step % 2]
            q_, z_, i_ = hq[(step + 1) % 2], hz[(step + 1) % 2], hi[(step + 1) % 2]
            pair = step - 1

            def rev(ap):
                return ap[:, ::-1]

            def levels(v, lev):
                w = v.rearrange("p (n s b) -> p n s b", s=2, b=1 << lev)
                return w[:, :, 0, :], w[:, :, 1, :]

            def bank2(b):
                return PS[:, b:b + 2, :].rearrange("p b n -> p (b n)")

            def order(dr):
                return list(range(NB)) if dr == 0 else list(range(NB))[::-1]

            def exponents(eng, dr):
                b = buf_b[dr]
                for lev in range(LEV):
                    B = 1 << lev
                    left, right = levels(b[:, 0:L], lev)
                    xl, xr = levels(buf_x[dr][:, lev * L:(lev + 1) * L], lev)
                    n = L // (2 * B)
                    if dr == 0:
                        ref = left[:, :, B - 1:B].to_broadcast([P, n, B])
                        eng.tensor_tensor(xr, right, ref, O.subtract)
                        last = eng.tensor_tensor(xl, ref, left, O.subtract)
                    else:
                        ref = right[:, :, 0:1].to_broadcast([P, n, B])
                        eng.tensor_tensor(xl, left, ref, O.subtract)
                        last = eng.tensor_tensor(xr, ref, right, O.subtract)
                return last

            with nc.Block() as block:
                @block.sync
                def _(sp):
                    sp.sem_clear(N.range)
                    if projects:
                        issue(sp, src1, u0, u0 + 5, NU1, S.pe_tile, 2)

                if scans:
                    @block.gpsimd
                    def _(pool):
                        for j in range(2):
                            pool.wait_ge(S.decays, j + 1)
                            exponents(nc.gpsimd, 1).then_inc(S.ready, 1)

                @block.vector
                def _(dve):
                    steps = [0]

                    def link(ins):
                        steps[0] += 1
                        ins.then_inc(S.dve_step, 1)
                        dve.wait_ge(S.dve_step, steps[0])

                    def gate_sum(j, dr):
                        u = 2 * j + dr
                        z = z_[:, dr, j, :]
                        t1, lf, b = buf_t1[dr], buf_lf[dr], buf_b[dr]
                        dve.wait_ge(S.absolute, u + 1)
                        if j >= 1:
                            dve.wait_ge(S.head_root, j)
                        link(nc.vector.scalar_tensor_tensor(lf, z, 0.0, t1, O.min, O.subtract))
                        nc.vector.tensor_tensor(t1, lf, z, O.subtract).then_inc(S.log_k, 1)
                        if dr == 0:
                            nc.vector.tensor_tensor_scan(b[:, 0:L], const("reset"), lf[:, 0:L], 0.0, O.mult, O.add)
                            link(nc.vector.tensor_tensor_scan(b[:, L:T], const("one"), lf[:, L:T], 0.0,
                                                              O.mult, O.add))
                        else:
                            nc.vector.tensor_tensor_scan(rev(b[:, 0:L]), const("reset"), rev(lf[:, 0:L]), 0.0,
                                                         O.mult, O.add)
                            nc.vector.tensor_tensor_scan(rev(b[:, L:T]), const("one"), rev(lf[:, L:T]), 0.0,
                                                         O.mult, O.add).then_inc(S.decays, 1)
                            dve.wait_ge(S.decays, j + 1)
                        end = P - 1 if dr == 0 else 0
                        b4 = b[:, 0:L].rearrange("p (n c) -> p n c", c=P)
                        nc.vector.tensor_tensor(lf[:, 0:L].rearrange("p (n c) -> p n c", c=P),
                                                b4[:, :, end:end + 1].to_broadcast([P, NB, P]), b4, O.subtract)
                        cend = T - 1 if dr == 0 else L
                        last = nc.vector.tensor_tensor(lf[:, L:T], b[:, cend:cend + 1].to_broadcast([P, LC]),
                                                       b[:, L:T], O.subtract)
                        if dr == 0:
                            last = exponents(nc.vector, 0)
                        last.then_inc(S.exponents, 1)

                    def weigh(j, dr):
                        q, k_ = q_[:, j, :], buf_k[dr]
                        dve.wait_ge(S.weights, 2 * j + dr + 1)
                        nc.vector.tensor_tensor(buf_t1[dr][:, 0:L], q, buf_eb[dr], O.mult)
                        nc.vector.tensor_tensor(buf_lf[dr], buf_lf[dr], k_, O.mult).then_inc(S.state_keys, 1)
                        for lev in range(LEV):
                            xl, xr = levels(buf_x[dr][:, lev * L:(lev + 1) * L], lev)
                            ql, qr = levels(q, lev)
                            kl, kr = levels(k_[:, 0:L], lev)
                            if dr == 0:
                                nc.vector.tensor_tensor(xr, xr, qr, O.mult)
                                last = nc.vector.tensor_tensor(xl, xl, kl, O.mult)
                            else:
                                nc.vector.tensor_tensor(xl, xl, ql, O.mult)
                                last = nc.vector.tensor_tensor(xr, xr, kr, O.mult)
                        last.then_inc(S.levelled, 1)

                    def states(j, dr):
                        u = 2 * j + dr
                        s, eb = buf_s[dr], buf_eb[dr]
                        dve.wait_ge(S.flipped, u + 1)
                        nc.vector.tensor_copy(buf_kt, bank2(2 * dr)[:, 0:5 * P]).then_inc(S.copied, 1)
                        dve.wait_ge(S.own, u + 1)
                        end = P - 1 if dr == 0 else 0
                        for i in range(NB):
                            o = s[:, i * P:(i + 1) * P]
                            if i == 0:
                                link(nc.vector.tensor_copy(o, PS[:, 4, 0:P]))
                            else:
                                dec = order(dr)[i - 1] * P + end
                                link(nc.vector.scalar_tensor_tensor(o, s[:, (i - 1) * P:i * P], eb[:, dec:dec + 1],
                                                                    PS[:, 4, i * P:(i + 1) * P], O.mult, O.add))

                    def masks(j, n):
                        i = j * NB + n
                        for dr in range(2):
                            dve.wait_ge(S.products, 2 * i + dr + 1)
                            m = constb("scan")[:, dr * 1024:(dr + 1) * 1024]
                            nc.vector.tensor_tensor(prod, bank2(2 * dr), m, O.mult).then_inc(S.masked, 1)
                            dve.wait_ge(S.masked, 2 * i + dr + 1)
                            if dr == 0 and i >= 1:
                                dve.wait_ge(S.chunk_out, i)
                            link(nc.vector.tensor_reduce(am[dr], prod.rearrange("p (l c) -> p c l", l=8), AX, O.add))
                        nc.vector.tensor_tensor(am[0], am[0], am[1], O.add).then_inc(S.summed, 1)

                    if scans:
                        link(nc.vector.tensor_scalar(q_, q_, KSCALE, None, O.mult))
                        for j in range(2):
                            gate_sum(j, 0)
                            gate_sum(j, 1)
                            for dr in range(2):
                                weigh(j, dr)
                                states(j, dr)
                            for n in range(NB):
                                masks(j, n)
                            o = buf_b[0][:, 0:L]
                            dve.wait_ge(S.chunk_out, NB * (j + 1))
                            nc.vector.tensor_copy(o, PS[:, 5, :]).then_inc(S.head_copied, 1)
                            dve.wait_ge(S.head_root, j + 1)
                            link(nc.vector.reciprocal(buf_eb[0], buf_eb[0]))
                            link(nc.vector.scalar_tensor_tensor(o, o, vec1("gnorm"), buf_eb[0], O.mult, O.mult))
                            y = yh[:, 2 * pair + j, :]
                            nc.vector.tensor_tensor(y, y, o, O.mult).then_inc(S.normed, 1)

                @block.scalar
                def _(act):
                    def empty(i):
                        if not projects:
                            return
                        kind, j, u = C_TILES[i]
                        act.wait_ge(S.pe_tile, i + 1)
                        if kind == "q":
                            ins = nc.scalar.activation(qn[:, j, :], bank2(6)[:, 0:L], A.Silu)
                        elif kind == "z":
                            ins = nc.scalar.activation(zn[:, j // 2, j % 2, :], bank2(6)[:, 0:T], A.Copy)
                        elif kind == "g":
                            ins = nc.scalar.activation(yh[:, 2 * step + j, :], bank2(6)[:, 0:L], A.Silu)
                        else:
                            n = 4 if j == 0 else 2
                            ins = nc.scalar.activation(iv[:, 4 * j:4 * j + n, :],
                                                       bank2(6)[:, 0:n * 256].rearrange("p (i n) -> p i n", i=n),
                                                       A.Copy)
                        ins.then_inc(S.act_out, 1)

                    steps = [0]

                    def link(ins):
                        steps[0] += 1
                        ins.then_inc(S.act_step, 1)
                        act.wait_ge(S.act_step, steps[0])

                    def weights(j, dr):
                        u = 2 * j + dr
                        act.wait_ge(S.log_k, u + 1)
                        nc.scalar.activation(buf_k[dr], buf_t1[dr], A.Exp)
                        act.wait_ge(S.exponents, u + 1)
                        nc.scalar.activation(buf_eb[dr], buf_b[dr][:, 0:L], A.Exp)
                        link(nc.scalar.activation(buf_lf[dr], buf_lf[dr], A.Exp))
                        if dr == 1:
                            act.wait_ge(S.ready, j + 1)
                        nc.scalar.activation(buf_x[dr], buf_x[dr], A.Exp).then_inc(S.weights, 1)

                    for j in range(2):
                        if scans:
                            for dr in range(2):
                                link(nc.scalar.activation(buf_t1[dr], z_[:, dr, j, :], A.Abs))
                            for t1 in buf_t1:
                                link(nc.scalar.activation(t1, t1, A.Exp, scale=-1.0))
                            for t1 in buf_t1:
                                nc.scalar.activation(t1, t1, A.Ln, bias=1.0).then_inc(S.absolute, 1)
                        empty(5 * j)
                        empty(5 * j + 1)
                        if scans:
                            weights(j, 0)
                        empty(5 * j + 2)
                        if scans:
                            weights(j, 1)
                        empty(5 * j + 3)
                        empty(5 * j + 4)
                        if scans:
                            act.wait_ge(S.head_copied, j + 1)
                            nc.scalar.activation(buf_k[0][:, 0:L], buf_b[0][:, 0:L], A.Square)\
                                .then_inc(S.head_squared, 1)
                            act.wait_ge(S.head_sum, j + 1)
                            nc.scalar.activation(buf_eb[0], PS[:, 5, :], A.Sqrt, bias=const("eps")[:, 1:2],
                                                 scale=1.0 / P).then_inc(S.head_root, 1)

                @block.tensor
                def _(pe):
                    def tile(i):
                        if not projects:
                            return
                        kind, j, u = C_TILES[i]
                        if i % 2 == 0:
                            arrived(pe, u0 + u)
                        if i >= 1:
                            pe.wait_ge(S.act_out, i)
                        w = unit(u0 + u).rearrange("p (k n) -> p k n", k=KT)
                        ps = bank2(6)
                        if kind == "i":
                            for m in (range(4) if j == 0 else range(4, 6)):
                                for k in range(KT):
                                    last = nc.tensor.matmul(ps[:, (m % 4) * 256:(m % 4 + 1) * 256],
                                                            AT[:, k, m * P:(m + 1) * P], w[:, k, :],
                                                            start=(k == 0), stop=(k == KT - 1))
                        else:
                            for a, b in ((0, L), (L, T)) if kind == "z" else ((0, L),):
                                for k in range(KT):
                                    last = nc.tensor.matmul(ps[:, a:b], w[:, k, (j % 2) * P:(j % 2 + 1) * P],
                                                            AT[:, k, a:b], start=(k == 0), stop=(k == KT - 1))
                        last.then_inc(S.pe_tile, 1)

                    def own_states(j, dr):
                        if not scans:
                            return
                        u = 2 * j + dr
                        od = order(dr)
                        pe.wait_ge(S.state_keys, u + 1)
                        if dr == 0 and j >= 1:
                            pe.wait_ge(S.summed, NB * j)
                        for i in range(5):
                            a = L + i * P if i < 2 else od[i - 2] * P
                            last = nc.tensor.transpose(bank2(2 * dr)[:, i * P:(i + 1) * P], buf_lf[dr][:, a:a + P], ident)
                        last.then_inc(S.flipped, 1)
                        pe.wait_ge(S.copied, u + 1)
                        v = i_[:, :, j * P:(j + 1) * P]
                        for i in range(2):
                            nc.tensor.matmul(PS[:, 4, 0:P], buf_kt[:, i * P:(i + 1) * P], v[:, 4 + i, :],
                                             start=(i == 0), stop=(i == 1))
                        for i in range(3):
                            last = nc.tensor.matmul(PS[:, 4, (i + 1) * P:(i + 2) * P],
                                                    buf_kt[:, (2 + i) * P:(3 + i) * P], v[:, od[i], :],
                                                    start=True, stop=True)
                        last.then_inc(S.own, 1)

                    def products(j, n, dr):
                        i = 2 * (j * NB + n) + dr
                        cs = slice(n * P, (n + 1) * P)
                        pe.wait_ge(S.levelled, 2 * j + dr + 1)
                        if n > 0:
                            pe.wait_ge(S.masked, i - 1)
                        for lev in range(LEV):
                            xv = buf_x[dr][:, lev * L + n * P:lev * L + (n + 1) * P]
                            nc.tensor.matmul(bank2(2 * dr)[:, lev * P:(lev + 1) * P], xv, xv, start=True, stop=True)
                        nc.tensor.matmul(bank2(2 * dr)[:, LEV * P:(LEV + 1) * P], buf_k[dr][:, cs], q_[:, j, cs],
                                         start=True, stop=True).then_inc(S.products, 1)

                    def chunk(j, n):
                        i = j * NB + n
                        cs = slice(n * P, (n + 1) * P)
                        if n == 0 and j >= 1:
                            pe.wait_ge(S.head_root, j)
                        pe.wait_ge(S.summed, i + 1)
                        o = PS[:, 5, cs]
                        nc.tensor.matmul(o, buf_s[0][:, cs], buf_t1[0][:, cs], start=True, stop=False)
                        r = NB - 1 - n
                        nc.tensor.matmul(o, buf_s[1][:, r * P:(r + 1) * P], buf_t1[1][:, cs], start=False, stop=False)
                        nc.tensor.matmul(o, i_[:, n, j * P:(j + 1) * P], am[0], start=False, stop=True)\
                            .then_inc(S.chunk_out, 1)

                    for j in range(2):
                        for i in range(3):
                            tile(5 * j + i)
                        own_states(j, 0)
                        tile(5 * j + 3)
                        own_states(j, 1)
                        tile(5 * j + 4)
                        if scans:
                            for n in range(NB):
                                products(j, n, 0)
                                products(j, n, 1)
                                if n >= 1:
                                    chunk(j, n - 1)
                            chunk(j, NB - 1)
                            pe.wait_ge(S.head_squared, j + 1)
                            nc.tensor.matmul(PS[:, 5, :], ones, buf_k[0][:, 0:L], start=True, stop=True)\
                                .then_inc(S.head_sum, 1)

        c = Carve()
        sq = c(KT * L).rearrange("p (k t) -> p k t", k=KT)
        fbuf = c(KT * L).rearrange("p (k t) -> p k t", k=KT)
        low_end = c.at
        y2 = c(KT * L).rearrange("p (k t) -> p k t", k=KT)
        rows = c(NR2)
        wgate = c(KT * 24).rearrange("p (k n) -> p k n", k=KT)
        rstd = c(2 * L).rearrange("p (g t) -> p g t", g=2)
        hid_at = c.at
        q2 = c(NT4 * L).rearrange("p (j t) -> p j t", j=NT4)
        kvc = c(2 * L).rearrange("p (g t) -> p g t", g=2)
        ksw = c(2 * L).rearrange("p (b t) -> p b t", b=2)
        vt2 = c(NB * 256).rearrange("p (i n) -> p i n", i=NB)
        zu = c(NT4 * L).rearrange("p (j t) -> p j t", j=NT4)
        zv = c(NB * L).rearrange("p (i n) -> p i n", i=NB)
        gates = c(NB * 24).rearrange("p (i n) -> p i n", i=NB)
        wsT = c(NH * P).rearrange("p (g t) -> p g t", g=NH)
        hT = c(4 * 64).rearrange("p (v h n) -> p v h n", v=2, h=2)
        kcT = c(64)
        vcr = c(2 * HD).rearrange("p (g e) -> p g e", g=2)
        pcT = c(NB * 2 * P).rearrange("p (i g q) -> p i g q", i=NB, g=2)
        c = Carve(0)
        blk = c(32 * 64).rearrange("p (l g n) -> p l g n", l=32, g=2)
        c = Carve(hid_at)
        hid = c(FT * L).rearrange("p (j t) -> p j t", j=FT)
        c = Carve(0)
        hc = c(2 * 2 * L).rearrange("p (b s t) -> p b s t", b=2, s=2)
        c = Carve(hid_at)
        pT = c(2 * L).rearrange("p (k t) -> p k t", k=2)
        pg = c(KT * L).rearrange("p (k t) -> p k t", k=KT)

        def row(name):
            return rows[:, R2[name][0]:R2[name][1]]

        def bank2(b):
            return PS[:, b:b + 2, :].rearrange("p b n -> p (b n)")

        def stage_rms(groups, before=None, residual=False, after=None):
            S, N = stage_sems()
            flat = [(g, k) for g, (src, _gain, _dst) in enumerate(groups) for k in range(len(src))]
            with nc.Block() as block:
                @block.sync
                def _(sp):
                    sp.sem_clear(N.range)
                    if before:
                        sp.wait_ge(S.load, before(sp, S))

                @block.scalar
                def _(act):
                    for i, (g, k) in enumerate(flat):
                        nc.scalar.activation(sq[:, i, :], groups[g][0][k], A.Square).then_inc(S.squares, 1)
                    for g, (src, _gain, _dst) in enumerate(groups):
                        act.wait_ge(S.sums, g + 1)
                        nc.scalar.activation(rstd[:, g, :], PS[:, g, :], A.Sqrt, bias=const("eps")[:, 1:2],
                                             scale=1.0 / (P * len(src))).then_inc(S.act_out, 1)

                @block.tensor
                def _(pe):
                    for i, (g, k) in enumerate(flat):
                        pe.wait_ge(S.squares, i + 1)
                        n = len(groups[g][0])
                        ins = nc.tensor.matmul(PS[:, g, :], ones, sq[:, i, :], start=(k == 0), stop=(k == n - 1))
                        if k == n - 1:
                            ins.then_inc(S.sums, 1)

                @block.vector
                def _(dve):
                    for g, (src, gain, dst) in enumerate(groups):
                        dve.wait_ge(S.act_out, g + 1)
                        nc.vector.reciprocal(rstd[:, g, :], rstd[:, g, :]).then_inc(S.dve_step, 1)
                        dve.wait_ge(S.dve_step, g + 1)
                        for k in range(len(src)):
                            if residual:
                                nc.vector.scalar_tensor_tensor(sq[:, k, :], src[k], gain(k), rstd[:, g, :],
                                                               O.mult, O.mult).then_inc(S.normed, 1)
                            else:
                                nc.vector.scalar_tensor_tensor(dst[k], src[k], gain(k), rstd[:, g, :],
                                                               O.mult, O.mult)
                    if residual:
                        for k in range(KT):
                            dve.wait_ge(S.normed, k + 1)
                            nc.vector.tensor_tensor(X[:, k, 0:L], X[:, k, 0:L], sq[:, k, :], O.add)

        def layer2(layer):
            def src2(n):
                return d["w2"][layer, n, :, :]

            def small_loads(sp, S):
                issue_first(sp, src2)
                sp.dma_start(v2[:, :], d["v2"][layer, :, :]).then_inc(S.load, 16)
                sp.dma_start(rows, d["r2"][layer, :, :]).then_inc(S.load, 16)
                sp.dma_start(wgate.rearrange("p k n -> p (k n)"), d["wgate"][layer, :, :]).then_inc(S.load, 16)
                sp.dma_start(wsT.rearrange("p g t -> p (g t)"), d["wsT"][layer, :, :]).then_inc(S.load, 16)
                return 64

            def stage_loads():
                S, N = stage_sems()
                with nc.Block() as block:
                    @block.sync
                    def _(sp):
                        sp.sem_clear(N.range)
                        sp.wait_ge(S.load, small_loads(sp, S))

            xt = [X[:, k, 0:L] for k in range(KT)]
            at = [AT[:, k, 0:L] for k in range(KT)]
            ft = [fbuf[:, k, :] for k in range(KT)]

            def stage_in2():
                S, N = stage_sems()
                u0 = U2["in2"]
                with nc.Block() as block:
                    @block.sync
                    def _(sp):
                        sp.sem_clear(N.range)
                        issue(sp, src2, u0, u0 + 9, NU2, S.pe_tile)

                    @block.tensor
                    def _(pe):
                        for u in range(10):
                            if u < 9:
                                arrived(pe, u0 + u)
                            if u >= 4:
                                pe.wait_ge(S.act_out, u - 3)
                            ps = bank2(2 * (u % 4))
                            w = unit(u0 + u).rearrange("p (k n) -> p k n", k=KT) if u < 9 else wgate
                            if u in (4, 7, 8, 9):
                                n = 24 if u == 9 else 256
                                for m in range(NB):
                                    for k in range(KT):
                                        last = nc.tensor.matmul(ps[:, m * n:(m + 1) * n], at[k][:, m * P:(m + 1) * P],
                                                                w[:, k, :], start=(k == 0), stop=(k == KT - 1))
                            else:
                                for h in range(2):
                                    for k in range(KT):
                                        last = nc.tensor.matmul(ps[:, h * L:(h + 1) * L], w[:, k, h * P:(h + 1) * P],
                                                                at[k], start=(k == 0), stop=(k == KT - 1))
                            last.then_inc(S.pe_tile, 1)

                    @block.scalar
                    def _(act):
                        for u in range(10):
                            act.wait_ge(S.pe_tile, u + 1)
                            ps = bank2(2 * (u % 4))
                            if u < 2:
                                ins = nc.scalar.activation(q2[:, 2 * u:2 * u + 2, :], ps.rearrange(
                                    "p (j t) -> p j t", j=2), A.Copy)
                            elif u == 2:
                                ins = nc.scalar.activation(kvc, ps.rearrange("p (j t) -> p j t", j=2), A.Copy)
                            elif u == 3:
                                ins = nc.scalar.activation(ksw, ps.rearrange("p (j t) -> p j t", j=2), A.Copy)
                            elif u == 4:
                                ins = nc.scalar.activation(vt2, ps.rearrange("p (j t) -> p j t", j=4), A.Copy)
                            elif u < 7:
                                ins = nc.scalar.activation(zu[:, 2 * (u - 5):2 * (u - 5) + 2, :], ps.rearrange(
                                    "p (j t) -> p j t", j=2), A.Gelu_apprx_tanh)
                            elif u < 9:
                                ins = nc.scalar.activation(zv[:, :, 256 * (u - 7):256 * (u - 6)], ps.rearrange(
                                    "p (j t) -> p j t", j=4), A.Gelu_apprx_tanh)
                            else:
                                ins = nc.scalar.activation(gates, ps[:, 0:96].rearrange("p (i n) -> p i n", i=NB),
                                                           A.Sigmoid)
                            ins.then_inc(S.act_out, 1)

            def stage_compress():
                S, N = stage_sems()
                u0 = U2["cmp1"]
                with nc.Block() as block:
                    @block.sync
                    def _(sp):
                        sp.sem_clear(N.range)
                        issue(sp, src2, u0, u0 + 4, NU2, S.pe_tile)

                    @block.vector
                    def _(dve):
                        nc.vector.memset(blk[:, :, :, NCMP:32], 0.0)
                        pe_ = v2[:, V2["pe"][0]:V2["pe"][1]]
                        for g in range(2):
                            for a in range(2):
                                src = kvc[:, g, 16 * a:16 * a + 16 * NCMP].rearrange("p (n b) -> p b n", b=16)
                                last = nc.vector.tensor_tensor(
                                    blk[:, 16 * a:16 * a + 16, g, 0:NCMP], src,
                                    pe_[:, 16 * a:16 * a + 16].unsqueeze(2).to_broadcast([P, 16, NCMP]), O.add)
                        last.then_inc(S.ready, 1)
                        dve.wait_ge(S.pe_tile, 6)
                        nc.vector.tensor_tensor(vcr, PS[:, 5, 0:P].rearrange("p (g e) -> p g e", g=2),
                                                row("b2v").unsqueeze(1).to_broadcast([P, 2, HD]), O.add)

                    @block.tensor
                    def _(pe):
                        pe.wait_ge(S.ready, 1)
                        for u in range(4):
                            arrived(pe, u0 + u)
                            w = unit(u0 + u).rearrange("p (l n) -> p l n", l=8)
                            for l8 in range(8):
                                l_ = 8 * u + l8
                                for kv in range(2):
                                    hs = slice(HD * kv, HD * kv + HD)
                                    for h in range(2):
                                        last = nc.tensor.matmul(
                                            PS[:, 2 * kv + h, 0:64], w[hs, l8, h * P:(h + 1) * P],
                                            blk[hs, l_, :, :].rearrange("p g n -> p (g n)"),
                                            start=(l_ == 0), stop=(l_ == 31))
                            last.then_inc(S.pe_tile, 1)
                        pe.wait_ge(S.act_out, 4)
                        w2k = row("w2k").rearrange("p (h n) -> p h n", h=2)
                        w2v = row("w2v").rearrange("p (h n) -> p h n", h=2)
                        for h in range(2):
                            last = nc.tensor.matmul(PS[:, 4, 0:64], w2k[:, h, :], hT[:, 0, h, :], start=(h == 0),
                                                    stop=(h == 1))
                        last.then_inc(S.pe_tile, 1)
                        for r in range(4):
                            for g in range(2):
                                for h in range(2):
                                    last = nc.tensor.matmul(PS[32 * r:32 * r + 32, 5, g * HD:(g + 1) * HD],
                                                            hT[:, 1, h, 32 * g:32 * g + 32], w2v[:, h, :],
                                                            start=(h == 0), stop=(h == 1))
                        last.then_inc(S.pe_tile, 1)

                    @block.scalar
                    def _(act):
                        act.wait_ge(S.pe_tile, 4)
                        for kv in range(2):
                            for h in range(2):
                                nc.scalar.activation(hT[:, kv, h, :], PS[:, 2 * kv + h, 0:64], A.Gelu_apprx_tanh,
                                                     bias=vec2("b1", 2 * kv + h)).then_inc(S.act_out, 1)
                        act.wait_ge(S.pe_tile, 5)
                        nc.scalar.activation(kcT, PS[:, 4, 0:64], A.Identity, bias=vec2("b2k"))

            def stage_cmp_attention():
                S, N = stage_sems()
                cc = Carve(0)
                e = cc(NB * 256).rearrange("p (i n) -> p i n", i=NB)
                st = cc(NB * 32).rearrange("p (i n) -> p i n", i=NB)
                with nc.Block() as block:
                    @block.sync
                    def _(sp):
                        sp.sem_clear(N.range)

                    @block.tensor
                    def _(pe):
                        for n in range(NB):
                            m = constb("cmp")[:, n * 32:(n + 1) * 32].unsqueeze(1).to_broadcast([P, 4, 32])
                            for g in range(2):
                                hs = slice(HD * g, HD * g + HD)
                                nc.tensor.matmul(PS[:, n + 4 * g, 0:P], constb("ident"), m, start=True, stop=False)
                                for h in range(4):
                                    last = nc.tensor.matmul(PS[:, n + 4 * g, 32 * h:32 * h + 32],
                                                            q2[hs, h, n * P:(n + 1) * P],
                                                            kcT[hs, 32 * g:32 * g + 32], start=False, stop=(h == 3))
                            last.then_inc(S.scores, 1)
                        for n in range(NB):
                            pe.wait_ge(S.normed, n + 1)
                            for g in range(2):
                                last = nc.tensor.transpose(PS[:, n, g * P:(g + 1) * P],
                                                           e[:, n, g * P:(g + 1) * P], ident)
                            last.then_inc(S.flipped, 1)

                    @block.scalar
                    def _(act):
                        for n in range(NB):
                            act.wait_ge(S.shift, n + 1)
                            nc.scalar.activation(e[:, n, :], e[:, n, :], A.Exp).then_inc(S.probs, 1)
                        for n in range(NB):
                            act.wait_ge(S.flipped, n + 1)
                            nc.scalar.activation(pcT[:, n, :, :].rearrange("p g q -> p (g q)"), PS[:, n, 0:256],
                                                 A.Copy)

                    @block.vector
                    def _(dve):
                        steps = [0]

                        def link(ins):
                            steps[0] += 1
                            ins.then_inc(S.dve_step, 1)
                            dve.wait_ge(S.dve_step, steps[0])

                        def heads(v):
                            return v.rearrange("p (h n) -> p h n", h=NH)

                        for n in range(NB):
                            dve.wait_ge(S.scores, n + 1)
                            b = st[:, n, :]
                            ps = [PS[:, n + 4 * g, 0:P].rearrange("p (h n) -> p h n", h=4) for g in range(2)]
                            for g in range(2):
                                last = nc.vector.tensor_reduce(b[:, 4 * g:4 * g + 4], ps[g], AX, O.max)
                            link(last)
                            link(nc.vector.tensor_scalar(b[:, 8:16], b[:, 0:8], NEG / 10, -ASCALE, O.max, O.mult))
                            for g in range(2):
                                last = nc.vector.scalar_tensor_tensor(
                                    heads(e[:, n, :])[:, 4 * g:4 * g + 4, :], ps[g], ASCALE,
                                    b[:, 8 + 4 * g:12 + 4 * g].unsqueeze(2).to_broadcast([P, 4, 32]), O.mult, O.add)
                            last.then_inc(S.shift, 1)
                        for n in range(NB):
                            dve.wait_ge(S.probs, n + 1)
                            b = st[:, n, :]
                            ev = heads(e[:, n, :])
                            link(nc.vector.tensor_reduce(b[:, 16:24], ev, AX, O.add))
                            link(nc.vector.tensor_scalar(b[:, 16:24], b[:, 16:24], 1e-30, None, O.max))
                            link(nc.vector.reciprocal(b[:, 24:32], b[:, 16:24]))
                            g = gates[:, n, :].rearrange("p (h c) -> p c h", c=3)[:, 0, :]
                            link(nc.vector.tensor_tensor(b[:, 24:32], b[:, 24:32], g, O.mult))
                            nc.vector.tensor_tensor(ev, ev, b[:, 24:32].unsqueeze(2).to_broadcast([P, NH, 32]),
                                                    O.mult).then_inc(S.normed, 1)

            def stage_attention():
                S, N = stage_sems()
                cc = Carve(0)
                pr = cc(3 * 2 * L).rearrange("p (b s t) -> p b s t", b=3, s=2)
                pt = cc(2 * 2 * L).rearrange("p (b s t) -> p b s t", b=2, s=2)
                st = cc(3 * 8).rearrange("p (b n) -> p b n", b=3)
                jobs = [(n, h) for n in range(NB) for h in range(NH)]
                NJ = len(jobs)

                def half(h):
                    g = h // 4
                    return slice(HD * g, HD * g + HD)

                def region(j):
                    return PS[:, 2 * (j % 2):2 * (j % 2) + 2, :]

                with nc.Block() as block:
                    @block.sync
                    def _(sp):
                        sp.sem_clear(N.range)

                    @block.tensor
                    def _(pe):
                        def scores(j):
                            n, h = jobs[j]
                            hs = half(h)
                            if j >= 2:
                                pe.wait_ge(S.probs, j - 1)
                            for s in range(2):
                                nc.tensor.matmul(region(j)[:, s, 0:(n + 1) * P], q2[hs, h % 4, n * P:(n + 1) * P],
                                                 ksw[hs, s, 0:(n + 1) * P], start=True, stop=False)
                                last = nc.tensor.matmul(region(j)[:, s, n * P:(n + 1) * P], constb("ident"),
                                                        constb("up"), start=False, stop=True)
                            last.then_inc(S.scores, 1)

                        def flip(j):
                            n, h = jobs[j]
                            pe.wait_ge(S.normed, j + 1)
                            if j >= 1:
                                pe.wait_ge(S.copied, j)
                            for s in range(2):
                                for i in range(n + 1):
                                    last = nc.tensor.transpose(PS[:, 4 + s, i * P:(i + 1) * P],
                                                               pr[:, j % 3, s, i * P:(i + 1) * P], ident)
                            last.then_inc(S.flipped, 1)

                        def mix(j):
                            n, h = jobs[j]
                            hs = half(h)
                            g, r = h // 4, h % 4
                            pe.wait_ge(S.copied, j + 1)
                            if j >= 2:
                                pe.wait_ge(S.dve_out, j - 1)
                            o = PS[hs, 6 + j % 2, 0:P]
                            for s in range(2):
                                for i in range(n + 1):
                                    nc.tensor.matmul(o, vt2[:, i, s * P + HD * g:s * P + HD * g + HD],
                                                     pt[:, j % 2, s, i * P:(i + 1) * P], start=(s + i == 0),
                                                     stop=False)
                            rs = slice(32 * r, 32 * r + 32)
                            nc.tensor.matmul(o, vcr[rs, g, :], pcT[rs, n, g, :], start=False, stop=True)\
                                .then_inc(S.mixed, 1)

                        for s in range(NJ + 3):
                            if s < NJ:
                                scores(s)
                            if 2 <= s < NJ + 2:
                                flip(s - 2)
                            if s >= 3:
                                mix(s - 3)

                    @block.scalar
                    def _(act):
                        def exps(j):
                            n = jobs[j][0]
                            w = (n + 1) * P
                            act.wait_ge(S.shift, j + 1)
                            if j >= 3:
                                act.wait_ge(S.flipped, j - 2)
                            b = st[:, j % 3, :]
                            for s in range(2):
                                last = nc.scalar.activation(pr[:, j % 3, s, 0:w], region(j)[:, s, 0:w], A.Exp,
                                                            bias=b[:, 2 + s:3 + s], scale=ASCALE,
                                                            accum_out=b[:, 4 + s:5 + s])
                            last.then_inc(S.probs, 1)

                        def copy(j):
                            w = (jobs[j][0] + 1) * P
                            act.wait_ge(S.flipped, j + 1)
                            if j >= 2:
                                act.wait_ge(S.mixed, j - 1)
                            nc.scalar.activation(pt[:, j % 2, :, 0:w], PS[:, 4:6, 0:w], A.Copy)\
                                .then_inc(S.copied, 1)

                        for s in range(NJ + 2):
                            if s < NJ:
                                exps(s)
                            if s >= 2:
                                copy(s - 2)

                    @block.vector
                    def _(dve):
                        steps = [0]

                        def link(ins):
                            steps[0] += 1
                            ins.then_inc(S.dve_step, 1)
                            dve.wait_ge(S.dve_step, steps[0])

                        def shift(j):
                            w = (jobs[j][0] + 1) * P
                            dve.wait_ge(S.scores, j + 1)
                            if j >= 3:
                                dve.wait_ge(S.normed, j - 2)
                            b = st[:, j % 3, :]
                            link(nc.vector.tensor_reduce(b[:, 0:2], region(j)[:, :, 0:w], AX, O.max))
                            nc.vector.tensor_scalar(b[:, 2:4], b[:, 0:2], -ASCALE, None, O.mult)\
                                .then_inc(S.shift, 1)

                        def norm(j):
                            n, h = jobs[j]
                            w = (n + 1) * P
                            dve.wait_ge(S.probs, j + 1)
                            b = st[:, j % 3, :]
                            link(nc.vector.reciprocal(b[:, 6:8], b[:, 4:6]))
                            link(nc.vector.tensor_tensor(b[:, 6:8], b[:, 6:8], gates[:, n, 3 * h + 1:3 * h + 3],
                                                         O.mult))
                            for s in range(2):
                                p_ = pr[:, j % 3, s, 0:w]
                                last = nc.vector.tensor_scalar(p_, p_, b[:, 6 + s:7 + s], None, O.mult)
                            last.then_inc(S.normed, 1)

                        def out(j):
                            n, h = jobs[j]
                            hs = half(h)
                            dve.wait_ge(S.mixed, j + 1)
                            nc.vector.tensor_copy(y2[hs, h % 4, n * P:(n + 1) * P], PS[hs, 6 + j % 2, 0:P])\
                                .then_inc(S.dve_out, 1)

                        for s in range(NJ + 3):
                            if s < NJ:
                                shift(s)
                            if 1 <= s < NJ + 1:
                                norm(s - 1)
                            if s >= 3:
                                out(s - 3)

            def stage_gmlp():
                S, N = stage_sems()
                cc = Carve(0)
                st = cc(NB * 16).rearrange("p (i n) -> p i n", i=NB)
                vm = cc(NT4 * L).rearrange("p (j t) -> p j t", j=NT4)
                with nc.Block() as block:
                    @block.sync
                    def _(sp):
                        sp.sem_clear(N.range)

                    @block.scalar
                    def _(act):
                        act.wait_ge(S.ready, 1)
                        nc.scalar.activation(st[:, :, 8:9], st[:, :, 7:8], A.Sqrt, bias=const("eps")[:, 1:2])\
                            .then_inc(S.act_out, 1)

                    @block.vector
                    def _(dve):
                        steps = [0]

                        def link(ins):
                            steps[0] += 1
                            ins.then_inc(S.dve_step, 1)
                            dve.wait_ge(S.dve_step, steps[0])

                        nc.vector.tensor_tensor(wsT, wsT, const2("tri").unsqueeze(1).to_broadcast([P, NH, P]),
                                                O.mult)
                        for i in range(NB):
                            last = nc.vector.bn_stats(st[:, i, 0:6], zv[:, i, :])
                        link(last)
                        for i in range(NB):
                            last = nc.vector.bn_aggr(st[:, i, 6:8], st[:, i, 0:6])
                        last.then_inc(S.ready, 1)
                        dve.wait_ge(S.act_out, 1)
                        link(nc.vector.reciprocal(st[:, :, 9:10], st[:, :, 8:9]))
                        for i in range(NB):
                            last = nc.vector.tensor_scalar(zv[:, i, :], zv[:, i, :], st[:, i, 6:7], st[:, i, 9:10],
                                                           O.subtract, O.mult)
                        link(last)
                        link(nc.vector.tensor_tensor(zv, zv, row("ln_g").unsqueeze(1).to_broadcast([P, NB, L]),
                                                     O.mult))
                        for i in range(NB):
                            nc.vector.tensor_tensor(zv[:, i, :], zv[:, i, :], row("ln_b"), O.add)\
                                .then_inc(S.normed, 1)
                        for j in range(NT4):
                            dve.wait_ge(S.pe_tile, j + 1)
                            b = row("bs").rearrange("p (j t) -> p j t", j=NT4)[:, j, :]
                            nc.vector.tensor_tensor(vm[:, j, :].rearrange("p (c t) -> p c t", c=NB),
                                                    PS[:, j, :].rearrange("p (c t) -> p c t", c=NB),
                                                    b.unsqueeze(1).to_broadcast([P, NB, P]), O.add)\
                                .then_inc(S.dve_out, 1)
                            dve.wait_ge(S.dve_out, j + 1)
                            nc.vector.tensor_tensor(y2[:, 4 + j, :], zu[:, j, :], vm[:, j, :], O.mult)

                    @block.tensor
                    def _(pe):
                        pe.wait_ge(S.normed, NB)
                        for j in range(NT4):
                            for h in range(2):
                                g = 2 * j + h
                                for ck in range(NB):
                                    last = nc.tensor.matmul(PS[HD * h:HD * h + HD, j, ck * P:(ck + 1) * P],
                                                            zv[:, ck, g * HD:(g + 1) * HD], wsT[:, g, :],
                                                            start=True, stop=True)
                            last.then_inc(S.pe_tile, 1)

            def stage_project(name, src, dst, nk):
                S, N = stage_sems()
                u0 = U2[name]
                per = (nk + 7) // 8
                with nc.Block() as block:
                    @block.sync
                    def _(sp):
                        sp.sem_clear(N.range)
                        issue(sp, src2, u0, u0 + 4 * per, NU2, S.pe_tile)

                    @block.tensor
                    def _(pe):
                        for m in range(4):
                            for v in range(per):
                                u = u0 + per * m + v
                                arrived(pe, u)
                                w = unit(u).rearrange("p (k n) -> p k n", k=8)
                                for h in range(2):
                                    for k in range(8 * v, min(8 * v + 8, nk)):
                                        last = nc.tensor.matmul(PS[:, 2 * m + h, :], w[:, k % 8, h * P:(h + 1) * P],
                                                                src[k], start=(k == 0), stop=(k == nk - 1))
                                last.then_inc(S.pe_tile, 1)

                    @block.scalar
                    def _(act):
                        for m in range(4):
                            act.wait_ge(S.pe_tile, per * (m + 1))
                            nc.scalar.activation(dst[:, 2 * m:2 * m + 2, :], PS[:, 2 * m:2 * m + 2, :], A.Copy)

            def stage_up():
                S, N = stage_sems()
                u0 = U2["up"]
                with nc.Block() as block:
                    @block.sync
                    def _(sp):
                        sp.sem_clear(N.range)
                        issue(sp, src2, u0, u0 + FT, NU2, S.pe_tile)

                    @block.tensor
                    def _(pe):
                        for j in range(FT):
                            arrived(pe, u0 + j)
                            if j >= 4:
                                pe.wait_ge(S.dve_out, j - 3)
                            w = unit(u0 + j).rearrange("p (k n) -> p k n", k=KT)
                            for h in range(2):
                                for k in range(KT):
                                    last = nc.tensor.matmul(PS[:, 2 * (j % 4) + h, :], w[:, k, h * P:(h + 1) * P],
                                                            at[k], start=(k == 0), stop=(k == KT - 1))
                            last.then_inc(S.pe_tile, 1)

                    @block.scalar
                    def _(act):
                        for j in range(FT):
                            act.wait_ge(S.pe_tile, j + 1)
                            if j >= 2:
                                act.wait_ge(S.ready, j - 1)
                            for h in range(2):
                                last = nc.scalar.activation(hc[:, j % 2, h, :], PS[:, 2 * (j % 4) + h, :], A.Identity,
                                                            bias=vec2("cb", 2 * j + h),
                                                            scale=vec2("cw", 3 * (2 * j + h) + 2))
                            last.then_inc(S.act_out, 1)
                            act.wait_ge(S.dve_out, j + 1)
                            nc.scalar.activation(hc[:, j % 2, 0, :], hc[:, j % 2, 0, :], A.Silu)\
                                .then_inc(S.act_step, 1)

                    @block.vector
                    def _(dve):
                        for j in range(FT):
                            dve.wait_ge(S.act_out, j + 1)
                            for s in (1, 2):
                                for h in range(2):
                                    b = hc[:, j % 2, h, s:L]
                                    last = nc.vector.scalar_tensor_tensor(
                                        b, PS[:, 2 * (j % 4) + h, 0:L - s], vec2("cw", 3 * (2 * j + h) + 2 - s), b,
                                        O.mult, O.add)
                                last.then_inc(S.dve_step if s == 1 else S.dve_out, 1)
                                if s == 1:
                                    dve.wait_ge(S.dve_step, j + 1)
                            dve.wait_ge(S.act_step, j + 1)
                            nc.vector.tensor_tensor(hid[:, j, :], hc[:, j % 2, 0, :], hc[:, j % 2, 1, :], O.mult)\
                                .then_inc(S.ready, 1)

            def stage_ple():
                S, N = stage_sems()
                u0 = U2["pleg"]
                with nc.Block() as block:
                    @block.sync
                    def _(sp):
                        sp.sem_clear(N.range)
                        sp.dma_start(pT, d["pT"][layer, :, :].rearrange("p (k t) -> p k t", k=2)).then_inc(S.load, 16)
                        issue(sp, src2, u0, u0 + 5, NU2, S.pe_tile)
                        sp.wait_ge(S.load, 16)

                    @block.tensor
                    def _(pe):
                        for m in range(4):
                            arrived(pe, u0 + m)
                            w = unit(u0 + m).rearrange("p (k n) -> p k n", k=8)
                            for h in range(2):
                                for k in range(KT):
                                    last = nc.tensor.matmul(PS[:, 2 * m + h, :], w[:, k, h * P:(h + 1) * P],
                                                            at[k], start=(k == 0), stop=(k == KT - 1))
                            last.then_inc(S.pe_tile, 1)
                        arrived(pe, u0 + 4)
                        pe.wait_ge(S.load, 16)
                        w = unit(u0 + 4).rearrange("p (k n) -> p k n", k=2)
                        for j in range(KT):
                            pe.wait_ge(S.act_out, j // 2 + 1)
                            for k in range(2):
                                last = nc.tensor.matmul(PS[:, j, :], w[:, k, j * P:(j + 1) * P], pT[:, k, :],
                                                        start=(k == 0), stop=(k == 1))
                            last.then_inc(S.mixed, 1)

                    @block.scalar
                    def _(act):
                        for m in range(4):
                            act.wait_ge(S.pe_tile, m + 1)
                            nc.scalar.activation(pg[:, 2 * m:2 * m + 2, :], PS[:, 2 * m:2 * m + 2, :], A.Sigmoid)\
                                .then_inc(S.act_out, 1)

                    @block.vector
                    def _(dve):
                        for j in range(KT):
                            dve.wait_ge(S.mixed, j + 1)
                            nc.vector.tensor_tensor(pg[:, j, :], pg[:, j, :], PS[:, j, :], O.mult)\
                                .then_inc(S.dve_out, 1)
                            dve.wait_ge(S.dve_out, j + 1)
                            nc.vector.tensor_tensor(xt[j], xt[j], pg[:, j, :], O.add)

            stage_loads()
            stage_rms([(xt, lambda k: vec2("pre_mix", k), at)])
            stage_in2()
            stage_compress()
            cos2, sin2 = const2("cos2"), const2("sin2")
            stage_rope([(q2[:, j, :], cos2, sin2, L) for j in range(NT4)]
                       + [(ksw[:, s, :], cos2, sin2, L) for s in range(2)]
                       + [(kcT, const2("cosc"), const2("sinc"), 64)], const("r2"), sq[:, 0, :])
            stage_cmp_attention()
            stage_attention()
            stage_gmlp()
            yt = [y2[:, k, :] for k in range(KT)]
            stage_rms([(yt[0:4], lambda k: vec2("attn_g", k), yt[0:4]),
                       (yt[4:8], lambda k: vec2("mlp_g", k), yt[4:8])])
            stage_project("wo", yt, fbuf, KT)
            stage_rms([(ft, lambda k: vec2("post_mix", k), None)], residual=True)
            stage_rms([(xt, lambda k: vec2("pre_ffn", k), at)])
            stage_up()
            stage_project("down", [hid[:, k, :] for k in range(FT)], fbuf, FT)
            stage_rms([(ft, lambda k: vec2("post_ffn", k), None)], residual=True)
            stage_rms([(xt, lambda k: vec2("ple_g", k), at)])
            stage_ple()

        def cut(v, n):
            return [v[:, i * n:(i + 1) * n] for i in range(v.shape[1] // n)]

        stage_load()
        stage_mod(0, U1["ada0"])
        stage_modulate(0)
        stage_ab_in()
        cos1, sin1 = ca[:, CA["cos1"][0]:CA["cos1"][1]], ca[:, CA["sin1"][0]:CA["sin1"][1]]
        stage_rope([(qT[:, j, 0:L], cos1, sin1, L) for j in range(NT4)] + [(kT[:, 0:L], cos1, sin1, L)],
                   const("r1"), xbt[:, 0, 0:L])
        stage_ab_attention()
        stage_out1(0, U1["ab_out"], yin, T)
        c = Carve()
        sq1, tmp1 = c(KT * T).rearrange("p (k t) -> p k t", k=KT), c(T + 1)
        stage_layer_norm(0, T, sq1, tmp1)
        stage_mod(1, U1["ada1"])
        stage_modulate(1)
        for step in range(CH // 2 + 1):
            stage_c(step)
        stage_out1(1, U1["c_out"], yh, L)
        stage_layer_norm(1, L, sq1, tmp1)
        S, N = stage_sems()
        with nc.Block() as block:
            @block.sync
            def _(sp):
                sp.sem_clear(N.range)
                sp.dma_start(arena[:, NARENA - NCG:NARENA], d["cg"]).then_inc(S.load, 16)
                sp.wait_ge(S.load, 16)
        before = turn[0]
        with nc.Fori(0, 2) as layer:
            layer2(layer)
            if (turn[0] - before) % 2:
                S, N = stage_sems()
                with nc.Block() as block:
                    @block.sync
                    def _(sp):
                        sp.sem_clear(N.range)
        S, N = stage_sems()
        with nc.Block() as block:
            @block.sync
            def _(sp):
                sp.dma_start(d["out"], X[:, :, 0:L]).then_inc(S.store, 16)
                sp.wait_ge(S.store, 16)


HEAD_COLUMNS = np.concatenate([np.arange(HD) + HD * h for t in range(NT4) for h in (t, t + 4)])


def ktiles(w):
    return w.reshape(-1, P, w.shape[1]).transpose(1, 0, 2)


def units_of(w):
    return w.reshape(KT, P, -1, 256).transpose(2, 1, 0, 3).reshape(-1, P, UNIT)


def vec(v):
    return v.reshape(-1, P).T


def partner(halves):
    r = np.zeros((P, P), np.float32)
    for h in range(2):
        for start, half in halves:
            for i in range(half):
                a, b = h * HD + start + i, h * HD + start + half + i
                r[b, a] = -1.0
                r[a, b] = 1.0
    return r


def constants():
    c = np.zeros((P, NCF), np.float32)
    c2 = np.zeros((P, NCG), np.float32)

    def put(name, v):
        if name in CF:
            c[:, CF[name][0]:CF[name][1]] = v
        else:
            c2[:, CG[name][0]:CG[name][1]] = v

    i = np.arange(P)
    put("ident", np.eye(P))
    put("ones", 1.0)
    put("r1", partner([(0, 16), (32, 16)]))
    put("r2", partner([(0, 8)]))
    put("tri", i[:, None] <= i[None, :])
    inv = (np.float32(500000.0) ** (-np.arange(8, dtype=np.float32) / 8)).astype(np.float32)

    def table(pos):
        ang = np.zeros((HD, len(pos)), np.float32)
        ang[0:16] = np.tile(inv, 2)[:, None] * pos.astype(np.float32)[None, :]
        return np.tile(np.cos(ang), (2, 1)), np.tile(np.sin(ang), (2, 1))

    cs, sn = table(np.arange(L))
    put("cos2", cs)
    put("sin2", sn)
    cp = np.arange(32) * 16 + 31
    cs, sn = table(np.concatenate([cp, cp]))
    put("cosc", cs)
    put("sinc", sn)
    put("reset", (np.arange(L) % P != 0)[None, :])
    put("one", 1.0)
    put("eps", np.array([LN_EPS, RMS_EPS])[None, :])
    f = (np.float32(10000.0) ** (-np.arange(16, dtype=np.float32) / 16)).astype(np.float32)
    t = np.arange(L)
    ang = np.concatenate([np.tile(f, 2)[:, None] * (t // 64).astype(np.float32)[None, :],
                          np.tile(f, 2)[:, None] * (t % 64).astype(np.float32)[None, :]])
    ca = np.concatenate([np.tile(np.cos(ang), (2, 1)), np.tile(np.sin(ang), (2, 1))], axis=1).astype(np.float32)
    b = np.zeros((P, NCB), np.float32)

    def putb(name, v):
        b[:, CB[name][0]:CB[name][1]] = v

    putb("ident", np.eye(P))
    putb("up", np.where(i[None, :] > i[:, None], NEG, 0))
    putb("low", np.where(i[None, :] < i[:, None], NEG, 0))
    cm = np.zeros((P, NB, 32), np.float32)
    for n in range(NB):
        ok = (cp[None, :] <= n * P + i[:, None]) & (np.arange(32)[None, :] < NCMP)
        cm[:, n] = np.where(ok, 0, NEG)
    putb("cmp", cm.reshape(P, -1))
    m = np.zeros((2, 8, P, P), np.float32)
    for lev in range(LEV):
        B = 1 << lev
        same = (i[:, None] // (2 * B)) == (i[None, :] // (2 * B))
        left, right = (i // B) % 2 == 0, (i // B) % 2 == 1
        m[0, lev] = same & left[:, None] & right[None, :]
        m[1, lev] = same & right[:, None] & left[None, :]
    m[:, 7] = np.eye(P)
    putb("scan", m.transpose(2, 0, 1, 3).reshape(P, -1))
    return c, c2, b, ca


def layout(i):
    f = {k: np.asarray(v) for k, v in i.items()}
    out = {}
    out["xT"] = np.ascontiguousarray(f["x"][0].T.reshape(KT, P, L).transpose(1, 0, 2))
    out["ctxT"] = np.ascontiguousarray(f["ctx"][0].T.reshape(KT, P, LC).transpose(1, 0, 2))
    v = np.zeros((P, NV1), np.float32)
    for name, a in [("c", f["c"][0]), ("cc", f["c_ctx"]), ("b_ada0", f["b_ada"][0]), ("b_ada1", f["b_ada"][1]),
                    ("ln_g0", f["ln_g"][0]), ("ln_b0", f["ln_b"][0]), ("ln_g1", f["ln_g"][1]),
                    ("ln_b1", f["ln_b"][1]), ("conv", f["conv_ab"][0].reshape(-1)), ("gnorm", f["gnorm_c"][0])]:
        v[:, V1[name][0]:V1[name][1]] = vec(a)
    out["v1"] = v
    out["sink"] = np.ascontiguousarray(np.broadcast_to(f["sink_ab"][0][None, :], (P, NH)))
    w = f["w_in_ab"][0]
    q, k, vv, ga, xb, bg, cg, gb = np.split(w, np.cumsum([512, 128, 128, 512, 512, 512, 512]), axis=1)
    ab_in = np.concatenate([q[:, HEAD_COLUMNS], k, vv, ga[:, HEAD_COLUMNS], xb, cg, gb, bg], axis=1)
    wo = f["w_out_ab"][0]
    ab_out = np.concatenate([wo[0:512][HEAD_COLUMNS], wo[512:]], axis=0)
    w = f["w_in_c"][0]
    parts = np.split(w, 5, axis=1)
    c_in = np.concatenate([x[:, 256 * p:256 * (p + 1)] for p in range(4) for x in parts], axis=1)
    out["w1"] = np.concatenate([units_of(x) for x in (f["w_ada"][0], ab_in, ab_out, f["w_ada"][1], c_in,
                                                      f["w_out_c"][0])])
    seg, v2, r2, wsT, wg, pT = [], [], [], [], [], []
    for l in range(2):
        g = {k[:-2]: v[l] for k, v in f.items() if k.endswith("_2")}
        w = g["w_in"]
        q, kc, vc, ks, vs, kw, vw, zg, zu, zv = np.split(
            w, np.cumsum([512, 128, 128, 128, 128, 128, 128, 24, 512]), axis=1)
        win = np.concatenate([q[:, HEAD_COLUMNS], kc[:, :64], vc[:, :64], kc[:, 64:], vc[:, 64:], ks, kw, vs, vw,
                              zu, zv], axis=1)
        c1 = g["cmp_w1"].reshape(2, 4, 8, HD, 256).transpose(1, 0, 3, 2, 4).reshape(4, P, UNIT)
        wo = np.concatenate([g["w_o"][0:512][HEAD_COLUMNS], g["w_o"][512:]], axis=0)
        up = g["w_up"].reshape(D, 2, FT, P).transpose(0, 2, 1, 3).reshape(D, -1)
        dn = np.concatenate([g["w_down"], np.zeros((24 * P - FF, D), np.float32)])
        dn = dn.reshape(3, 8, P, 4, 256).transpose(3, 0, 2, 1, 4).reshape(12, P, UNIT)
        pj = ktiles(g["w_ple_proj"]).reshape(1, P, UNIT)
        seg.append(np.concatenate([units_of(win), c1, units_of(wo), units_of(up), dn, units_of(g["w_ple_gate"]), pj]))
        a = np.zeros((P, NV2), np.float32)
        for name, x in [("pre_mix", vec(g["pre_mix_g"])), ("b1", vec(g["cmp_b1"].reshape(-1))),
                        ("pe", g["cmp_pe"].transpose(0, 2, 1).reshape(P, 32)),
                        ("b2k", np.tile(g["cmp_b2"][0], 2)[:, None]),
                        ("attn_g", vec(g["attn_out_g"][HEAD_COLUMNS])), ("mlp_g", vec(g["mlp_out_g"])),
                        ("post_mix", vec(g["post_mix_g"])), ("pre_ffn", vec(g["pre_ffn_g"])),
                        ("cw", g["conv_w"].reshape(3, 2, FT, P).transpose(3, 2, 1, 0).reshape(P, -1)),
                        ("cb", g["conv_b"].reshape(2, FT, P).transpose(2, 1, 0).reshape(P, -1)),
                        ("post_ffn", vec(g["post_ffn_g"])), ("ple_g", vec(g["ple_norm_g"]))]:
            a[:, V2[name][0]:V2[name][1]] = x
        v2.append(a)
        r = np.zeros((P, NR2), np.float32)
        for name, x in [("ln_g", g["gmlp_ln_g"][None]), ("ln_b", g["gmlp_ln_b"][None]), ("b2v", g["cmp_b2"][1][None]),
                        ("bs", np.repeat(g["gmlp_bs"].reshape(NT4, 2, P).transpose(1, 0, 2).reshape(2, -1), HD, axis=0)),
                        ("w2k", np.concatenate([ktiles(g["cmp_w2"][0])] * 2, axis=2).reshape(P, -1)),
                        ("w2v", ktiles(g["cmp_w2"][1]).reshape(P, -1))]:
            r[:, R2[name][0]:R2[name][1]] = x
        r2.append(r)
        wsT.append(g["gmlp_ws"].transpose(2, 0, 1).reshape(P, -1))
        wg.append(ktiles(zg).reshape(P, -1))
        pT.append(g["p"][0].T.reshape(2, P, L).transpose(1, 0, 2).reshape(P, -1))
    out["w2"] = np.stack(seg)
    out["v2"], out["r2"], out["wsT"], out["wgate"], out["pT"] = (np.stack(x) for x in (v2, r2, wsT, wg, pT))
    out["cf"], out["cg"], out["cb"], out["ca"] = constants()
    return {k: np.ascontiguousarray(v) for k, v in out.items()}


def kernel(**inputs):
    import numpy as _np
    import concourse.bacc as _bacc
    from concourse import mybir as _mybir
    from concourse.bass_utils import run_bass_kernel_spmd as _run

    nc = _bacc.Bacc("TRN2", target_bir_lowering=False, num_devices=1)
    arrays = layout(inputs)
    d = {n: nc.dram_tensor(n + "_dram", a.shape, _mybir.dt.from_np(a.dtype), kind="ExternalInput").ap()
         for n, a in arrays.items()}
    d["out"] = nc.dram_tensor("out_dram", (P, KT, L), _mybir.dt.float32, kind="ExternalOutput").ap()
    program(nc, d)
    r = _run(nc, [{n + "_dram": a for n, a in arrays.items()}], core_ids=[0])
    o = r.results[0]["out_dram"]
    return _np.ascontiguousarray(o.transpose(2, 1, 0).reshape(1, L, D))
```

```python
import numpy as np
from contextlib import ExitStack
import concourse.bass as bass
from concourse import mybir

P = 128
D = 1024
L = 512
LC = 256
T = L + LC
KT = D // P
HD = 64
NH = 8
NT4 = 4
NB = L // P
CH = 8
LEV = 7
FF = 2816
FT = FF // P
NCMP = 31
UNIT = 2048
RING = 3
RAW = 2
SLOTS = 2
ALPHA = 4 ** 0.25
LN_EPS = 1e-5
RMS_EPS = 1e-6
NEG = -1e30
ASCALE = HD ** -0.5
KSCALE = P ** -0.5

SEG1 = [("ada0", 12), ("ab_in", 13), ("ab_out", 4), ("ada1", 12), ("c_in", 20), ("c_out", 4)]
SEG2 = [("in2", 9), ("cmp1", 4), ("wo", 4), ("up", FT), ("down", 12), ("pleg", 4), ("plep", 1)]


def first_units(seg):
    at, out = 0, {}
    for name, n in seg:
        out[name] = at
        at += n
    return out, at


U1, NU1 = first_units(SEG1)
U2, NU2 = first_units(SEG2)
NSPLIT = NU2 - 1


def columns(parts):
    at, out = 0, {}
    for name, n in parts:
        out[name] = (at, at + n)
        at += n
    return out, at


V1, NV1 = columns([("c", 8), ("cc", 8), ("b_ada0", 24), ("b_ada1", 24), ("ln_g0", 8), ("ln_b0", 8), ("ln_g1", 8),
                   ("ln_b1", 8), ("conv", 12), ("gnorm", 1)])
V2, NV2 = columns([("pre_mix", 8), ("pe", 32), ("b1", 4), ("b2k", 1), ("attn_g", 4), ("mlp_g", 4), ("post_mix", 8),
                   ("pre_ffn", 8), ("cw", 3 * 2 * FT), ("cb", 2 * FT), ("post_ffn", 8), ("ple_g", 8)])
R2, NR2 = columns([("ln_g", 512), ("ln_b", 512), ("b2v", 64), ("bs", NT4 * P), ("w2k", 2 * P), ("w2v", 2 * HD)])
CF, NCF = columns([("ident", P), ("ones", P), ("r1", P), ("r2", P), ("reset", L), ("one", LC), ("eps", 2)])
CG, NCG = columns([("tri", P), ("cos2", L), ("sin2", L), ("cosc", 64), ("sinc", 64), ("fold", 64)])
CA, NCA = columns([("cos1", L), ("sin1", L)])
CB, NCB = columns([("ident", P), ("up", P), ("low", P), ("cmp", NB * 32), ("scan", 2 * 8 * P)])


class Sems:
    def __init__(self, nc, es, tag):
        def sem(name):
            return es.enter_context(nc.semaphore(f"{name}_{tag}"))

        self.load = sem("load")
        self.load2 = sem("load2")
        self.store = sem("store")
        self.act_step = sem("act_step")
        self.dve_step = sem("dve_step")
        self.pe_tile = sem("pe_tile")
        self.act_out = sem("act_out")
        self.dve_out = sem("dve_out")
        self.scores = sem("scores")
        self.shift = sem("shift")
        self.probs = sem("probs")
        self.normed = sem("normed")
        self.flipped = sem("flipped")
        self.copied = sem("copied")
        self.mixed = sem("mixed")
        self.squares = sem("squares")
        self.sums = sem("sums")
        self.ready = sem("ready")
        self.decays = sem("decays")
        self.absolute = sem("absolute")
        self.log_k = sem("log_k")
        self.exponents = sem("exponents")
        self.weights = sem("weights")
        self.state_keys = sem("state_keys")
        self.levelled = sem("levelled")
        self.own = sem("own")
        self.products = sem("products")
        self.masked = sem("masked")
        self.summed = sem("summed")
        self.chunk_out = sem("chunk_out")
        self.head_copied = sem("head_copied")
        self.head_squared = sem("head_squared")
        self.head_sum = sem("head_sum")
        self.head_root = sem("head_root")
        self.rms_squares = sem("rms_squares")
        self.rms_sums = sem("rms_sums")
        self.rms_root = sem("rms_root")
        self.rms_step = sem("rms_step")
        self.rms_scaled = sem("rms_scaled")
        self.rms_high = sem("rms_high")
        self.rms_odd = sem("rms_odd")
        self.rms_even = sem("rms_even")
        self.range = range(self.load.num, self.rms_even.num + 1)
        assert len(self.range) == 42


def program(nc, d):
    f32, f32r, bf16 = mybir.dt.float32, mybir.dt.float32r, mybir.dt.bfloat16
    A = mybir.ActivationFunctionType
    O = mybir.AluOpType
    AX = mybir.AxisListType.X
    es = ExitStack()
    with es:
        def sb(name, cols, dt=f32):
            return es.enter_context(nc.sbuf_tensor(name, [P, cols], dt))

        xb_ = sb("x", KT * T)
        cf = sb("cf", NCF)
        cb = sb("cb", NCB, bf16)
        v1 = sb("v1", NV1)
        v2 = sb("v2", NV2)
        mod = sb("mod", 2 * 48)
        cond = sb("cond", 32)

        first = ExitStack()
        ringb = first.enter_context(nc.sbuf_tensor("ring", [P, RING * UNIT], f32))
        ab_ = first.enter_context(nc.sbuf_tensor("a", [P, KT * T], f32))
        NARENA = 31500
        arena = first.enter_context(nc.sbuf_tensor("arena", [P, NARENA], f32))
        psb = es.enter_context(nc.psum_tensor("ps", [P, 8 * 512], f32))

        X = xb_[:, :].rearrange("p (k t) -> p k t", k=KT)
        AT = ab_[:, :].rearrange("p (k t) -> p k t", k=KT)
        PS = psb[:, :].rearrange("p (b n) -> p b n", b=8)

        def const(name):
            return cf[:, CF[name][0]:CF[name][1]]

        def constb(name):
            return cb[:, CB[name][0]:CB[name][1]]

        def vec1(name, j=0):
            return v1[:, V1[name][0] + j:V1[name][0] + j + 1]

        def vec2(name, j=0):
            return v2[:, V2[name][0] + j:V2[name][0] + j + 1]

        def modv(l, part, who, j):
            c = l * 48 + (part * 8 + j) * 2 + who
            return mod[:, c:c + 1]

        ident, ones = const("ident"), const("ones")

        class Carve:
            def __init__(self, at=0, memory=None):
                self.at, self.memory = at, arena if memory is None else memory

            def __call__(self, n):
                a = self.at
                self.at += n
                assert self.at <= self.memory.shape[1], self.at
                return self.memory[:, a:a + n]

        sets = [Sems(nc, es, "a"), Sems(nc, es, "b")]
        w_arrived = [es.enter_context(nc.semaphore(f"w_arrived{i}")) for i in range(RING)]
        w_hi = es.enter_context(nc.semaphore("w_hi"))
        w_split = es.enter_context(nc.semaphore("w_split"))
        w_range = range(w_arrived[0].num, w_split.num + 1)
        assert len(w_range) == RING + 2
        turn = [0]

        def stage_sems():
            turn[0] += 1
            return sets[turn[0] % 2], sets[(turn[0] + 1) % 2]

        def unit(n):
            return ringb[:, (n % RING) * UNIT:(n % RING + 1) * UNIT]

        def issue(sp, src, a, b, total, tile_done, per_unit=1):
            for n in range(a + RING, min(b + RING, total)):
                sp.wait_ge(tile_done, (n - RING - a + 1) * per_unit)
                sp.dma_start(unit(n), src(n)).then_inc(w_arrived[n % RING], 16)

        def issue_first(sp, src):
            sp.sem_clear(w_range)
            for n in range(RING):
                sp.dma_start(unit(n), src(n)).then_inc(w_arrived[n], 16)

        def arrived(pe, n):
            pe.wait_ge(w_arrived[n % RING], 16 * (n // RING + 1))

        def src1(n):
            return d["w1"][n]

        silu_c = cond[:, 16:32].rearrange("p (w k) -> p k w", w=2)

        def stage_load():
            S, N = stage_sems()
            with nc.Block() as block:
                @block.sync
                def _(sp):
                    sp.sem_clear(N.range)
                    sp.dma_start(v1[:, :], d["v1"]).then_inc(S.load, 16)
                    issue_first(sp, src1)
                    sp.dma_start(X[:, :, 0:L], d["xT"]).then_inc(S.load2, 16)
                    sp.dma_start(X[:, :, L:T], d["ctxT"]).then_inc(S.load2, 16)
                    sp.dma_start(cf[:, :], d["cf"]).then_inc(S.load2, 16)
                    sp.dma_start(arena[:, 0:NCB], d["cb"]).then_inc(S.load2, 16)
                    sp.wait_ge(S.load, 16)
                    sp.wait_ge(S.load2, 64)

                @block.scalar
                def _(act):
                    act.wait_ge(S.load, 16)
                    nc.scalar.activation(cond[:, 16:32], v1[:, 0:16], A.Silu).then_inc(S.act_out, 1)

                @block.vector
                def _(dve):
                    dve.wait_ge(S.load2, 64)
                    nc.vector.tensor_copy(cb[:, :], arena[:, 0:NCB]).then_inc(S.dve_out, 1)

        def stage_mod(l, u0):
            S, N = stage_sems()
            rowsT = arena[0:2, 0:24 * P]
            with nc.Block() as block:
                @block.sync
                def _(sp):
                    sp.sem_clear(N.range)
                    issue(sp, src1, u0, u0 + 12, NU1, S.pe_tile)

                @block.tensor
                def _(pe):
                    def flip(b):
                        pe.wait_ge(S.act_out, b + 1)
                        for j in range(4 * b, 4 * b + 4):
                            last = nc.tensor.transpose(PS[:, 6, 2 * j:2 * j + 2], rowsT[:, j * P:(j + 1) * P],
                                                       ident[0:2, 0:2])
                        last.then_inc(S.flipped, 1)

                    for u in range(12):
                        arrived(pe, u0 + u)
                        w = unit(u0 + u).rearrange("p (k n) -> p k n", k=KT)
                        for k in range(KT):
                            last = nc.tensor.matmul(PS[0:2, u // 2, (u % 2) * 256:(u % 2 + 1) * 256],
                                                    silu_c[:, k, :], w[:, k, :], start=(k == 0), stop=(k == KT - 1))
                        last.then_inc(S.pe_tile, 1)
                        if u % 2 and u > 1:
                            flip(u // 2 - 1)
                    flip(5)

                @block.scalar
                def _(act):
                    for b in range(6):
                        act.wait_ge(S.pe_tile, 2 * b + 2)
                        nc.scalar.activation(rowsT[:, b * 512:(b + 1) * 512], PS[0:2, b, :], A.Copy)\
                            .then_inc(S.act_out, 1)

                @block.vector
                def _(dve):
                    b = v1[:, V1[f"b_ada{l}"][0]:V1[f"b_ada{l}"][1]]
                    m = mod[:, l * 48:(l + 1) * 48]
                    dve.wait_ge(S.flipped, 6)
                    nc.vector.tensor_tensor(m.rearrange("p (j w) -> p j w", w=2),
                                            PS[:, 6, 0:48].rearrange("p (j w) -> p j w", w=2),
                                            b.unsqueeze(2).to_broadcast([P, 24, 2]), O.add).then_inc(S.dve_step, 1)
                    dve.wait_ge(S.dve_step, 1)
                    nc.vector.tensor_scalar(m[:, 16:32], m[:, 16:32], 1.0, None, O.add)

        def stage_modulate(l):
            S, N = stage_sems()
            with nc.Block() as block:
                @block.sync
                def _(sp):
                    sp.sem_clear(N.range)

                @block.vector
                def _(dve):
                    for k in range(KT):
                        for who, (a, b) in enumerate(((0, L), (L, T))):
                            nc.vector.tensor_scalar(AT[:, k, a:b], X[:, k, a:b], modv(l, 1, who, k),
                                                    modv(l, 0, who, k), O.mult, O.add).then_inc(S.dve_out, 1)

                @block.scalar
                def _(act):
                    for k in range(KT):
                        act.wait_ge(S.dve_out, 2 * k + 2)
                        nc.scalar.mul(X[:, k, :], X[:, k, :], ALPHA)

        c = Carve()
        qT = c(NT4 * T).rearrange("p (j t) -> p j t", j=NT4)
        kT = c(T)
        vtok = c(6 * P).rearrange("p (i n) -> p i n", i=6)
        yin = c(KT * T).rearrange("p (j t) -> p j t", j=KT)
        ca = c(NCA)
        esink = c(16)
        nsink = esink[:, 0:8]
        ab_mark = c.at
        xbt = c(NT4 * T).rearrange("p (j t) -> p j t", j=NT4)
        UP = T + 4
        upad = c(NT4 * UP).rearrange("p (j t) -> p j t", j=NT4)
        yc = c(NT4 * UP).rearrange("p (j t) -> p j t", j=NT4)

        def stage_ab_in():
            S, N = stage_sems()
            u0 = U1["ab_in"]
            tiles = ([("q", j) for j in range(4)] + [("k", 0), ("v", 0)] + [("ga", j) for j in range(4)]
                     + [("xb", j) for j in range(4)] + [("cg", j) for j in range(4)]
                     + [("gb", j) for j in range(4)] + [("bg", j) for j in range(4)])
            index = {t: i for i, t in enumerate(tiles)}
            by_dve = ("cg", "bg")

            def count(t):
                mine = t[0] in by_dve
                return sum((x[0] in by_dve) == mine for x in tiles[:index[t] + 1])

            def wide(i):
                return PS[:, 2 * (i % 4):2 * (i % 4) + 2, :].rearrange("p b n -> p (b n)")

            with nc.Block() as block:
                @block.sync
                def _(sp):
                    sp.sem_clear(N.range)
                    sp.dma_start(ca, d["ca"]).then_inc(S.load, 16)
                    sp.dma_start(nsink, d["sink"]).then_inc(S.load, 16)
                    issue(sp, src1, u0, u0 + 13, NU1, S.pe_tile, 2)
                    sp.wait_ge(S.load, 32)

                @block.tensor
                def _(pe):
                    for i, t in enumerate(tiles):
                        if i % 2 == 0:
                            arrived(pe, u0 + i // 2)
                        if i >= 4:
                            old = tiles[i - 4]
                            pe.wait_ge(S.dve_out if old[0] in by_dve else S.act_out, count(old))
                        w = unit(u0 + i // 2).rearrange("p (k n) -> p k n", k=KT)[:, :, (i % 2) * P:(i % 2 + 1) * P]
                        ps = wide(i)
                        if t[0] == "v":
                            for m in range(6):
                                for k in range(KT):
                                    last = nc.tensor.matmul(ps[:, m * P:(m + 1) * P], AT[:, k, m * P:(m + 1) * P],
                                                            w[:, k, :], start=(k == 0), stop=(k == KT - 1))
                        else:
                            for a, b in ((0, L), (L, T)):
                                for k in range(KT):
                                    last = nc.tensor.matmul(ps[:, a:b], w[:, k, :], AT[:, k, a:b],
                                                            start=(k == 0), stop=(k == KT - 1))
                        last.then_inc(S.pe_tile, 1)

                @block.scalar
                def _(act):
                    for i, (kind, j) in enumerate(tiles):
                        if kind in by_dve:
                            continue
                        act.wait_ge(S.pe_tile, i + 1)
                        dst = {"q": qT[:, j, :], "k": kT, "v": vtok.rearrange("p i n -> p (i n)"),
                               "ga": yin[:, j, :], "xb": xbt[:, j, :], "gb": yin[:, 4 + j, :]}[kind]
                        nc.scalar.activation(dst, wide(i)[:, 0:T], A.Silu if kind in ("ga", "gb") else A.Copy)\
                            .then_inc(S.act_out, 1)

                @block.vector
                def _(dve):
                    steps = [0]

                    def link(ins):
                        steps[0] += 1
                        ins.then_inc(S.dve_step, 1)
                        dve.wait_ge(S.dve_step, steps[0])

                    link(nc.vector.memset(upad, 0.0))
                    for j in range(4):
                        i = index[("cg", j)]
                        dve.wait_ge(S.pe_tile, i + 1)
                        dve.wait_ge(S.act_out, count(("xb", j)))
                        nc.vector.tensor_tensor(upad[:, j, 1:1 + L], wide(i)[:, 0:L], xbt[:, j, 0:L], O.mult)
                        nc.vector.tensor_tensor(upad[:, j, L + 3:T + 3], wide(i)[:, L:T], xbt[:, j, L:T], O.mult)\
                            .then_inc(S.dve_out, 1)
                        dve.wait_ge(S.dve_out, j + 1)
                        y, u = yc[:, j, 1:T + 3], upad[:, j, :]
                        link(nc.vector.tensor_scalar(y, u[:, 1:T + 3], vec1("conv", 4 + j), None, O.mult))
                        link(nc.vector.scalar_tensor_tensor(y, u[:, 0:T + 2], vec1("conv", j), y, O.mult, O.add))
                        link(nc.vector.scalar_tensor_tensor(y, u[:, 2:T + 4], vec1("conv", 8 + j), y, O.mult, O.add))
                    for j in range(4):
                        i = index[("bg", j)]
                        dve.wait_ge(S.pe_tile, i + 1)
                        dve.wait_ge(S.act_out, count(("gb", j)))
                        o = yin[:, 4 + j, :]
                        nc.vector.tensor_tensor(o, o, wide(i)[:, 0:T], O.mult).then_inc(S.dve_out, 1)
                        dve.wait_ge(S.dve_out, 4 + j + 1)
                        nc.vector.tensor_tensor(o[:, 0:L], o[:, 0:L], yc[:, j, 1:1 + L], O.mult)
                        nc.vector.tensor_tensor(o[:, L:T], o[:, L:T], yc[:, j, L + 3:T + 3], O.mult)

        def stage_rope(items, rot, tmp):
            S, N = stage_sems()
            with nc.Block() as block:
                @block.sync
                def _(sp):
                    sp.sem_clear(N.range)

                @block.tensor
                def _(pe):
                    for i, (x, _c, _s, n) in enumerate(items):
                        nc.tensor.matmul(PS[:, i, 0:n], rot, x, start=True, stop=True).then_inc(S.pe_tile, 1)

                @block.vector
                def _(dve):
                    for i, (x, cos, sin, n) in enumerate(items):
                        dve.wait_ge(S.pe_tile, i + 1)
                        nc.vector.tensor_tensor(tmp[:, 0:n], PS[:, i, 0:n], sin, O.mult)
                        nc.vector.tensor_tensor(x, x, cos, O.mult).then_inc(S.dve_step, 1)
                        dve.wait_ge(S.dve_step, 2 * i + 1)
                        nc.vector.tensor_tensor(x, x, tmp[:, 0:n], O.add).then_inc(S.dve_step, 1)
                        dve.wait_ge(S.dve_step, 2 * i + 2)

        def stage_ab_attention():
            S, N = stage_sems()
            cc = Carve(ab_mark)
            pr = cc(3 * 640).rearrange("p (b n) -> p b n", b=3)
            pt = cc(2 * 640).rearrange("p (b n) -> p b n", b=2)
            st = cc(3 * 8).rearrange("p (b n) -> p b n", b=3)
            jobs = []
            for n in range(NB):
                lo, hi = max(0, n - 1), min(NB - 1, n + 1)
                for h in range(NH):
                    jobs.append((n * P, list(range(lo, hi + 1)), n, h))
            for n in range(LC // P):
                for h in range(NH):
                    jobs.append((L + n * P, [], None, h))
            NJ = len(jobs)

            def region(j):
                return PS[:, 2 * (j % 2):2 * (j % 2) + 2, :].rearrange("p b n -> p (b n)")

            flips = PS[:, 4:6, :].rearrange("p b n -> p (b n)")

            def half(h):
                g = h // 4
                return slice(HD * g, HD * g + HD)

            with nc.Block() as block:
                @block.sync
                def _(sp):
                    sp.sem_clear(N.range)

                @block.tensor
                def _(pe):
                    def scores(j):
                        q0, loc, n, h = jobs[j]
                        nl = len(loc)
                        hs = half(h)
                        q = qT[hs, h % 4, q0:q0 + P]
                        if j >= 2:
                            pe.wait_ge(S.probs, j - 1)
                        r = region(j)
                        if nl:
                            nc.tensor.matmul(r[:, L - P * nl:L], q, kT[hs, loc[0] * P:(loc[-1] + 1) * P],
                                             start=True, stop=False)
                            edges = [m for m in loc if m != n]
                            for m in edges:
                                a = L - P * nl + (m - loc[0]) * P
                                nc.tensor.matmul(r[:, a:a + P], constb("ident"), constb("low" if m < n else "up"),
                                                 start=False, stop=(m == edges[-1]))
                        nc.tensor.matmul(r[:, L:L + LC], q, kT[hs, L:T], start=True, stop=True)\
                            .then_inc(S.scores, 1)

                    def flip(j):
                        pe.wait_ge(S.normed, j + 1)
                        if j >= 1:
                            pe.wait_ge(S.copied, j)
                        for i in range(len(jobs[j][1]) + 2):
                            last = nc.tensor.transpose(flips[:, i * P:(i + 1) * P],
                                                       pr[:, j % 3, i * P:(i + 1) * P], ident)
                        last.then_inc(S.flipped, 1)

                    def mix(j):
                        q0, loc, n, h = jobs[j]
                        hs = half(h)
                        pe.wait_ge(S.copied, j + 1)
                        if j >= 2:
                            pe.wait_ge(S.dve_out, j - 1)
                        keys = loc + [4, 5]
                        for i, m in enumerate(keys):
                            last = nc.tensor.matmul(PS[hs, 6 + j % 2, 0:P], vtok[:, m, hs],
                                                    pt[:, j % 2, i * P:(i + 1) * P], start=(i == 0),
                                                    stop=(i == len(keys) - 1))
                        last.then_inc(S.mixed, 1)

                    for s in range(NJ + 3):
                        if s < NJ:
                            scores(s)
                        if 2 <= s < NJ + 2:
                            flip(s - 2)
                        if s >= 3:
                            mix(s - 3)

                @block.scalar
                def _(act):
                    def exps(j):
                        nl = len(jobs[j][1])
                        act.wait_ge(S.shift, j + 1)
                        if j >= 3:
                            act.wait_ge(S.flipped, j - 2)
                        b = st[:, j % 3, :]
                        nc.scalar.activation(b[:, 3:4], b[:, 6:7], A.Exp)
                        nc.scalar.activation(pr[:, j % 3, 0:P * (nl + 2)], region(j)[:, L - P * nl:L + LC], A.Exp,
                                             bias=b[:, 1:2], scale=ASCALE, accum_out=b[:, 2:3]).then_inc(S.probs, 1)

                    def copy(j):
                        nk = len(jobs[j][1]) + 2
                        act.wait_ge(S.flipped, j + 1)
                        if j >= 2:
                            act.wait_ge(S.mixed, j - 1)
                        nc.scalar.activation(pt[:, j % 2, 0:nk * P], flips[:, 0:nk * P], A.Copy)\
                            .then_inc(S.copied, 1)

                    for s in range(NJ + 2):
                        if s < NJ:
                            exps(s)
                        if s >= 2:
                            copy(s - 2)

                @block.vector
                def _(dve):
                    steps = [0]

                    def link(ins):
                        steps[0] += 1
                        ins.then_inc(S.dve_step, 1)
                        dve.wait_ge(S.dve_step, steps[0])

                    def shift(j):
                        h, nl = jobs[j][3], len(jobs[j][1])
                        dve.wait_ge(S.scores, j + 1)
                        if j >= 3:
                            dve.wait_ge(S.normed, j - 2)
                        b = st[:, j % 3, :]
                        link(nc.vector.tensor_reduce(b[:, 0:1], region(j)[:, L - P * nl:L + LC], AX, O.max))
                        link(nc.vector.tensor_scalar(b[:, 1:2], b[:, 0:1], -ASCALE, esink[:, 8 + h:9 + h],
                                                     O.mult, O.min))
                        nc.vector.tensor_tensor(b[:, 6:7], b[:, 1:2], nsink[:, h:h + 1], O.add).then_inc(S.shift, 1)

                    def norm(j):
                        nk = len(jobs[j][1]) + 2
                        dve.wait_ge(S.probs, j + 1)
                        b = st[:, j % 3, :]
                        link(nc.vector.tensor_tensor(b[:, 4:5], b[:, 2:3], b[:, 3:4], O.add))
                        link(nc.vector.reciprocal(b[:, 5:6], b[:, 4:5]))
                        p_ = pr[:, j % 3, 0:nk * P]
                        nc.vector.tensor_scalar(p_, p_, b[:, 5:6], None, O.mult).then_inc(S.normed, 1)

                    def out(j):
                        q0, loc, n, h = jobs[j]
                        hs = half(h)
                        dve.wait_ge(S.mixed, j + 1)
                        y = yin[hs, h % 4, q0:q0 + P]
                        nc.vector.tensor_tensor(y, y, PS[hs, 6 + j % 2, 0:P], O.mult)\
                            .then_inc(S.dve_out, 1)

                    link(nc.vector.tensor_scalar(esink[:, 8:16], nsink, -1.0, None, O.mult))
                    for s in range(NJ + 3):
                        if s < NJ:
                            shift(s)
                        if 1 <= s < NJ + 1:
                            norm(s - 1)
                        if s >= 3:
                            out(s - 3)

        def stage_out1(l, u0, y, W):
            S, N = stage_sems()

            def wide(i):
                return PS[:, 2 * (i % 4):2 * (i % 4) + 2, :].rearrange("p b n -> p (b n)")

            parts = [(0, L)] + ([(L, T)] if W > L else [])
            with nc.Block() as block:
                @block.sync
                def _(sp):
                    sp.sem_clear(N.range)
                    issue(sp, src1, u0, u0 + 4, NU1, S.pe_tile, 2)

                @block.tensor
                def _(pe):
                    for i in range(KT):
                        if i % 2 == 0:
                            arrived(pe, u0 + i // 2)
                        if i >= 4:
                            pe.wait_ge(S.dve_out, i - 3)
                        w = unit(u0 + i // 2).rearrange("p (k n) -> p k n", k=KT)[:, :, (i % 2) * P:(i % 2 + 1) * P]
                        for a, b in parts:
                            for k in range(KT):
                                last = nc.tensor.matmul(wide(i)[:, a:b], w[:, k, :], y[:, k, a:b],
                                                        start=(k == 0), stop=(k == KT - 1))
                        last.then_inc(S.pe_tile, 1)

                @block.vector
                def _(dve):
                    for i in range(KT):
                        dve.wait_ge(S.pe_tile, i + 1)
                        for who, (a, b) in enumerate(parts):
                            last = nc.vector.scalar_tensor_tensor(X[:, i, a:b], wide(i)[:, a:b], modv(l, 2, who, i),
                                                                  X[:, i, a:b], O.mult, O.add)
                        last.then_inc(S.dve_out, 1)

        def stage_layer_norm(l, W, sq, tmp):
            S, N = stage_sems()
            parts = [(0, L)] + ([(L, T)] if W > L else [])
            mean = PS[:, 0:2, :].rearrange("p b n -> p (b n)")
            var = PS[:, 2:4, :].rearrange("p b n -> p (b n)")
            with nc.Block() as block:
                @block.sync
                def _(sp):
                    sp.sem_clear(N.range)

                @block.tensor
                def _(pe):
                    for a, b in parts:
                        for k in range(KT):
                            last = nc.tensor.matmul(mean[:, a:b], ones, X[:, k, a:b], start=(k == 0),
                                                    stop=(k == KT - 1))
                    last.then_inc(S.sums, 1)
                    for k in range(KT):
                        pe.wait_ge(S.squares, k + 1)
                        for a, b in parts:
                            last = nc.tensor.matmul(var[:, a:b], ones, sq[:, k, a:b], start=(k == 0),
                                                    stop=(k == KT - 1))
                    last.then_inc(S.sums, 1)

                @block.scalar
                def _(act):
                    for k in range(KT):
                        act.wait_ge(S.dve_out, k + 1)
                        nc.scalar.activation(sq[:, k, 0:W], X[:, k, 0:W], A.Square).then_inc(S.squares, 1)
                    act.wait_ge(S.sums, 2)
                    nc.scalar.activation(tmp[:, 0:W], var[:, 0:W], A.Sqrt, bias=const("eps")[:, 0:1], scale=1.0 / D)\
                        .then_inc(S.act_out, 1)
                    for k in range(KT):
                        act.wait_ge(S.normed, k + 1)
                        nc.scalar.activation(X[:, k, 0:W], X[:, k, 0:W], A.Identity, bias=vec1(f"ln_b{l}", k),
                                             scale=vec1(f"ln_g{l}", k))

                @block.vector
                def _(dve):
                    dve.wait_ge(S.sums, 1)
                    for k in range(KT):
                        nc.vector.scalar_tensor_tensor(X[:, k, 0:W], mean[:, 0:W], -1.0 / D, X[:, k, 0:W],
                                                       O.mult, O.add).then_inc(S.dve_out, 1)
                    dve.wait_ge(S.act_out, 1)
                    dve.wait_ge(S.dve_out, KT)
                    nc.vector.reciprocal(tmp[:, 0:W], tmp[:, 0:W]).then_inc(S.dve_step, 1)
                    dve.wait_ge(S.dve_step, 1)
                    dve.wait_ge(S.squares, KT)
                    for k in range(KT):
                        nc.vector.tensor_tensor(X[:, k, 0:W], X[:, k, 0:W], tmp[:, 0:W], O.mult)\
                            .then_inc(S.normed, 1)

        c = Carve()
        yh = c(CH * L).rearrange("p (j t) -> p j t", j=CH)
        hq = [c(2 * L).rearrange("p (j t) -> p j t", j=2) for _ in range(2)]
        hz = [c(4 * T).rearrange("p (d j t) -> p d j t", d=2, j=2) for _ in range(2)]
        hi = [c(6 * 256).rearrange("p (i n) -> p i n", i=6), X[:, 0:6, L:T]]
        buf_t1 = [c(T), c(T)]
        buf_lf = [c(T), c(T)]
        buf_k = [c(T), c(T)]
        buf_b = [c(T), c(T)]
        buf_eb = [c(L), c(L)]
        buf_x = [c(LEV * L), c(LEV * L)]
        buf_kt = c(5 * P)
        buf_s = [c(4 * P), c(4 * P)]
        prod = c(1024)
        am = [c(P), c(P)]

        C_TILES = [("q", 0, 0), ("q", 1, 0), ("z", 0, 1), ("z", 1, 1), ("z", 2, 2), ("z", 3, 2), ("i", 0, 3),
                   ("i", 1, 3), ("g", 0, 4), ("g", 1, 4)]

        def stage_c(step):
            S, N = stage_sems()
            u0 = U1["c_in"] + 5 * step
            projects, scans = step < CH // 2, step > 0
            qn, zn, iv = hq[step % 2], hz[step % 2], hi[step % 2]
            q_, z_, i_ = hq[(step + 1) % 2], hz[(step + 1) % 2], hi[(step + 1) % 2]
            pair = step - 1

            def rev(ap):
                return ap[:, ::-1]

            def levels(v, lev):
                w = v.rearrange("p (n s b) -> p n s b", s=2, b=1 << lev)
                return w[:, :, 0, :], w[:, :, 1, :]

            def bank2(b):
                return PS[:, b:b + 2, :].rearrange("p b n -> p (b n)")

            def order(dr):
                return list(range(NB)) if dr == 0 else list(range(NB))[::-1]

            def exponents(eng, dr):
                b = buf_b[dr]
                for lev in range(LEV):
                    B = 1 << lev
                    left, right = levels(b[:, 0:L], lev)
                    xl, xr = levels(buf_x[dr][:, lev * L:(lev + 1) * L], lev)
                    n = L // (2 * B)
                    if dr == 0:
                        ref = left[:, :, B - 1:B].to_broadcast([P, n, B])
                        eng.tensor_tensor(xr, right, ref, O.subtract)
                        last = eng.tensor_tensor(xl, ref, left, O.subtract)
                    else:
                        ref = right[:, :, 0:1].to_broadcast([P, n, B])
                        eng.tensor_tensor(xl, left, ref, O.subtract)
                        last = eng.tensor_tensor(xr, ref, right, O.subtract)
                return last

            with nc.Block() as block:
                @block.sync
                def _(sp):
                    sp.sem_clear(N.range)
                    if projects:
                        issue(sp, src1, u0, u0 + 5, NU1, S.pe_tile, 2)

                if scans:
                    @block.gpsimd
                    def _(pool):
                        for j in range(2):
                            pool.wait_ge(S.decays, j + 1)
                            exponents(nc.gpsimd, 1).then_inc(S.ready, 1)

                @block.vector
                def _(dve):
                    steps = [0]

                    def link(ins):
                        steps[0] += 1
                        ins.then_inc(S.dve_step, 1)
                        dve.wait_ge(S.dve_step, steps[0])

                    def gate_sum(j, dr):
                        u = 2 * j + dr
                        z = z_[:, dr, j, :]
                        t1, lf, b = buf_t1[dr], buf_lf[dr], buf_b[dr]
                        dve.wait_ge(S.absolute, u + 1)
                        if j >= 1:
                            dve.wait_ge(S.head_root, j)
                        link(nc.vector.scalar_tensor_tensor(lf, z, 0.0, t1, O.min, O.subtract))
                        nc.vector.tensor_tensor(t1, lf, z, O.subtract).then_inc(S.log_k, 1)
                        if dr == 0:
                            nc.vector.tensor_tensor_scan(b[:, 0:L], const("reset"), lf[:, 0:L], 0.0, O.mult, O.add)
                            link(nc.vector.tensor_tensor_scan(b[:, L:T], const("one"), lf[:, L:T], 0.0,
                                                              O.mult, O.add))
                        else:
                            nc.vector.tensor_tensor_scan(rev(b[:, 0:L]), const("reset"), rev(lf[:, 0:L]), 0.0,
                                                         O.mult, O.add)
                            nc.vector.tensor_tensor_scan(rev(b[:, L:T]), const("one"), rev(lf[:, L:T]), 0.0,
                                                         O.mult, O.add).then_inc(S.decays, 1)
                            dve.wait_ge(S.decays, j + 1)
                        end = P - 1 if dr == 0 else 0
                        b4 = b[:, 0:L].rearrange("p (n c) -> p n c", c=P)
                        nc.vector.tensor_tensor(lf[:, 0:L].rearrange("p (n c) -> p n c", c=P),
                                                b4[:, :, end:end + 1].to_broadcast([P, NB, P]), b4, O.subtract)
                        cend = T - 1 if dr == 0 else L
                        last = nc.vector.tensor_tensor(lf[:, L:T], b[:, cend:cend + 1].to_broadcast([P, LC]),
                                                       b[:, L:T], O.subtract)
                        if dr == 0:
                            last = exponents(nc.vector, 0)
                        last.then_inc(S.exponents, 1)

                    def weigh(j, dr):
                        q, k_ = q_[:, j, :], buf_k[dr]
                        dve.wait_ge(S.weights, 2 * j + dr + 1)
                        nc.vector.tensor_tensor(buf_t1[dr][:, 0:L], q, buf_eb[dr], O.mult)
                        nc.vector.tensor_tensor(buf_lf[dr], buf_lf[dr], k_, O.mult).then_inc(S.state_keys, 1)
                        for lev in range(LEV):
                            xl, xr = levels(buf_x[dr][:, lev * L:(lev + 1) * L], lev)
                            ql, qr = levels(q, lev)
                            kl, kr = levels(k_[:, 0:L], lev)
                            if dr == 0:
                                nc.vector.tensor_tensor(xr, xr, qr, O.mult)
                                last = nc.vector.tensor_tensor(xl, xl, kl, O.mult)
                            else:
                                nc.vector.tensor_tensor(xl, xl, ql, O.mult)
                                last = nc.vector.tensor_tensor(xr, xr, kr, O.mult)
                        last.then_inc(S.levelled, 1)

                    def states(j, dr):
                        u = 2 * j + dr
                        s, eb = buf_s[dr], buf_eb[dr]
                        dve.wait_ge(S.flipped, u + 1)
                        nc.vector.tensor_copy(buf_kt, bank2(2 * dr)[:, 0:5 * P]).then_inc(S.copied, 1)
                        dve.wait_ge(S.own, u + 1)
                        end = P - 1 if dr == 0 else 0
                        for i in range(NB):
                            o = s[:, i * P:(i + 1) * P]
                            if i == 0:
                                link(nc.vector.tensor_copy(o, PS[:, 4, 0:P]))
                            else:
                                dec = order(dr)[i - 1] * P + end
                                link(nc.vector.scalar_tensor_tensor(o, s[:, (i - 1) * P:i * P], eb[:, dec:dec + 1],
                                                                    PS[:, 4, i * P:(i + 1) * P], O.mult, O.add))

                    def masks(j, n):
                        i = j * NB + n
                        for dr in range(2):
                            dve.wait_ge(S.products, 2 * i + dr + 1)
                            m = constb("scan")[:, dr * 1024:(dr + 1) * 1024]
                            nc.vector.tensor_tensor(prod, bank2(2 * dr), m, O.mult).then_inc(S.masked, 1)
                            dve.wait_ge(S.masked, 2 * i + dr + 1)
                            if dr == 0 and i >= 1:
                                dve.wait_ge(S.chunk_out, i)
                            link(nc.vector.tensor_reduce(am[dr], prod.rearrange("p (l c) -> p c l", l=8), AX, O.add))
                        nc.vector.tensor_tensor(am[0], am[0], am[1], O.add).then_inc(S.summed, 1)

                    if scans:
                        link(nc.vector.tensor_scalar(q_, q_, KSCALE, None, O.mult))
                        for j in range(2):
                            gate_sum(j, 0)
                            gate_sum(j, 1)
                            for dr in range(2):
                                weigh(j, dr)
                                states(j, dr)
                            for n in range(NB):
                                masks(j, n)
                            o = buf_b[0][:, 0:L]
                            dve.wait_ge(S.chunk_out, NB * (j + 1))
                            nc.vector.tensor_copy(o, PS[:, 5, :]).then_inc(S.head_copied, 1)
                            dve.wait_ge(S.head_root, j + 1)
                            link(nc.vector.reciprocal(buf_eb[0], buf_eb[0]))
                            link(nc.vector.scalar_tensor_tensor(o, o, vec1("gnorm"), buf_eb[0], O.mult, O.mult))
                            y = yh[:, 2 * pair + j, :]
                            nc.vector.tensor_tensor(y, y, o, O.mult).then_inc(S.normed, 1)

                @block.scalar
                def _(act):
                    def empty(i):
                        if not projects:
                            return
                        kind, j, u = C_TILES[i]
                        act.wait_ge(S.pe_tile, i + 1)
                        if kind == "q":
                            ins = nc.scalar.activation(qn[:, j, :], bank2(6)[:, 0:L], A.Silu)
                        elif kind == "z":
                            ins = nc.scalar.activation(zn[:, j // 2, j % 2, :], bank2(6)[:, 0:T], A.Copy)
                        elif kind == "g":
                            ins = nc.scalar.activation(yh[:, 2 * step + j, :], bank2(6)[:, 0:L], A.Silu)
                        else:
                            n = 4 if j == 0 else 2
                            ins = nc.scalar.activation(iv[:, 4 * j:4 * j + n, :],
                                                       bank2(6)[:, 0:n * 256].rearrange("p (i n) -> p i n", i=n),
                                                       A.Copy)
                        ins.then_inc(S.act_out, 1)

                    steps = [0]

                    def link(ins):
                        steps[0] += 1
                        ins.then_inc(S.act_step, 1)
                        act.wait_ge(S.act_step, steps[0])

                    def weights(j, dr):
                        u = 2 * j + dr
                        act.wait_ge(S.log_k, u + 1)
                        nc.scalar.activation(buf_k[dr], buf_t1[dr], A.Exp)
                        act.wait_ge(S.exponents, u + 1)
                        nc.scalar.activation(buf_eb[dr], buf_b[dr][:, 0:L], A.Exp)
                        link(nc.scalar.activation(buf_lf[dr], buf_lf[dr], A.Exp))
                        if dr == 1:
                            act.wait_ge(S.ready, j + 1)
                        nc.scalar.activation(buf_x[dr], buf_x[dr], A.Exp).then_inc(S.weights, 1)

                    for j in range(2):
                        if scans:
                            for dr in range(2):
                                link(nc.scalar.activation(buf_t1[dr], z_[:, dr, j, :], A.Abs))
                            for t1 in buf_t1:
                                link(nc.scalar.activation(t1, t1, A.Exp, scale=-1.0))
                            for t1 in buf_t1:
                                nc.scalar.activation(t1, t1, A.Ln, bias=1.0).then_inc(S.absolute, 1)
                        empty(5 * j)
                        empty(5 * j + 1)
                        if scans:
                            weights(j, 0)
                        empty(5 * j + 2)
                        if scans:
                            weights(j, 1)
                        empty(5 * j + 3)
                        empty(5 * j + 4)
                        if scans:
                            act.wait_ge(S.head_copied, j + 1)
                            nc.scalar.activation(buf_k[0][:, 0:L], buf_b[0][:, 0:L], A.Square)\
                                .then_inc(S.head_squared, 1)
                            act.wait_ge(S.head_sum, j + 1)
                            nc.scalar.activation(buf_eb[0], PS[:, 5, :], A.Sqrt, bias=const("eps")[:, 1:2],
                                                 scale=1.0 / P).then_inc(S.head_root, 1)

                @block.tensor
                def _(pe):
                    def tile(i):
                        if not projects:
                            return
                        kind, j, u = C_TILES[i]
                        if i % 2 == 0:
                            arrived(pe, u0 + u)
                        if i >= 1:
                            pe.wait_ge(S.act_out, i)
                        w = unit(u0 + u).rearrange("p (k n) -> p k n", k=KT)
                        ps = bank2(6)
                        if kind == "i":
                            for m in (range(4) if j == 0 else range(4, 6)):
                                for k in range(KT):
                                    last = nc.tensor.matmul(ps[:, (m % 4) * 256:(m % 4 + 1) * 256],
                                                            AT[:, k, m * P:(m + 1) * P], w[:, k, :],
                                                            start=(k == 0), stop=(k == KT - 1))
                        else:
                            for a, b in ((0, L), (L, T)) if kind == "z" else ((0, L),):
                                for k in range(KT):
                                    last = nc.tensor.matmul(ps[:, a:b], w[:, k, (j % 2) * P:(j % 2 + 1) * P],
                                                            AT[:, k, a:b], start=(k == 0), stop=(k == KT - 1))
                        last.then_inc(S.pe_tile, 1)

                    def own_states(j, dr):
                        if not scans:
                            return
                        u = 2 * j + dr
                        od = order(dr)
                        pe.wait_ge(S.state_keys, u + 1)
                        if dr == 0 and j >= 1:
                            pe.wait_ge(S.summed, NB * j)
                        for i in range(5):
                            a = L + i * P if i < 2 else od[i - 2] * P
                            last = nc.tensor.transpose(bank2(2 * dr)[:, i * P:(i + 1) * P], buf_lf[dr][:, a:a + P], ident)
                        last.then_inc(S.flipped, 1)
                        pe.wait_ge(S.copied, u + 1)
                        v = i_[:, :, j * P:(j + 1) * P]
                        for i in range(2):
                            nc.tensor.matmul(PS[:, 4, 0:P], buf_kt[:, i * P:(i + 1) * P], v[:, 4 + i, :],
                                             start=(i == 0), stop=(i == 1))
                        for i in range(3):
                            last = nc.tensor.matmul(PS[:, 4, (i + 1) * P:(i + 2) * P],
                                                    buf_kt[:, (2 + i) * P:(3 + i) * P], v[:, od[i], :],
                                                    start=True, stop=True)
                        last.then_inc(S.own, 1)

                    def products(j, n, dr):
                        i = 2 * (j * NB + n) + dr
                        cs = slice(n * P, (n + 1) * P)
                        pe.wait_ge(S.levelled, 2 * j + dr + 1)
                        if n > 0:
                            pe.wait_ge(S.masked, i - 1)
                        for lev in range(LEV):
                            xv = buf_x[dr][:, lev * L + n * P:lev * L + (n + 1) * P]
                            nc.tensor.matmul(bank2(2 * dr)[:, lev * P:(lev + 1) * P], xv, xv, start=True, stop=True)
                        nc.tensor.matmul(bank2(2 * dr)[:, LEV * P:(LEV + 1) * P], buf_k[dr][:, cs], q_[:, j, cs],
                                         start=True, stop=True).then_inc(S.products, 1)

                    def chunk(j, n):
                        i = j * NB + n
                        cs = slice(n * P, (n + 1) * P)
                        if n == 0 and j >= 1:
                            pe.wait_ge(S.head_root, j)
                        pe.wait_ge(S.summed, i + 1)
                        o = PS[:, 5, cs]
                        nc.tensor.matmul(o, buf_s[0][:, cs], buf_t1[0][:, cs], start=True, stop=False)
                        r = NB - 1 - n
                        nc.tensor.matmul(o, buf_s[1][:, r * P:(r + 1) * P], buf_t1[1][:, cs], start=False, stop=False)
                        nc.tensor.matmul(o, i_[:, n, j * P:(j + 1) * P], am[0], start=False, stop=True)\
                            .then_inc(S.chunk_out, 1)

                    for j in range(2):
                        for i in range(3):
                            tile(5 * j + i)
                        own_states(j, 0)
                        tile(5 * j + 3)
                        own_states(j, 1)
                        tile(5 * j + 4)
                        if scans:
                            for n in range(NB):
                                products(j, n, 0)
                                products(j, n, 1)
                                if n >= 1:
                                    chunk(j, n - 1)
                            chunk(j, NB - 1)
                            pe.wait_ge(S.head_squared, j + 1)
                            nc.tensor.matmul(PS[:, 5, :], ones, buf_k[0][:, 0:L], start=True, stop=True)\
                                .then_inc(S.head_sum, 1)

        stage_load()
        stage_mod(0, U1["ada0"])
        stage_modulate(0)
        stage_ab_in()
        cos1, sin1 = ca[:, CA["cos1"][0]:CA["cos1"][1]], ca[:, CA["sin1"][0]:CA["sin1"][1]]
        stage_rope([(qT[:, j, 0:L], cos1, sin1, L) for j in range(NT4)] + [(kT[:, 0:L], cos1, sin1, L)],
                   const("r1"), xbt[:, 0, 0:L])
        stage_ab_attention()
        stage_out1(0, U1["ab_out"], yin, T)
        c = Carve()
        sq1, tmp1 = c(KT * T).rearrange("p (k t) -> p k t", k=KT), c(T + 1)
        stage_layer_norm(0, T, sq1, tmp1)
        stage_mod(1, U1["ada1"])
        stage_modulate(1)
        for step in range(CH // 2 + 1):
            stage_c(step)
        stage_out1(1, U1["c_out"], yh, L)
        stage_layer_norm(1, L, sq1, tmp1)
        first.close()

        raw_ring = sb("raw_ring", RAW * UNIT)
        w_high, w_low = sb("w_high", SLOTS * UNIT, f32r), sb("w_low", SLOTS * UNIT, f32r)
        a_high, a_low = sb("a_high", KT * L, f32r), sb("a_low", KT * L, f32r)
        gate_high, gate_low = sb("gate_high", KT * 24, f32r), sb("gate_low", KT * 24, f32r)
        arena2 = sb("arena2", 23019)
        ah = [a_high[:, k * L:(k + 1) * L] for k in range(KT)]
        al = [a_low[:, k * L:(k + 1) * L] for k in range(KT)]
        c = Carve(0, arena2)
        rows = c(NR2)
        wgate = c(KT * 24)
        rstd = c(2 * L).rearrange("p (g t) -> p g t", g=2)
        cg = c(NCG)
        fbuf_at = c.at
        fbuf = c(KT * L).rearrange("p (k t) -> p k t", k=KT)
        sq_at = c.at
        sq = c(KT * L).rearrange("p (k t) -> p k t", k=KT)
        hid_at = sq_at
        scratch_at = fbuf_at
        c = Carve(scratch_at + 5144, arena2)
        q2 = c(NT4 * L).rearrange("p (j t) -> p j t", j=NT4)
        ksw = c(2 * L).rearrange("p (b t) -> p b t", b=2)
        assert c.at > sq_at + KT * L
        y2 = c(KT * L).rearrange("p (k t) -> p k t", k=KT)
        zu = y2[:, NT4:, :]
        after_y2 = c.at
        pcT = c(NB * 2 * P).rearrange("p (i g q) -> p i g q", i=NB, g=2)
        kvc = arena2[:, after_y2:after_y2 + 2 * L].rearrange("p (g t) -> p g t", g=2)
        vt2 = c(NB * 256).rearrange("p (i n) -> p i n", i=NB)
        zv = c(NB * L).rearrange("p (i n) -> p i n", i=NB)
        gates = c(NB * 24).rearrange("p (i n) -> p i n", i=NB)
        wsT = c(NH * P).rearrange("p (g t) -> p g t", g=NH)
        hT = c(4 * 64).rearrange("p (v h n) -> p v h n", v=2, h=2)
        kcT = c(64)
        vcr = c(2 * HD).rearrange("p (g e) -> p g e", g=2)
        c = Carve(scratch_at, arena2)
        blk = c(32 * 64)
        blk4 = blk.rearrange("p (l g n) -> p l g n", l=32, g=2)
        blk3 = blk.rearrange("p (l n) -> p l n", l=32)
        raw_h = c(2 * 256)
        blocks = a_high[:, :].rearrange("p (l s n) -> p l s n", l=32, s=2)
        c = Carve(hid_at, arena2)
        hid = c(FT * L).rearrange("p (j t) -> p j t", j=FT)
        c = Carve(fbuf_at, arena2)
        hc = c(2 * 2 * L).rearrange("p (b s t) -> p b s t", b=2, s=2)
        c = Carve(hid_at + KT * L, arena2)
        pT = c(2 * L).rearrange("p (k t) -> p k t", k=2)
        pg = c(KT * L).rearrange("p (k t) -> p k t", k=KT)

        def const2(name):
            return cg[:, CG[name][0]:CG[name][1]]

        def raw(n):
            return raw_ring[:, (n % RAW) * UNIT:(n % RAW + 1) * UNIT]

        def high(n):
            return w_high[:, (n % SLOTS) * UNIT:(n % SLOTS + 1) * UNIT]

        def low(n):
            return w_low[:, (n % SLOTS) * UNIT:(n % SLOTS + 1) * UNIT]

        def stream_raw(sp, src, a, b):
            for n in range(a + RAW + 1, min(b + RAW + 1, NSPLIT + 1)):
                if n - RAW < NSPLIT:
                    sp.wait_ge(w_split, n - RAW + 1)
                sp.dma_start(raw(n), src(n)).then_inc(w_arrived[n % RAW], 16)

        def split_high(act, S, a, n):
            if n >= NSPLIT:
                return
            act.wait_ge(w_arrived[n % RAW], 16 * (n // RAW + 1))
            if n - SLOTS >= a:
                act.wait_ge(S.pe_tile, n - SLOTS - a + 1)
            nc.scalar.activation(high(n), raw(n), A.Copy).then_inc(w_hi, 1)

        def split_low(dve, n):
            if n >= NSPLIT:
                return
            dve.wait_ge(w_hi, n + 1)
            nc.vector.tensor_tensor(low(n), raw(n), high(n).bitcast(f32), O.subtract).then_inc(w_split, 1)

        def product3(out, wh, wl, xh, xl, start, stop):
            nc.tensor.matmul(out, wh, xh, start=start, stop=False)
            nc.tensor.matmul(out, wh, xl, start=False, stop=False)
            return nc.tensor.matmul(out, wl, xh, start=False, stop=stop)

        def row(name):
            return rows[:, R2[name][0]:R2[name][1]]

        def bank2(b):
            return PS[:, b:b + 2, :].rearrange("p b n -> p (b n)")

        class Normalise:
            def __init__(self, S, groups):
                self.S, self.groups = S, groups
                self.flat = [(g, k) for g, (src, _gain) in enumerate(groups) for k in range(len(src))]

            def squares(self, act):
                for i, (g, k) in enumerate(self.flat):
                    nc.scalar.activation(sq[:, i, :], self.groups[g][0][k], A.Square)\
                        .then_inc(self.S.rms_squares, 1)

            def high(self, act):
                for g, (src, _gain) in enumerate(self.groups):
                    act.wait_ge(self.S.rms_sums, g + 1)
                    nc.scalar.activation(rstd[:, g, :], PS[:, 6 + g, :], A.Sqrt, bias=const("eps")[:, 1:2],
                                         scale=1.0 / (P * len(src))).then_inc(self.S.rms_root, 1)
                for i in range(KT):
                    act.wait_ge(self.S.rms_scaled, i + 1)
                    nc.scalar.activation(ah[i], sq[:, i, :], A.Copy).then_inc(self.S.rms_high, 1)

            def sums(self, pe):
                for i, (g, k) in enumerate(self.flat):
                    pe.wait_ge(self.S.rms_squares, i + 1)
                    n = len(self.groups[g][0])
                    ins = nc.tensor.matmul(PS[:, 6 + g, :], ones, sq[:, i, :], start=(k == 0), stop=(k == n - 1))
                    if k == n - 1:
                        ins.then_inc(self.S.rms_sums, 1)

            def low(self, eng, which, i):
                if i >= 0 and i % 2 == which:
                    eng.wait_ge(self.S.rms_high, i + 1)
                    (nc.vector if which else nc.gpsimd).tensor_tensor(
                        al[i], sq[:, i, :], ah[i].bitcast(f32), O.subtract)\
                        .then_inc(self.S.rms_odd if which else self.S.rms_even, 1)

            def scale(self, dve):
                for g in range(len(self.groups)):
                    dve.wait_ge(self.S.rms_root, g + 1)
                    nc.vector.reciprocal(rstd[:, g, :], rstd[:, g, :]).then_inc(self.S.rms_step, 1)
                    dve.wait_ge(self.S.rms_step, g + 1)
                    for i, (gi, k) in enumerate(self.flat):
                        if gi == g:
                            src, gain = self.groups[g]
                            nc.vector.scalar_tensor_tensor(sq[:, i, :], src[k], gain(k), rstd[:, g, :],
                                                           O.mult, O.mult).then_inc(self.S.rms_scaled, 1)
                            self.low(dve, 1, i - 1)
                self.low(dve, 1, KT - 1)

            def even(self, pool):
                for i in range(KT):
                    self.low(pool, 0, i)

            def tile(self, pe, k):
                if k % 2:
                    pe.wait_ge(self.S.rms_odd, k // 2 + 1)
                else:
                    pe.wait_ge(self.S.rms_even, k // 2 + 1)

        def stage_residual(gain):
            S, N = stage_sems()
            with nc.Block() as block:
                @block.sync
                def _(sp):
                    sp.sem_clear(N.range)

                @block.scalar
                def _(act):
                    for k in range(KT):
                        nc.scalar.activation(sq[:, k, :], fbuf[:, k, :], A.Square).then_inc(S.squares, 1)
                    act.wait_ge(S.sums, 1)
                    nc.scalar.activation(rstd[:, 0, :], PS[:, 0, :], A.Sqrt, bias=const("eps")[:, 1:2],
                                         scale=1.0 / D).then_inc(S.act_out, 1)

                @block.tensor
                def _(pe):
                    for k in range(KT):
                        pe.wait_ge(S.squares, k + 1)
                        last = nc.tensor.matmul(PS[:, 0, :], ones, sq[:, k, :], start=(k == 0), stop=(k == KT - 1))
                    last.then_inc(S.sums, 1)

                @block.vector
                def _(dve):
                    def add(k):
                        if k >= 0 and k % 2:
                            dve.wait_ge(S.normed, k + 1)
                            nc.vector.tensor_tensor(X[:, k, 0:L], X[:, k, 0:L], sq[:, k, :], O.add)

                    dve.wait_ge(S.act_out, 1)
                    nc.vector.reciprocal(rstd[:, 0, :], rstd[:, 0, :]).then_inc(S.dve_step, 1)
                    dve.wait_ge(S.dve_step, 1)
                    for k in range(KT):
                        nc.vector.scalar_tensor_tensor(sq[:, k, :], fbuf[:, k, :], gain(k), rstd[:, 0, :],
                                                       O.mult, O.mult).then_inc(S.normed, 1)
                        add(k - 1)
                    add(KT - 1)

                @block.gpsimd
                def _(pool):
                    for k in range(0, KT, 2):
                        pool.wait_ge(S.normed, k + 1)
                        nc.gpsimd.tensor_tensor(X[:, k, 0:L], X[:, k, 0:L], sq[:, k, :], O.add)

        def layer2(layer):
            def src2(n):
                return d["w2"][layer, n, :, :]

            def small_loads(sp, S):
                sp.sem_clear(w_range)
                for n in range(RAW):
                    sp.dma_start(raw(n), src2(n)).then_inc(w_arrived[n], 16)
                sp.dma_start(v2[:, :], d["v2"][layer, :, :]).then_inc(S.load, 16)
                sp.dma_start(rows, d["r2"][layer, :, :]).then_inc(S.load, 16)
                sp.dma_start(wgate, d["wgate"][layer, :, :]).then_inc(S.load, 16)
                sp.dma_start(wsT.rearrange("p g t -> p (g t)"), d["wsT"][layer, :, :]).then_inc(S.load, 16)
                return 64

            def stage_loads():
                S, N = stage_sems()
                with nc.Block() as block:
                    @block.sync
                    def _(sp):
                        sp.sem_clear(N.range)
                        sp.wait_ge(S.load, small_loads(sp, S))

            xt = [X[:, k, 0:L] for k in range(KT)]

            def stage_in2(groups):
                S, N = stage_sems()
                norm = Normalise(S, groups)
                u0 = U2["in2"]
                with nc.Block() as block:
                    @block.sync
                    def _(sp):
                        sp.sem_clear(N.range)
                        stream_raw(sp, src2, u0 - 1, u0 + 9)

                    @block.gpsimd
                    def _(pool):
                        norm.even(pool)

                    @block.tensor
                    def _(pe):
                        norm.sums(pe)
                        for u in range(10):
                            if u < 9:
                                pe.wait_ge(w_split, u0 + u + 1)
                            else:
                                pe.wait_ge(S.dve_step, 1)
                            if u >= 4:
                                pe.wait_ge(S.act_out, u - 3)
                            ps = bank2(2 * (u % 4))
                            wh, wl = [v.rearrange("p (k n) -> p k n", k=KT) for v in
                                      ((high(u0 + u), low(u0 + u)) if u < 9 else (gate_high[:, :], gate_low[:, :]))]
                            if u in (4, 7, 8, 9):
                                n = 24 if u == 9 else 256
                                for m in range(NB):
                                    ts = slice(m * P, (m + 1) * P)
                                    for k in range(KT):
                                        last = product3(ps[:, m * n:(m + 1) * n], ah[k][:, ts], al[k][:, ts],
                                                        wh[:, k, :], wl[:, k, :], k == 0, k == KT - 1)
                            else:
                                for h in range(2):
                                    hs = slice(h * P, (h + 1) * P)
                                    for k in range(KT):
                                        if u + h == 0:
                                            norm.tile(pe, k)
                                        last = product3(ps[:, h * L:(h + 1) * L], wh[:, k, hs], wl[:, k, hs],
                                                        ah[k], al[k], k == 0, k == KT - 1)
                            last.then_inc(S.pe_tile, 1)

                    @block.scalar
                    def _(act):
                        norm.squares(act)
                        split_high(act, S, u0, u0)
                        nc.scalar.activation(gate_high[:, :], wgate, A.Copy).then_inc(S.act_step, 1)
                        norm.high(act)
                        for u in range(10):
                            if u < 9:
                                split_high(act, S, u0, u0 + u + 1)
                            act.wait_ge(S.pe_tile, u + 1)
                            ps = bank2(2 * (u % 4))
                            if u < 2:
                                ins = nc.scalar.activation(q2[:, 2 * u:2 * u + 2, :], ps.rearrange(
                                    "p (j t) -> p j t", j=2), A.Copy)
                            elif u == 2:
                                ins = nc.scalar.activation(kvc, ps.rearrange("p (j t) -> p j t", j=2), A.Copy)
                            elif u == 3:
                                ins = nc.scalar.activation(ksw, ps.rearrange("p (j t) -> p j t", j=2), A.Copy)
                            elif u == 4:
                                ins = nc.scalar.activation(vt2, ps.rearrange("p (j t) -> p j t", j=4), A.Copy)
                            elif u < 7:
                                ins = nc.scalar.activation(zu[:, 2 * (u - 5):2 * (u - 5) + 2, :], ps.rearrange(
                                    "p (j t) -> p j t", j=2), A.Gelu_apprx_tanh)
                            elif u < 9:
                                ins = nc.scalar.activation(zv[:, :, 256 * (u - 7):256 * (u - 6)], ps.rearrange(
                                    "p (j t) -> p j t", j=4), A.Gelu_apprx_tanh)
                            else:
                                ins = nc.scalar.activation(gates, ps[:, 0:96].rearrange("p (i n) -> p i n", i=NB),
                                                           A.Sigmoid)
                            ins.then_inc(S.act_out, 1)

                    @block.vector
                    def _(dve):
                        split_low(dve, u0)
                        dve.wait_ge(S.act_step, 1)
                        nc.vector.tensor_tensor(gate_low[:, :], wgate, gate_high[:, :].bitcast(f32), O.subtract)\
                            .then_inc(S.dve_step, 1)
                        norm.scale(dve)
                        for u in range(9):
                            split_low(dve, u0 + u + 1)

            def stage_compress():
                S, N = stage_sems()
                u0 = U2["cmp1"]
                with nc.Block() as block:
                    @block.sync
                    def _(sp):
                        sp.sem_clear(N.range)
                        stream_raw(sp, src2, u0, u0 + 4)

                    @block.gpsimd
                    def _(pool):
                        src = blk4[:, :, :, NCMP:32]
                        nc.gpsimd.memset(src, 0.0).then_inc(S.ready, 1)

                    @block.vector
                    def _(dve):
                        pe_ = v2[:, V2["pe"][0]:V2["pe"][1]]
                        for a in range(2):
                            for g in range(2):
                                src = kvc[:, g, 16 * a:16 * a + 16 * NCMP].rearrange("p (n b) -> p b n", b=16)
                                last = nc.vector.tensor_tensor(
                                    blk4[:, 16 * a:16 * a + 16, g, 0:NCMP], src,
                                    pe_[:, 16 * a:16 * a + 16].unsqueeze(2).to_broadcast([P, 16, NCMP]), O.add)
                            last.then_inc(S.dve_step, 1)
                        for a in range(2):
                            ls = slice(16 * a, 16 * a + 16)
                            dve.wait_ge(S.copied, a + 1)
                            nc.vector.tensor_tensor(blocks[:, ls, 1, :], blk3[:, ls, :],
                                                    blocks[:, ls, 0, :].bitcast(f32), O.subtract)\
                                .then_inc(S.normed, 1)
                        for u in range(4):
                            split_low(dve, u0 + u + 1)
                        dve.wait_ge(S.pe_tile, 6)
                        nc.vector.tensor_tensor(vcr, PS[:, 5, 0:P].rearrange("p (g e) -> p g e", g=2),
                                                row("b2v").unsqueeze(1).to_broadcast([P, 2, HD]), O.add)

                    @block.tensor
                    def _(pe):
                        for u in range(4):
                            pe.wait_ge(w_split, u0 + u + 1)
                            wh, wl = [v.rearrange("p (l n) -> p l n", l=8) for v in (high(u0 + u), low(u0 + u))]
                            if u in (0, 2):
                                pe.wait_ge(S.normed, u // 2 + 1)
                            for l8 in range(8):
                                l_ = 8 * u + l8
                                for w in (wh, wl):
                                    for kv in range(2):
                                        hs = slice(HD * kv, HD * kv + HD)
                                        last = nc.tensor.matmul(
                                            PS[:, kv, 0:256], blocks[hs, l_, :, :].rearrange("p s n -> p (s n)"),
                                            w[hs, l8, :], start=(l_ == 0 and w is wh), stop=(l_ == 31 and w is wl))
                            last.then_inc(S.pe_tile, 1)
                        pe.wait_ge(S.act_out, 1)
                        for i in range(4):
                            last = nc.tensor.matmul(PS[:, 2, 64 * i:64 * i + 64], raw_h[:, i * P:(i + 1) * P],
                                                    const2("fold"), start=True, stop=True)
                        last.then_inc(S.flipped, 1)
                        pe.wait_ge(S.act_out, 5)
                        w2k = row("w2k").rearrange("p (h n) -> p h n", h=2)
                        w2v = row("w2v").rearrange("p (h n) -> p h n", h=2)
                        for h in range(2):
                            last = nc.tensor.matmul(PS[:, 4, 0:64], w2k[:, h, :], hT[:, 0, h, :], start=(h == 0),
                                                    stop=(h == 1))
                        last.then_inc(S.pe_tile, 1)
                        for r in range(4):
                            for g in range(2):
                                for h in range(2):
                                    last = nc.tensor.matmul(PS[32 * r:32 * r + 32, 5, g * HD:(g + 1) * HD],
                                                            hT[:, 1, h, 32 * g:32 * g + 32], w2v[:, h, :],
                                                            start=(h == 0), stop=(h == 1))
                        last.then_inc(S.pe_tile, 1)

                    @block.scalar
                    def _(act):
                        act.wait_ge(S.ready, 1)
                        for a in range(2):
                            ls = slice(16 * a, 16 * a + 16)
                            act.wait_ge(S.dve_step, a + 1)
                            nc.scalar.activation(blocks[:, ls, 0, :], blk3[:, ls, :], A.Copy).then_inc(S.copied, 1)
                        for u in range(4):
                            split_high(act, S, u0, u0 + u + 1)
                        act.wait_ge(S.pe_tile, 4)
                        nc.scalar.activation(raw_h.rearrange("p (v n) -> p v n", v=2), PS[:, 0:2, 0:256], A.Copy)\
                            .then_inc(S.act_out, 1)
                        act.wait_ge(S.flipped, 1)
                        for kv in range(2):
                            for h in range(2):
                                i = 2 * kv + h
                                nc.scalar.activation(hT[:, kv, h, :], PS[:, 2, 64 * i:64 * i + 64],
                                                     A.Gelu_apprx_tanh, bias=vec2("b1", i)).then_inc(S.act_out, 1)
                        act.wait_ge(S.pe_tile, 5)
                        nc.scalar.activation(kcT, PS[:, 4, 0:64], A.Identity, bias=vec2("b2k"))

            def stage_cmp_attention():
                S, N = stage_sems()
                cc = Carve(scratch_at, arena2)
                e = cc(NB * 256).rearrange("p (i n) -> p i n", i=NB)
                st = cc(NB * 32).rearrange("p (i n) -> p i n", i=NB)
                with nc.Block() as block:
                    @block.sync
                    def _(sp):
                        sp.sem_clear(N.range)

                    @block.tensor
                    def _(pe):
                        for n in range(NB):
                            m = constb("cmp")[:, n * 32:(n + 1) * 32].unsqueeze(1).to_broadcast([P, 4, 32])
                            for g in range(2):
                                hs = slice(HD * g, HD * g + HD)
                                nc.tensor.matmul(PS[:, n + 4 * g, 0:P], constb("ident"), m, start=True, stop=False)
                                for h in range(4):
                                    last = nc.tensor.matmul(PS[:, n + 4 * g, 32 * h:32 * h + 32],
                                                            q2[hs, h, n * P:(n + 1) * P],
                                                            kcT[hs, 32 * g:32 * g + 32], start=False, stop=(h == 3))
                            last.then_inc(S.scores, 1)
                        for n in range(NB):
                            pe.wait_ge(S.normed, n + 1)
                            for g in range(2):
                                last = nc.tensor.transpose(PS[:, n, g * P:(g + 1) * P],
                                                           e[:, n, g * P:(g + 1) * P], ident)
                            last.then_inc(S.flipped, 1)

                    @block.scalar
                    def _(act):
                        for n in range(NB):
                            act.wait_ge(S.shift, n + 1)
                            nc.scalar.activation(e[:, n, :], e[:, n, :], A.Exp).then_inc(S.probs, 1)
                        for n in range(NB):
                            act.wait_ge(S.flipped, n + 1)
                            nc.scalar.activation(pcT[:, n, :, :].rearrange("p g q -> p (g q)"), PS[:, n, 0:256],
                                                 A.Copy)

                    @block.vector
                    def _(dve):
                        steps = [0]

                        def link(ins):
                            steps[0] += 1
                            ins.then_inc(S.dve_step, 1)
                            dve.wait_ge(S.dve_step, steps[0])

                        def heads(v):
                            return v.rearrange("p (h n) -> p h n", h=NH)

                        for n in range(NB):
                            dve.wait_ge(S.scores, n + 1)
                            b = st[:, n, :]
                            ps = [PS[:, n + 4 * g, 0:P].rearrange("p (h n) -> p h n", h=4) for g in range(2)]
                            for g in range(2):
                                last = nc.vector.tensor_reduce(b[:, 4 * g:4 * g + 4], ps[g], AX, O.max)
                            link(last)
                            link(nc.vector.tensor_scalar(b[:, 8:16], b[:, 0:8], NEG / 10, -ASCALE, O.max, O.mult))
                            for g in range(2):
                                last = nc.vector.scalar_tensor_tensor(
                                    heads(e[:, n, :])[:, 4 * g:4 * g + 4, :], ps[g], ASCALE,
                                    b[:, 8 + 4 * g:12 + 4 * g].unsqueeze(2).to_broadcast([P, 4, 32]), O.mult, O.add)
                            last.then_inc(S.shift, 1)
                        for n in range(NB):
                            dve.wait_ge(S.probs, n + 1)
                            b = st[:, n, :]
                            ev = heads(e[:, n, :])
                            link(nc.vector.tensor_reduce(b[:, 16:24], ev, AX, O.add))
                            link(nc.vector.tensor_scalar(b[:, 16:24], b[:, 16:24], 1e-30, None, O.max))
                            link(nc.vector.reciprocal(b[:, 24:32], b[:, 16:24]))
                            g = gates[:, n, :].rearrange("p (h c) -> p c h", c=3)[:, 0, :]
                            link(nc.vector.tensor_tensor(b[:, 24:32], b[:, 24:32], g, O.mult))
                            nc.vector.tensor_tensor(ev, ev, b[:, 24:32].unsqueeze(2).to_broadcast([P, NH, 32]),
                                                    O.mult).then_inc(S.normed, 1)

            def stage_attention():
                S, N = stage_sems()
                cc = Carve(scratch_at, arena2)
                pr = cc(3 * 2 * L).rearrange("p (b s t) -> p b s t", b=3, s=2)
                pt = cc(2 * 2 * L).rearrange("p (b s t) -> p b s t", b=2, s=2)
                st = cc(3 * 8).rearrange("p (b n) -> p b n", b=3)
                jobs = [(n, h) for n in range(NB) for h in range(NH)]
                NJ = len(jobs)

                def half(h):
                    g = h // 4
                    return slice(HD * g, HD * g + HD)

                def region(j):
                    return PS[:, 2 * (j % 2):2 * (j % 2) + 2, :]

                with nc.Block() as block:
                    @block.sync
                    def _(sp):
                        sp.sem_clear(N.range)

                    @block.tensor
                    def _(pe):
                        def scores(j):
                            n, h = jobs[j]
                            hs = half(h)
                            if j >= 2:
                                pe.wait_ge(S.probs, j - 1)
                            for s in range(2):
                                nc.tensor.matmul(region(j)[:, s, 0:(n + 1) * P], q2[hs, h % 4, n * P:(n + 1) * P],
                                                 ksw[hs, s, 0:(n + 1) * P], start=True, stop=False)
                                last = nc.tensor.matmul(region(j)[:, s, n * P:(n + 1) * P], constb("ident"),
                                                        constb("up"), start=False, stop=True)
                            last.then_inc(S.scores, 1)

                        def flip(j):
                            n, h = jobs[j]
                            pe.wait_ge(S.normed, j + 1)
                            if j >= 1:
                                pe.wait_ge(S.copied, j)
                            for s in range(2):
                                for i in range(n + 1):
                                    last = nc.tensor.transpose(PS[:, 4 + s, i * P:(i + 1) * P],
                                                               pr[:, j % 3, s, i * P:(i + 1) * P], ident)
                            last.then_inc(S.flipped, 1)

                        def mix(j):
                            n, h = jobs[j]
                            hs = half(h)
                            g, r = h // 4, h % 4
                            pe.wait_ge(S.copied, j + 1)
                            if j >= 2:
                                pe.wait_ge(S.dve_out, j - 1)
                            o = PS[hs, 6 + j % 2, 0:P]
                            for s in range(2):
                                for i in range(n + 1):
                                    nc.tensor.matmul(o, vt2[:, i, s * P + HD * g:s * P + HD * g + HD],
                                                     pt[:, j % 2, s, i * P:(i + 1) * P], start=(s + i == 0),
                                                     stop=False)
                            rs = slice(32 * r, 32 * r + 32)
                            nc.tensor.matmul(o, vcr[rs, g, :], pcT[rs, n, g, :], start=False, stop=True)\
                                .then_inc(S.mixed, 1)

                        for s in range(NJ + 3):
                            if s < NJ:
                                scores(s)
                            if 2 <= s < NJ + 2:
                                flip(s - 2)
                            if s >= 3:
                                mix(s - 3)

                    @block.scalar
                    def _(act):
                        def exps(j):
                            n = jobs[j][0]
                            w = (n + 1) * P
                            act.wait_ge(S.shift, j + 1)
                            if j >= 3:
                                act.wait_ge(S.flipped, j - 2)
                            b = st[:, j % 3, :]
                            for s in range(2):
                                last = nc.scalar.activation(pr[:, j % 3, s, 0:w], region(j)[:, s, 0:w], A.Exp,
                                                            bias=b[:, 2 + s:3 + s], scale=ASCALE,
                                                            accum_out=b[:, 4 + s:5 + s])
                            last.then_inc(S.probs, 1)

                        def copy(j):
                            w = (jobs[j][0] + 1) * P
                            act.wait_ge(S.flipped, j + 1)
                            if j >= 2:
                                act.wait_ge(S.mixed, j - 1)
                            nc.scalar.activation(pt[:, j % 2, :, 0:w], PS[:, 4:6, 0:w], A.Copy)\
                                .then_inc(S.copied, 1)

                        for s in range(NJ + 2):
                            if s < NJ:
                                exps(s)
                            if s >= 2:
                                copy(s - 2)

                    @block.vector
                    def _(dve):
                        steps = [0]

                        def link(ins):
                            steps[0] += 1
                            ins.then_inc(S.dve_step, 1)
                            dve.wait_ge(S.dve_step, steps[0])

                        def shift(j):
                            w = (jobs[j][0] + 1) * P
                            dve.wait_ge(S.scores, j + 1)
                            if j >= 3:
                                dve.wait_ge(S.normed, j - 2)
                            b = st[:, j % 3, :]
                            link(nc.vector.tensor_reduce(b[:, 0:2], region(j)[:, :, 0:w], AX, O.max))
                            nc.vector.tensor_scalar(b[:, 2:4], b[:, 0:2], -ASCALE, None, O.mult)\
                                .then_inc(S.shift, 1)

                        def norm(j):
                            n, h = jobs[j]
                            w = (n + 1) * P
                            dve.wait_ge(S.probs, j + 1)
                            b = st[:, j % 3, :]
                            link(nc.vector.reciprocal(b[:, 6:8], b[:, 4:6]))
                            link(nc.vector.tensor_tensor(b[:, 6:8], b[:, 6:8], gates[:, n, 3 * h + 1:3 * h + 3],
                                                         O.mult))
                            for s in range(2):
                                p_ = pr[:, j % 3, s, 0:w]
                                last = nc.vector.tensor_scalar(p_, p_, b[:, 6 + s:7 + s], None, O.mult)
                            last.then_inc(S.normed, 1)

                        def out(j):
                            n, h = jobs[j]
                            hs = half(h)
                            dve.wait_ge(S.mixed, j + 1)
                            nc.vector.tensor_copy(y2[hs, h % 4, n * P:(n + 1) * P], PS[hs, 6 + j % 2, 0:P])\
                                .then_inc(S.dve_out, 1)

                        for s in range(NJ + 3):
                            if s < NJ:
                                shift(s)
                            if 1 <= s < NJ + 1:
                                norm(s - 1)
                            if s >= 3:
                                out(s - 3)

            def stage_gmlp():
                S, N = stage_sems()
                cc = Carve(scratch_at, arena2)
                st = cc(NB * 16).rearrange("p (i n) -> p i n", i=NB)
                vm = cc(NT4 * L).rearrange("p (j t) -> p j t", j=NT4)
                with nc.Block() as block:
                    @block.sync
                    def _(sp):
                        sp.sem_clear(N.range)

                    @block.scalar
                    def _(act):
                        act.wait_ge(S.ready, 1)
                        nc.scalar.activation(st[:, :, 8:9], st[:, :, 7:8], A.Sqrt, bias=const("eps")[:, 1:2])\
                            .then_inc(S.act_out, 1)

                    @block.vector
                    def _(dve):
                        steps = [0]

                        def link(ins):
                            steps[0] += 1
                            ins.then_inc(S.dve_step, 1)
                            dve.wait_ge(S.dve_step, steps[0])

                        nc.vector.tensor_tensor(wsT, wsT, const2("tri").unsqueeze(1).to_broadcast([P, NH, P]),
                                                O.mult)
                        for i in range(NB):
                            last = nc.vector.bn_stats(st[:, i, 0:6], zv[:, i, :])
                        link(last)
                        for i in range(NB):
                            last = nc.vector.bn_aggr(st[:, i, 6:8], st[:, i, 0:6])
                        last.then_inc(S.ready, 1)
                        dve.wait_ge(S.act_out, 1)
                        link(nc.vector.reciprocal(st[:, :, 9:10], st[:, :, 8:9]))
                        for i in range(NB):
                            last = nc.vector.tensor_scalar(zv[:, i, :], zv[:, i, :], st[:, i, 6:7], st[:, i, 9:10],
                                                           O.subtract, O.mult)
                        link(last)
                        link(nc.vector.tensor_tensor(zv, zv, row("ln_g").unsqueeze(1).to_broadcast([P, NB, L]),
                                                     O.mult))
                        for i in range(NB):
                            nc.vector.tensor_tensor(zv[:, i, :], zv[:, i, :], row("ln_b"), O.add)\
                                .then_inc(S.normed, 1)
                        for j in range(NT4):
                            dve.wait_ge(S.pe_tile, j + 1)
                            b = row("bs").rearrange("p (j t) -> p j t", j=NT4)[:, j, :]
                            nc.vector.tensor_tensor(vm[:, j, :].rearrange("p (c t) -> p c t", c=NB),
                                                    PS[:, j, :].rearrange("p (c t) -> p c t", c=NB),
                                                    b.unsqueeze(1).to_broadcast([P, NB, P]), O.add)\
                                .then_inc(S.dve_out, 1)
                            dve.wait_ge(S.dve_out, j + 1)
                            nc.vector.tensor_tensor(y2[:, 4 + j, :], zu[:, j, :], vm[:, j, :], O.mult)

                    @block.tensor
                    def _(pe):
                        pe.wait_ge(S.normed, NB)
                        for j in range(NT4):
                            for h in range(2):
                                g = 2 * j + h
                                for ck in range(NB):
                                    last = nc.tensor.matmul(PS[HD * h:HD * h + HD, j, ck * P:(ck + 1) * P],
                                                            zv[:, ck, g * HD:(g + 1) * HD], wsT[:, g, :],
                                                            start=True, stop=True)
                            last.then_inc(S.pe_tile, 1)

            def stage_project(name, nk, src=None, groups=None):
                S, N = stage_sems()
                norm = Normalise(S, groups) if groups else None
                u0 = U2[name]
                chunks = [range(8 * v, min(8 * v + 8, nk)) for v in range((nk + 7) // 8)]
                NU = 4 * len(chunks)
                with nc.Block() as block:
                    @block.sync
                    def _(sp):
                        sp.sem_clear(N.range)
                        stream_raw(sp, src2, u0, u0 + NU)

                    if norm:
                        @block.gpsimd
                        def _(pool):
                            norm.even(pool)

                    @block.tensor
                    def _(pe):
                        if norm:
                            norm.sums(pe)
                        for v, ks in enumerate(chunks):
                            for m in range(4):
                                u = u0 + 4 * v + m
                                pe.wait_ge(w_split, u + 1)
                                wh, wl = [x.rearrange("p (k n) -> p k n", k=8) for x in (high(u), low(u))]
                                for k in ks:
                                    if src and m == 0:
                                        pe.wait_ge(S.normed, k + 1)
                                    if norm and m == 0:
                                        norm.tile(pe, k)
                                    for h in range(2):
                                        hs = slice(h * P, (h + 1) * P)
                                        last = product3(PS[:, 2 * m + h, :], wh[:, k % 8, hs], wl[:, k % 8, hs],
                                                        ah[k % 8], al[k % 8], k == 0, k == nk - 1)
                                    if m == 3 and k < ks[-1]:
                                        last.then_inc(S.mixed, 1)
                                last.then_inc(S.pe_tile, 1)

                    @block.scalar
                    def _(act):
                        def split_chunk(v):
                            for k in chunks[v]:
                                if v:
                                    if k % 8 < 7:
                                        act.wait_ge(S.mixed, 7 * (v - 1) + k % 8 + 1)
                                    else:
                                        act.wait_ge(S.pe_tile, 4 * v)
                                nc.scalar.activation(ah[k % 8], src[k], A.Copy).then_inc(S.copied, 1)

                        if norm:
                            norm.squares(act)
                            norm.high(act)
                        if src:
                            split_chunk(0)
                        for i in range(NU):
                            split_high(act, S, u0, u0 + i + 1)
                            if src and i % 4 == 3 and i + 1 < NU:
                                split_chunk(i // 4 + 1)
                        for m in range(4):
                            act.wait_ge(S.pe_tile, NU - 3 + m)
                            nc.scalar.activation(fbuf[:, 2 * m:2 * m + 2, :], PS[:, 2 * m:2 * m + 2, :], A.Copy)

                    @block.vector
                    def _(dve):
                        def split_chunk(v):
                            for k in chunks[v]:
                                dve.wait_ge(S.copied, k + 1)
                                nc.vector.tensor_tensor(al[k % 8], src[k], ah[k % 8].bitcast(f32), O.subtract)\
                                    .then_inc(S.normed, 1)

                        if norm:
                            norm.scale(dve)
                        if src:
                            split_chunk(0)
                        for i in range(NU):
                            split_low(dve, u0 + i + 1)
                            if src and i % 4 == 3 and i + 1 < NU:
                                split_chunk(i // 4 + 1)

            def stage_up(groups):
                S, N = stage_sems()
                norm = Normalise(S, groups)
                u0 = U2["up"]
                with nc.Block() as block:
                    @block.sync
                    def _(sp):
                        sp.sem_clear(N.range)
                        stream_raw(sp, src2, u0, u0 + FT)

                    @block.gpsimd
                    def _(pool):
                        norm.even(pool)

                    @block.tensor
                    def _(pe):
                        norm.sums(pe)
                        for j in range(FT):
                            pe.wait_ge(w_split, u0 + j + 1)
                            if j >= 4:
                                pe.wait_ge(S.dve_out, j - 3)
                            wh, wl = [v.rearrange("p (k n) -> p k n", k=KT) for v in (high(u0 + j), low(u0 + j))]
                            for h in range(2):
                                hs = slice(h * P, (h + 1) * P)
                                for k in range(KT):
                                    if j + h == 0:
                                        norm.tile(pe, k)
                                    last = product3(PS[:, 2 * (j % 4) + h, :], wh[:, k, hs], wl[:, k, hs],
                                                    ah[k], al[k], k == 0, k == KT - 1)
                            last.then_inc(S.pe_tile, 1)

                    @block.scalar
                    def _(act):
                        norm.squares(act)
                        norm.high(act)
                        for j in range(FT):
                            split_high(act, S, u0, u0 + j + 1)
                            act.wait_ge(S.pe_tile, j + 1)
                            if j >= 2:
                                act.wait_ge(S.ready, j - 1)
                            for h in range(2):
                                last = nc.scalar.activation(hc[:, j % 2, h, :], PS[:, 2 * (j % 4) + h, :], A.Identity,
                                                            bias=vec2("cb", 2 * j + h),
                                                            scale=vec2("cw", 3 * (2 * j + h) + 2))
                            last.then_inc(S.act_out, 1)
                            act.wait_ge(S.dve_out, j + 1)
                            nc.scalar.activation(hc[:, j % 2, 0, :], hc[:, j % 2, 0, :], A.Silu)\
                                .then_inc(S.act_step, 1)

                    @block.vector
                    def _(dve):
                        norm.scale(dve)
                        for j in range(FT):
                            split_low(dve, u0 + j + 1)
                            dve.wait_ge(S.act_out, j + 1)
                            for s in (1, 2):
                                for h in range(2):
                                    b = hc[:, j % 2, h, s:L]
                                    last = nc.vector.scalar_tensor_tensor(
                                        b, PS[:, 2 * (j % 4) + h, 0:L - s], vec2("cw", 3 * (2 * j + h) + 2 - s), b,
                                        O.mult, O.add)
                                last.then_inc(S.dve_step if s == 1 else S.dve_out, 1)
                                if s == 1:
                                    dve.wait_ge(S.dve_step, j + 1)
                            dve.wait_ge(S.act_step, j + 1)
                            nc.vector.tensor_tensor(hid[:, j, :], hc[:, j % 2, 0, :], hc[:, j % 2, 1, :], O.mult)\
                                .then_inc(S.ready, 1)

            def stage_ple(groups):
                S, N = stage_sems()
                norm = Normalise(S, groups)
                u0 = U2["pleg"]
                with nc.Block() as block:
                    @block.sync
                    def _(sp):
                        sp.sem_clear(N.range)
                        sp.dma_start(pT, d["pT"][layer, :, :].rearrange("p (k t) -> p k t", k=2)).then_inc(S.load, 16)
                        stream_raw(sp, src2, u0, u0 + 5)
                        sp.wait_ge(S.load, 16)

                    @block.gpsimd
                    def _(pool):
                        norm.even(pool)

                    @block.tensor
                    def _(pe):
                        norm.sums(pe)
                        for m in range(4):
                            pe.wait_ge(w_split, u0 + m + 1)
                            wh, wl = [v.rearrange("p (k n) -> p k n", k=8) for v in (high(u0 + m), low(u0 + m))]
                            for h in range(2):
                                hs = slice(h * P, (h + 1) * P)
                                for k in range(KT):
                                    if m + h == 0:
                                        norm.tile(pe, k)
                                    last = product3(PS[:, 2 * m + h, :], wh[:, k, hs], wl[:, k, hs], ah[k], al[k],
                                                    k == 0, k == KT - 1)
                            last.then_inc(S.pe_tile, 1)
                        pe.wait_ge(w_arrived[(u0 + 4) % RAW], 16 * ((u0 + 4) // RAW + 1))
                        pe.wait_ge(S.load, 16)
                        w = raw(u0 + 4).rearrange("p (k n) -> p k n", k=2)
                        for j in range(KT):
                            pe.wait_ge(S.act_out, j // 2 + 1)
                            for k in range(2):
                                last = nc.tensor.matmul(PS[:, j, :], w[:, k, j * P:(j + 1) * P], pT[:, k, :],
                                                        start=(k == 0), stop=(k == 1))
                            last.then_inc(S.mixed, 1)

                    @block.scalar
                    def _(act):
                        norm.squares(act)
                        norm.high(act)
                        for m in range(4):
                            split_high(act, S, u0, u0 + m + 1)
                            act.wait_ge(S.pe_tile, m + 1)
                            nc.scalar.activation(pg[:, 2 * m:2 * m + 2, :], PS[:, 2 * m:2 * m + 2, :], A.Sigmoid)\
                                .then_inc(S.act_out, 1)

                    @block.vector
                    def _(dve):
                        norm.scale(dve)
                        for m in range(4):
                            split_low(dve, u0 + m + 1)
                        for j in range(KT):
                            dve.wait_ge(S.mixed, j + 1)
                            nc.vector.tensor_tensor(pg[:, j, :], pg[:, j, :], PS[:, j, :], O.mult)\
                                .then_inc(S.dve_out, 1)
                            dve.wait_ge(S.dve_out, j + 1)
                            nc.vector.tensor_tensor(xt[j], xt[j], pg[:, j, :], O.add)

            stage_loads()
            stage_in2([(xt, lambda k: vec2("pre_mix", k))])
            stage_compress()
            cos2, sin2 = const2("cos2"), const2("sin2")
            stage_rope([(q2[:, j, :], cos2, sin2, L) for j in range(NT4)]
                       + [(ksw[:, s, :], cos2, sin2, L) for s in range(2)]
                       + [(kcT, const2("cosc"), const2("sinc"), 64)], const("r2"), arena2[:, scratch_at:scratch_at + L])
            stage_cmp_attention()
            stage_attention()
            stage_gmlp()
            yt = [y2[:, k, :] for k in range(KT)]
            stage_project("wo", KT, groups=[(yt[0:4], lambda k: vec2("attn_g", k)),
                                            (yt[4:8], lambda k: vec2("mlp_g", k))])
            stage_residual(lambda k: vec2("post_mix", k))
            stage_up([(xt, lambda k: vec2("pre_ffn", k))])
            stage_project("down", FT, [hid[:, k, :] for k in range(FT)])
            stage_residual(lambda k: vec2("post_ffn", k))
            stage_ple([(xt, lambda k: vec2("ple_g", k))])

        S, N = stage_sems()
        with nc.Block() as block:
            @block.sync
            def _(sp):
                sp.sem_clear(N.range)
                sp.dma_start(cg, d["cg"]).then_inc(S.load, 16)
                sp.wait_ge(S.load, 16)
        before = turn[0]
        with nc.Fori(0, 2) as layer:
            layer2(layer)
            if (turn[0] - before) % 2:
                S, N = stage_sems()
                with nc.Block() as block:
                    @block.sync
                    def _(sp):
                        sp.sem_clear(N.range)
        S, N = stage_sems()
        with nc.Block() as block:
            @block.sync
            def _(sp):
                sp.dma_start(d["out"], X[:, :, 0:L]).then_inc(S.store, 16)
                sp.wait_ge(S.store, 16)


HEAD_COLUMNS = np.concatenate([np.arange(HD) + HD * h for t in range(NT4) for h in (t, t + 4)])


def ktiles(w):
    return w.reshape(-1, P, w.shape[1]).transpose(1, 0, 2)


def units_of(w):
    return w.reshape(KT, P, -1, 256).transpose(2, 1, 0, 3).reshape(-1, P, UNIT)


def vec(v):
    return v.reshape(-1, P).T


def partner(halves):
    r = np.zeros((P, P), np.float32)
    for h in range(2):
        for start, half in halves:
            for i in range(half):
                a, b = h * HD + start + i, h * HD + start + half + i
                r[b, a] = -1.0
                r[a, b] = 1.0
    return r


def constants():
    c = np.zeros((P, NCF), np.float32)
    c2 = np.zeros((P, NCG), np.float32)

    def put(name, v):
        if name in CF:
            c[:, CF[name][0]:CF[name][1]] = v
        else:
            c2[:, CG[name][0]:CG[name][1]] = v

    i = np.arange(P)
    put("ident", np.eye(P))
    put("ones", 1.0)
    put("r1", partner([(0, 16), (32, 16)]))
    put("r2", partner([(0, 8)]))
    put("tri", i[:, None] <= i[None, :])
    inv = (np.float32(500000.0) ** (-np.arange(8, dtype=np.float32) / 8)).astype(np.float32)

    def table(pos):
        ang = np.zeros((HD, len(pos)), np.float32)
        ang[0:16] = np.tile(inv, 2)[:, None] * pos.astype(np.float32)[None, :]
        return np.tile(np.cos(ang), (2, 1)), np.tile(np.sin(ang), (2, 1))

    cs, sn = table(np.arange(L))
    put("cos2", cs)
    put("sin2", sn)
    cp = np.arange(32) * 16 + 31
    cs, sn = table(np.concatenate([cp, cp]))
    put("cosc", cs)
    put("sinc", sn)
    put("fold", np.tile(np.eye(64), (2, 1)))
    put("reset", (np.arange(L) % P != 0)[None, :])
    put("one", 1.0)
    put("eps", np.array([LN_EPS, RMS_EPS])[None, :])
    f = (np.float32(10000.0) ** (-np.arange(16, dtype=np.float32) / 16)).astype(np.float32)
    t = np.arange(L)
    ang = np.concatenate([np.tile(f, 2)[:, None] * (t // 64).astype(np.float32)[None, :],
                          np.tile(f, 2)[:, None] * (t % 64).astype(np.float32)[None, :]])
    ca = np.concatenate([np.tile(np.cos(ang), (2, 1)), np.tile(np.sin(ang), (2, 1))], axis=1).astype(np.float32)
    b = np.zeros((P, NCB), np.float32)

    def putb(name, v):
        b[:, CB[name][0]:CB[name][1]] = v

    putb("ident", np.eye(P))
    putb("up", np.where(i[None, :] > i[:, None], NEG, 0))
    putb("low", np.where(i[None, :] < i[:, None], NEG, 0))
    cm = np.zeros((P, NB, 32), np.float32)
    for n in range(NB):
        ok = (cp[None, :] <= n * P + i[:, None]) & (np.arange(32)[None, :] < NCMP)
        cm[:, n] = np.where(ok, 0, NEG)
    putb("cmp", cm.reshape(P, -1))
    m = np.zeros((2, 8, P, P), np.float32)
    for lev in range(LEV):
        B = 1 << lev
        same = (i[:, None] // (2 * B)) == (i[None, :] // (2 * B))
        left, right = (i // B) % 2 == 0, (i // B) % 2 == 1
        m[0, lev] = same & left[:, None] & right[None, :]
        m[1, lev] = same & right[:, None] & left[None, :]
    m[:, 7] = np.eye(P)
    putb("scan", m.transpose(2, 0, 1, 3).reshape(P, -1))
    return c, c2, b, ca


def layout(i):
    f = {k: np.asarray(v) for k, v in i.items()}
    out = {}
    out["xT"] = np.ascontiguousarray(f["x"][0].T.reshape(KT, P, L).transpose(1, 0, 2))
    out["ctxT"] = np.ascontiguousarray(f["ctx"][0].T.reshape(KT, P, LC).transpose(1, 0, 2))
    v = np.zeros((P, NV1), np.float32)
    for name, a in [("c", f["c"][0]), ("cc", f["c_ctx"]), ("b_ada0", f["b_ada"][0]), ("b_ada1", f["b_ada"][1]),
                    ("ln_g0", f["ln_g"][0]), ("ln_b0", f["ln_b"][0]), ("ln_g1", f["ln_g"][1]),
                    ("ln_b1", f["ln_b"][1]), ("conv", f["conv_ab"][0].reshape(-1)), ("gnorm", f["gnorm_c"][0])]:
        v[:, V1[name][0]:V1[name][1]] = vec(a)
    out["v1"] = v
    out["sink"] = np.ascontiguousarray(np.broadcast_to(f["sink_ab"][0][None, :], (P, NH)))
    w = f["w_in_ab"][0]
    q, k, vv, ga, xb, bg, cg, gb = np.split(w, np.cumsum([512, 128, 128, 512, 512, 512, 512]), axis=1)
    ab_in = np.concatenate([q[:, HEAD_COLUMNS], k, vv, ga[:, HEAD_COLUMNS], xb, cg, gb, bg], axis=1)
    wo = f["w_out_ab"][0]
    ab_out = np.concatenate([wo[0:512][HEAD_COLUMNS], wo[512:]], axis=0)
    w = f["w_in_c"][0]
    parts = np.split(w, 5, axis=1)
    c_in = np.concatenate([x[:, 256 * p:256 * (p + 1)] for p in range(4) for x in parts], axis=1)
    out["w1"] = np.concatenate([units_of(x) for x in (f["w_ada"][0], ab_in, ab_out, f["w_ada"][1], c_in,
                                                      f["w_out_c"][0])])
    seg, v2, r2, wsT, wg, pT = [], [], [], [], [], []
    for l in range(2):
        g = {k[:-2]: v[l] for k, v in f.items() if k.endswith("_2")}
        w = g["w_in"]
        q, kc, vc, ks, vs, kw, vw, zg, zu, zv = np.split(
            w, np.cumsum([512, 128, 128, 128, 128, 128, 128, 24, 512]), axis=1)
        win = np.concatenate([q[:, HEAD_COLUMNS], kc[:, :64], vc[:, :64], kc[:, 64:], vc[:, 64:], ks, kw, vs, vw,
                              zu, zv], axis=1)
        c1 = g["cmp_w1"].reshape(2, 4, 8, HD, 256).transpose(1, 0, 3, 2, 4).reshape(4, P, UNIT)
        wo = np.concatenate([g["w_o"][0:512][HEAD_COLUMNS], g["w_o"][512:]], axis=0)
        up = g["w_up"].reshape(D, 2, FT, P).transpose(0, 2, 1, 3).reshape(D, -1)
        dn = np.concatenate([g["w_down"], np.zeros((24 * P - FF, D), np.float32)])
        dn = dn.reshape(3, 8, P, 4, 256).transpose(0, 3, 2, 1, 4).reshape(12, P, UNIT)
        pj = ktiles(g["w_ple_proj"]).reshape(1, P, UNIT)
        seg.append(np.concatenate([units_of(win), c1, units_of(wo), units_of(up), dn, units_of(g["w_ple_gate"]), pj]))
        a = np.zeros((P, NV2), np.float32)
        for name, x in [("pre_mix", vec(g["pre_mix_g"])), ("b1", vec(g["cmp_b1"].reshape(-1))),
                        ("pe", g["cmp_pe"].transpose(0, 2, 1).reshape(P, 32)),
                        ("b2k", np.tile(g["cmp_b2"][0], 2)[:, None]),
                        ("attn_g", vec(g["attn_out_g"][HEAD_COLUMNS])), ("mlp_g", vec(g["mlp_out_g"])),
                        ("post_mix", vec(g["post_mix_g"])), ("pre_ffn", vec(g["pre_ffn_g"])),
                        ("cw", g["conv_w"].reshape(3, 2, FT, P).transpose(3, 2, 1, 0).reshape(P, -1)),
                        ("cb", g["conv_b"].reshape(2, FT, P).transpose(2, 1, 0).reshape(P, -1)),
                        ("post_ffn", vec(g["post_ffn_g"])), ("ple_g", vec(g["ple_norm_g"]))]:
            a[:, V2[name][0]:V2[name][1]] = x
        v2.append(a)
        r = np.zeros((P, NR2), np.float32)
        for name, x in [("ln_g", g["gmlp_ln_g"][None]), ("ln_b", g["gmlp_ln_b"][None]), ("b2v", g["cmp_b2"][1][None]),
                        ("bs", np.repeat(g["gmlp_bs"].reshape(NT4, 2, P).transpose(1, 0, 2).reshape(2, -1), HD, axis=0)),
                        ("w2k", np.concatenate([ktiles(g["cmp_w2"][0])] * 2, axis=2).reshape(P, -1)),
                        ("w2v", ktiles(g["cmp_w2"][1]).reshape(P, -1))]:
            r[:, R2[name][0]:R2[name][1]] = x
        r2.append(r)
        wsT.append(g["gmlp_ws"].transpose(2, 0, 1).reshape(P, -1))
        wg.append(ktiles(zg).reshape(P, -1))
        pT.append(g["p"][0].T.reshape(2, P, L).transpose(1, 0, 2).reshape(P, -1))
    out["w2"] = np.stack(seg)
    out["v2"], out["r2"], out["wsT"], out["wgate"], out["pT"] = (np.stack(x) for x in (v2, r2, wsT, wg, pT))
    out["cf"], out["cg"], out["cb"], out["ca"] = constants()
    return {k: np.ascontiguousarray(v) for k, v in out.items()}


def kernel(**inputs):
    import numpy as _np
    import concourse.bacc as _bacc
    from concourse import mybir as _mybir
    from concourse.bass_utils import run_bass_kernel_spmd as _run

    nc = _bacc.Bacc("TRN2", target_bir_lowering=False, num_devices=1)
    arrays = layout(inputs)
    d = {n: nc.dram_tensor(n + "_dram", a.shape, _mybir.dt.from_np(a.dtype), kind="ExternalInput").ap()
         for n, a in arrays.items()}
    d["out"] = nc.dram_tensor("out_dram", (P, KT, L), _mybir.dt.float32, kind="ExternalOutput").ap()
    program(nc, d)
    r = _run(nc, [{n + "_dram": a for n, a in arrays.items()}], core_ids=[0])
    o = r.results[0]["out_dram"]
    return _np.ascontiguousarray(o.transpose(2, 1, 0).reshape(1, L, D))
```

```python
import numpy as np
from contextlib import ExitStack
import concourse.bass as bass
from concourse import mybir

P = 128
D = 1024
L = 512
LC = 256
T = L + LC
KT = D // P
HD = 64
NH = 8
NT4 = 4
NB = L // P
CH = 8
LEV = 7
FF = 2816
FT = FF // P
NCMP = 31
UNIT = 2048
HALF = UNIT // 2
RING0 = 8
RAW = 2
SLOTS = 2
ALPHA = 4 ** 0.25
LN_EPS = 1e-5
RMS_EPS = 1e-6
NEG = -1e30
ASCALE = HD ** -0.5
KSCALE = P ** -0.5

SEG_ADA = [("ada0", 12), ("ada1", 12)]
SEG_AB = [("ab_in", 13), ("ab_out", 4)]
SEG_C = [("c_in", 40), ("c_out", 8)]
SEG2 = [("in2", 9), ("cmp1", 4), ("wo", 4), ("up", FT), ("down", 12), ("pleg", 4), ("plep", 1)]


def first_units(seg):
    at, out = 0, {}
    for name, n in seg:
        out[name] = at
        at += n
    return out, at


U0, NU0 = first_units(SEG_ADA)
U1, NU1 = first_units(SEG_AB)
UC, NUC = first_units(SEG_C)
U2, NU2 = first_units(SEG2)
NSPLIT = NU2 - 1


def columns(parts):
    at, out = 0, {}
    for name, n in parts:
        out[name] = (at, at + n)
        at += n
    return out, at


V1, NV1 = columns([("c", 8), ("cc", 8), ("b_ada0", 24), ("b_ada1", 24), ("ln_g0", 8), ("ln_b0", 8), ("ln_g1", 8),
                   ("ln_b1", 8), ("conv", 12), ("gnorm", 1)])
V2, NV2 = columns([("pre_mix", 8), ("pe", 32), ("b1", 4), ("b2k", 1), ("attn_g", 4), ("mlp_g", 4), ("post_mix", 8),
                   ("pre_ffn", 8), ("cw", 3 * 2 * FT), ("cb", 2 * FT), ("post_ffn", 8), ("ple_g", 8)])
R2, NR2 = columns([("ln_g", 512), ("ln_b", 512), ("b2v", 64), ("bs", NT4 * P), ("w2k", 2 * P), ("w2v", 2 * HD)])
CF, NCF = columns([("ident", P), ("ones", P), ("r1", P), ("r2", P), ("reset", L), ("one", LC), ("eps", 2)])
CG, NCG = columns([("tri", P), ("cos2", L), ("sin2", L), ("cosc", 64), ("sinc", 64), ("fold", 64)])
CA, NCA = columns([("cos1", L), ("sin1", L)])
CB, NCB = columns([("ident", P), ("up", P), ("low", P), ("cmp", NB * 32), ("scan", 2 * 8 * P)])


class Sems:
    def __init__(self, nc, es, tag):
        def sem(name):
            return es.enter_context(nc.semaphore(f"{name}_{tag}"))

        self.load = sem("load")
        self.load2 = sem("load2")
        self.store = sem("store")
        self.act_step = sem("act_step")
        self.dve_step = sem("dve_step")
        self.pe_tile = sem("pe_tile")
        self.act_out = sem("act_out")
        self.dve_out = sem("dve_out")
        self.scores = sem("scores")
        self.shift = sem("shift")
        self.probs = sem("probs")
        self.normed = sem("normed")
        self.flipped = sem("flipped")
        self.copied = sem("copied")
        self.mixed = sem("mixed")
        self.squares = sem("squares")
        self.sums = sem("sums")
        self.ready = sem("ready")
        self.decays = sem("decays")
        self.absolute = sem("absolute")
        self.log_k = sem("log_k")
        self.exponents = sem("exponents")
        self.weights = sem("weights")
        self.state_keys = sem("state_keys")
        self.levelled = sem("levelled")
        self.own = sem("own")
        self.products = sem("products")
        self.masked = sem("masked")
        self.summed = sem("summed")
        self.chunk_out = sem("chunk_out")
        self.head_copied = sem("head_copied")
        self.head_squared = sem("head_squared")
        self.head_sum = sem("head_sum")
        self.head_root = sem("head_root")
        self.tree = sem("tree")
        self.forward_sum = sem("forward_sum")
        self.res_squares = sem("res_squares")
        self.res_sums = sem("res_sums")
        self.res_root = sem("res_root")
        self.res_step = sem("res_step")
        self.res_scaled = sem("res_scaled")
        self.res_odd = sem("res_odd")
        self.res_even = sem("res_even")
        self.res_next = sem("res_next")
        self.rms_squares = sem("rms_squares")
        self.rms_sums = sem("rms_sums")
        self.rms_root = sem("rms_root")
        self.rms_step = sem("rms_step")
        self.rms_scaled = sem("rms_scaled")
        self.rms_high = sem("rms_high")
        self.rms_odd = sem("rms_odd")
        self.rms_even = sem("rms_even")
        self.range = range(self.load.num, self.rms_even.num + 1)
        assert len(self.range) == 52


def program(nc, d):
    f32, f32r, bf16 = mybir.dt.float32, mybir.dt.float32r, mybir.dt.bfloat16
    A = mybir.ActivationFunctionType
    O = mybir.AluOpType
    AX = mybir.AxisListType.X
    es = ExitStack()
    with es:
        def sb(name, cols, dt=f32):
            return es.enter_context(nc.sbuf_tensor(name, [P, cols], dt))

        xb_ = sb("x", KT * T)
        cf = sb("cf", NCF)
        cb = sb("cb", NCB, bf16)
        v1 = sb("v1", NV1)
        mod = sb("mod", 2 * 48)
        cond = sb("cond", 32)

        psb = es.enter_context(nc.psum_tensor("ps", [P, 8 * 512], f32))

        X = xb_[:, :].rearrange("p (k t) -> p k t", k=KT)
        PS = psb[:, :].rearrange("p (b n) -> p b n", b=8)

        def const(name):
            return cf[:, CF[name][0]:CF[name][1]]

        def constb(name):
            return cb[:, CB[name][0]:CB[name][1]]

        def vec1(name, j=0):
            return v1[:, V1[name][0] + j:V1[name][0] + j + 1]

        def vec2(name, j=0):
            return v2[:, V2[name][0] + j:V2[name][0] + j + 1]

        def modv(l, part, who, j):
            c = l * 48 + (part * 8 + j) * 2 + who
            return mod[:, c:c + 1]

        ident, ones = const("ident"), const("ones")

        class Carve:
            def __init__(self, at, memory):
                self.at, self.memory = at, memory

            def __call__(self, n):
                a = self.at
                self.at += n
                assert self.at <= self.memory.shape[1], self.at
                return self.memory[:, a:a + n]

        sets = [Sems(nc, es, "a"), Sems(nc, es, "b")]
        w_arrived = [es.enter_context(nc.semaphore(f"w_arrived{i}")) for i in range(RING0)]
        w_hi = es.enter_context(nc.semaphore("w_hi"))
        w_split = es.enter_context(nc.semaphore("w_split"))
        w_range = range(w_arrived[0].num, w_split.num + 1)
        assert len(w_range) == RING0 + 2
        turn = [0]

        def stage_sems():
            turn[0] += 1
            return sets[turn[0] % 2], sets[(turn[0] + 1) % 2]

        class Ring:
            def __init__(self, memory, slots, total, first):
                self.memory, self.slots, self.total, self.first = memory, slots, total, first

            def unit(self, n):
                return self.memory[:, (n % self.slots) * UNIT:(n % self.slots + 1) * UNIT]

            def start(self, sp):
                sp.sem_clear(w_range)
                for n in range(self.slots):
                    sp.dma_start(self.unit(n), d["w1"][self.first + n]).then_inc(w_arrived[n], 16)

            def issue(self, sp, a, b, tile_done, per_unit=1):
                for n in range(a + self.slots, min(b + self.slots, self.total)):
                    sp.wait_ge(tile_done, (n - self.slots - a + 1) * per_unit)
                    sp.dma_start(self.unit(n), d["w1"][self.first + n]).then_inc(w_arrived[n % self.slots], 16)

            def arrived(self, pe, n):
                pe.wait_ge(w_arrived[n % self.slots], 16 * (n // self.slots + 1))

        class SplitStream:
            def __init__(self, total, nsplit, raw_ring, w_high, w_low, size=UNIT):
                self.total, self.nsplit, self.size = total, nsplit, size
                self.raw_ring, self.w_high, self.w_low = raw_ring, w_high, w_low

            def raw(self, n):
                return self.raw_ring[:, (n % RAW) * self.size:(n % RAW + 1) * self.size]

            def high(self, n):
                return self.w_high[:, (n % SLOTS) * self.size:(n % SLOTS + 1) * self.size]

            def low(self, n):
                return self.w_low[:, (n % SLOTS) * self.size:(n % SLOTS + 1) * self.size]

            def start(self, sp, src):
                sp.sem_clear(w_range)
                for n in range(RAW):
                    sp.dma_start(self.raw(n), src(n)).then_inc(w_arrived[n], 16)

            def load(self, sp, src, a, b):
                for n in range(a + RAW + 1, min(b + RAW + 1, self.total)):
                    sp.wait_ge(w_split, n - RAW + 1)
                    sp.dma_start(self.raw(n), src(n)).then_inc(w_arrived[n % RAW], 16)

            def split_high(self, act, S, a, n, per_unit=1, done=None):
                if n >= self.nsplit:
                    return
                act.wait_ge(w_arrived[n % RAW], 16 * (n // RAW + 1))
                if n - SLOTS >= a:
                    act.wait_ge(S.pe_tile, done[n - SLOTS - a] if done else (n - SLOTS - a + 1) * per_unit)
                nc.scalar.activation(self.high(n), self.raw(n), A.Copy).then_inc(w_hi, 1)

            def split_low(self, eng, n, by_pool=False):
                if n >= self.nsplit:
                    return
                eng.wait_ge(w_hi, n + 1)
                (nc.gpsimd if by_pool else nc.vector).tensor_tensor(self.low(n), self.raw(n), self.high(n).bitcast(f32), O.subtract)\
                    .then_inc(w_split, 1)

        def product3(out, wh, wl, xh, xl, start, stop):
            nc.tensor.matmul(out, wh, xh, start=start, stop=False)
            nc.tensor.matmul(out, wh, xl, start=False, stop=False)
            return nc.tensor.matmul(out, wl, xh, start=False, stop=stop)

        class SplitTiles:
            def __init__(self, S, src, high, low):
                self.S, self.src, self.high, self.low = S, src, high, low

            def split_high(self, act, k):
                nc.scalar.activation(self.high[k], self.src[k], A.Copy).then_inc(self.S.rms_high, 1)

            def split_low(self, eng, which, k):
                if k >= 0 and k % 2 == which:
                    eng.wait_ge(self.S.rms_high, k + 1)
                    (nc.vector if which else nc.gpsimd).tensor_tensor(
                        self.low[k], self.src[k], self.high[k].bitcast(f32), O.subtract)\
                        .then_inc(self.S.rms_odd if which else self.S.rms_even, 1)

            def on_act(self, act):
                for k in range(KT):
                    self.split_high(act, k)

            def on_dve(self, dve):
                for k in range(KT):
                    self.split_low(dve, 1, k)

            def on_pool(self, pool):
                for k in range(KT):
                    self.split_low(pool, 0, k)

            def tile(self, pe, k):
                if k % 2:
                    pe.wait_ge(self.S.rms_odd, k // 2 + 1)
                else:
                    pe.wait_ge(self.S.rms_even, k // 2 + 1)

        ada = ExitStack()
        ada_ring = Ring(ada.enter_context(nc.sbuf_tensor("ada_ring", [P, RING0 * UNIT], f32)), RING0, NU0, 0)
        arena0 = ada.enter_context(nc.sbuf_tensor("arena0", [P, 24 * P], f32))
        raw_cb = ada.enter_context(nc.sbuf_tensor("raw_cb", [P, NCB], f32))

        silu_c = cond[:, 16:32].rearrange("p (w k) -> p k w", w=2)

        def stage_load():
            S, N = stage_sems()
            with nc.Block() as block:
                @block.sync
                def _(sp):
                    sp.sem_clear(N.range)
                    sp.dma_start(v1[:, :], d["v1"]).then_inc(S.load, 16)
                    sp.dma_start(cf[:, :], d["cf"]).then_inc(S.load, 16)
                    ada_ring.start(sp)
                    sp.wait_ge(S.load, 32)

                @block.scalar
                def _(act):
                    act.wait_ge(S.load, 32)
                    nc.scalar.activation(cond[:, 16:32], v1[:, 0:16], A.Silu).then_inc(S.act_out, 1)

        def stage_mod(l, u0):
            S, N = stage_sems()
            rowsT = arena0[0:2, 0:24 * P]
            with nc.Block() as block:
                @block.sync
                def _(sp):
                    sp.sem_clear(N.range)
                    ada_ring.issue(sp, u0, u0 + 12, S.pe_tile)
                    if l == 1:
                        sp.dma_start(X[:, :, 0:L], d["xT"]).then_inc(S.load, 16)
                        sp.dma_start(X[:, :, L:T], d["ctxT"]).then_inc(S.load, 16)
                        sp.dma_start(raw_cb[:, :], d["cb"]).then_inc(S.load2, 16)
                        sp.wait_ge(S.load, 32)

                @block.tensor
                def _(pe):
                    def flip(b):
                        pe.wait_ge(S.act_out, b + 1)
                        for j in range(4 * b, 4 * b + 4):
                            last = nc.tensor.transpose(PS[:, 6, 2 * j:2 * j + 2], rowsT[:, j * P:(j + 1) * P],
                                                       ident[0:2, 0:2])
                        last.then_inc(S.flipped, 1)

                    for u in range(12):
                        ada_ring.arrived(pe, u0 + u)
                        w = ada_ring.unit(u0 + u).rearrange("p (k n) -> p k n", k=KT)
                        for k in range(KT):
                            last = nc.tensor.matmul(PS[0:2, u // 2, (u % 2) * 256:(u % 2 + 1) * 256],
                                                    silu_c[:, k, :], w[:, k, :], start=(k == 0), stop=(k == KT - 1))
                        last.then_inc(S.pe_tile, 1)
                        if u % 2 and u > 1:
                            flip(u // 2 - 1)
                    flip(5)

                @block.scalar
                def _(act):
                    for b in range(6):
                        act.wait_ge(S.pe_tile, 2 * b + 2)
                        nc.scalar.activation(rowsT[:, b * 512:(b + 1) * 512], PS[0:2, b, :], A.Copy)\
                            .then_inc(S.act_out, 1)

                @block.vector
                def _(dve):
                    b = v1[:, V1[f"b_ada{l}"][0]:V1[f"b_ada{l}"][1]]
                    m = mod[:, l * 48:(l + 1) * 48]
                    dve.wait_ge(S.flipped, 6)
                    nc.vector.tensor_tensor(m.rearrange("p (j w) -> p j w", w=2),
                                            PS[:, 6, 0:48].rearrange("p (j w) -> p j w", w=2),
                                            b.unsqueeze(2).to_broadcast([P, 24, 2]), O.add).then_inc(S.dve_step, 1)
                    dve.wait_ge(S.dve_step, 1)
                    nc.vector.tensor_scalar(m[:, 16:32], m[:, 16:32], 1.0, None, O.add)
                    if l == 1:
                        dve.wait_ge(S.load2, 16)
                        nc.vector.tensor_copy(cb[:, :], raw_cb[:, :]).then_inc(S.dve_out, 1)

        stage_load()
        stage_mod(0, U0["ada0"])
        stage_mod(1, U0["ada1"])
        ada.close()

        def stage_modulate(l, dst, start, high=None, low=None):
            S, N = stage_sems()
            tiles_in = SplitTiles(S, [dst[:, k, :] for k in range(KT)], high, low) if high else None
            with nc.Block() as block:
                @block.sync
                def _(sp):
                    sp.sem_clear(N.range)
                    start(sp)

                @block.vector
                def _(dve):
                    for k in range(KT):
                        for who, (a, b) in enumerate(((0, L), (L, T))):
                            nc.vector.tensor_scalar(dst[:, k, a:b], X[:, k, a:b], modv(l, 1, who, k),
                                                    modv(l, 0, who, k), O.mult, O.add).then_inc(S.dve_out, 1)
                    if tiles_in:
                        tiles_in.on_dve(dve)

                @block.scalar
                def _(act):
                    for k in range(KT):
                        act.wait_ge(S.dve_out, 2 * k + 2)
                        if tiles_in:
                            tiles_in.split_high(act, k)
                        nc.scalar.mul(X[:, k, :], X[:, k, :], ALPHA)

                if tiles_in:
                    @block.gpsimd
                    def _(pool):
                        tiles_in.on_pool(pool)

        ab = ExitStack()

        def absb(name, cols, dt=f32):
            return ab.enter_context(nc.sbuf_tensor(name, [P, cols], dt))

        ab_stream = SplitStream(NU1, NU1, absb("ab_raw", RAW * UNIT), absb("ab_high", SLOTS * UNIT, f32r),
                                absb("ab_low", SLOTS * UNIT, f32r))
        x_high, x_low = absb("x_high", KT * T, f32r), absb("x_low", KT * T, f32r)
        xh = [x_high[:, k * T:(k + 1) * T] for k in range(KT)]
        xl = [x_low[:, k * T:(k + 1) * T] for k in range(KT)]
        arena1 = absb("arena1", 19300)
        c = Carve(0, arena1)
        qT = c(NT4 * T).rearrange("p (j t) -> p j t", j=NT4)
        kT = c(T)
        vtok = c(6 * P).rearrange("p (i n) -> p i n", i=6)
        yin = c(KT * T).rearrange("p (j t) -> p j t", j=KT)
        ca = c(NCA)
        esink = c(16)
        nsink = esink[:, 0:8]
        ab_mark = c.at
        UP = T + 4
        upad = c(NT4 * UP).rearrange("p (j t) -> p j t", j=NT4)
        yc = c(NT4 * UP).rearrange("p (j t) -> p j t", j=NT4)
        xbt = yc[:, :, 0:T]

        def src_ab(n):
            return d["w1"][NU0 + n]


        def stage_ab_in():
            S, N = stage_sems()
            tiles_in = SplitTiles(S, [yin[:, k, :] for k in range(KT)], xh, xl)
            u0 = U1["ab_in"]
            tiles = ([("q", j) for j in range(4)] + [("k", 0), ("v", 0)] + [("ga", j) for j in range(4)]
                     + [("xb", j) for j in range(4)] + [("cg", j) for j in range(4)]
                     + [("gb", j) for j in range(4)] + [("bg", j) for j in range(4)])
            index = {t: i for i, t in enumerate(tiles)}
            by_dve = ("cg", "bg")

            def count(t):
                mine = t[0] in by_dve
                return sum((x[0] in by_dve) == mine for x in tiles[:index[t] + 1])

            def wide(i):
                return PS[:, 2 * (i % 4):2 * (i % 4) + 2, :].rearrange("p b n -> p (b n)")

            with nc.Block() as block:
                @block.sync
                def _(sp):
                    sp.sem_clear(N.range)
                    sp.dma_start(ca, d["ca"]).then_inc(S.load, 16)
                    sp.dma_start(nsink, d["sink"]).then_inc(S.load, 16)
                    ab_stream.load(sp, src_ab, u0 - 1, u0 + 13)
                    sp.wait_ge(S.load, 32)

                @block.gpsimd
                def _(pool):
                    tiles_in.on_pool(pool)

                @block.tensor
                def _(pe):
                    for i, t in enumerate(tiles):
                        if i % 2 == 0:
                            pe.wait_ge(w_split, u0 + i // 2 + 1)
                        if i >= 4:
                            old = tiles[i - 4]
                            pe.wait_ge(S.dve_out if old[0] in by_dve else S.act_out, count(old))
                        wh, wl = [w.rearrange("p (k n) -> p k n", k=KT)[:, :, (i % 2) * P:(i % 2 + 1) * P]
                                  for w in (ab_stream.high(u0 + i // 2), ab_stream.low(u0 + i // 2))]
                        ps = wide(i)
                        if t[0] == "v":
                            for m in range(6):
                                ts = slice(m * P, (m + 1) * P)
                                for k in range(KT):
                                    last = product3(ps[:, ts], xh[k][:, ts], xl[k][:, ts], wh[:, k, :], wl[:, k, :],
                                                    k == 0, k == KT - 1)
                        else:
                            for a, b in ((0, L), (L, T)):
                                for k in range(KT):
                                    if i + a == 0:
                                        tiles_in.tile(pe, k)
                                    last = product3(ps[:, a:b], wh[:, k, :], wl[:, k, :], xh[k][:, a:b],
                                                    xl[k][:, a:b], k == 0, k == KT - 1)
                        last.then_inc(S.pe_tile, 1)

                @block.scalar
                def _(act):
                    ab_stream.split_high(act, S, u0, u0, 2)
                    tiles_in.on_act(act)
                    for i, (kind, j) in enumerate(tiles):
                        if i % 2 == 0:
                            ab_stream.split_high(act, S, u0, u0 + i // 2 + 1, 2)
                        if kind in by_dve:
                            continue
                        act.wait_ge(S.pe_tile, i + 1)
                        dst = {"q": qT[:, j, :], "k": kT, "v": vtok.rearrange("p i n -> p (i n)"),
                               "ga": yin[:, j, :], "xb": xbt[:, j, :], "gb": yin[:, 4 + j, :]}[kind]
                        nc.scalar.activation(dst, wide(i)[:, 0:T], A.Silu if kind in ("ga", "gb") else A.Copy)\
                            .then_inc(S.act_out, 1)

                @block.vector
                def _(dve):
                    steps = [0]

                    def link(ins):
                        steps[0] += 1
                        ins.then_inc(S.dve_step, 1)
                        dve.wait_ge(S.dve_step, steps[0])

                    def gate(j):
                        i = index[("cg", j)]
                        dve.wait_ge(S.pe_tile, i + 1)
                        dve.wait_ge(S.act_out, count(("xb", j)))
                        nc.vector.tensor_tensor(upad[:, j, 1:1 + L], wide(i)[:, 0:L], xbt[:, j, 0:L], O.mult)
                        nc.vector.tensor_tensor(upad[:, j, L + 3:T + 3], wide(i)[:, L:T], xbt[:, j, L:T], O.mult)\
                            .then_inc(S.dve_out, 1)
                        dve.wait_ge(S.dve_out, j + 1)
                        y, u = yc[:, j, 1:T + 3], upad[:, j, :]
                        link(nc.vector.tensor_scalar(y, u[:, 1:T + 3], vec1("conv", 4 + j), None, O.mult))
                        link(nc.vector.scalar_tensor_tensor(y, u[:, 0:T + 2], vec1("conv", j), y, O.mult, O.add))
                        link(nc.vector.scalar_tensor_tensor(y, u[:, 2:T + 4], vec1("conv", 8 + j), y, O.mult, O.add))

                    def conv_out(j):
                        i = index[("bg", j)]
                        dve.wait_ge(S.pe_tile, i + 1)
                        dve.wait_ge(S.act_out, count(("gb", j)))
                        o = yin[:, 4 + j, :]
                        nc.vector.tensor_tensor(o, o, wide(i)[:, 0:T], O.mult).then_inc(S.dve_out, 1)
                        dve.wait_ge(S.dve_out, 4 + j + 1)
                        nc.vector.tensor_tensor(o[:, 0:L], o[:, 0:L], yc[:, j, 1:1 + L], O.mult)
                        nc.vector.tensor_tensor(o[:, L:T], o[:, L:T], yc[:, j, L + 3:T + 3], O.mult)

                    ab_stream.split_low(dve, u0)
                    tiles_in.on_dve(dve)
                    link(nc.vector.memset(upad, 0.0))
                    for i, (kind, j) in enumerate(tiles):
                        if i % 2 == 0:
                            ab_stream.split_low(dve, u0 + i // 2 + 1)
                        if kind == "cg":
                            gate(j)
                        elif kind == "bg":
                            conv_out(j)

        def stage_rope(items, rot, tmp):
            S, N = stage_sems()
            with nc.Block() as block:
                @block.sync
                def _(sp):
                    sp.sem_clear(N.range)

                @block.tensor
                def _(pe):
                    for i, (x, _c, _s, n) in enumerate(items):
                        nc.tensor.matmul(PS[:, i, 0:n], rot, x, start=True, stop=True).then_inc(S.pe_tile, 1)

                @block.vector
                def _(dve):
                    for i, (x, cos, sin, n) in enumerate(items):
                        dve.wait_ge(S.pe_tile, i + 1)
                        nc.vector.tensor_tensor(tmp[:, 0:n], PS[:, i, 0:n], sin, O.mult)
                        nc.vector.tensor_tensor(x, x, cos, O.mult).then_inc(S.dve_step, 1)
                        dve.wait_ge(S.dve_step, 2 * i + 1)
                        nc.vector.tensor_tensor(x, x, tmp[:, 0:n], O.add).then_inc(S.dve_step, 1)
                        dve.wait_ge(S.dve_step, 2 * i + 2)

        def stage_ab_attention():
            S, N = stage_sems()
            cc = Carve(ab_mark, arena1)
            pr = cc(3 * 640).rearrange("p (b n) -> p b n", b=3)
            pt = cc(2 * 640).rearrange("p (b n) -> p b n", b=2)
            st = cc(3 * 8).rearrange("p (b n) -> p b n", b=3)
            jobs = []
            for n in range(NB):
                lo, hi = max(0, n - 1), min(NB - 1, n + 1)
                for h in range(NH):
                    jobs.append((n * P, list(range(lo, hi + 1)), n, h))
            for n in range(LC // P):
                for h in range(NH):
                    jobs.append((L + n * P, [], None, h))
            NJ = len(jobs)

            def region(j):
                return PS[:, 2 * (j % 2):2 * (j % 2) + 2, :].rearrange("p b n -> p (b n)")

            flips = PS[:, 4:6, :].rearrange("p b n -> p (b n)")

            def half(h):
                g = h // 4
                return slice(HD * g, HD * g + HD)

            with nc.Block() as block:
                @block.sync
                def _(sp):
                    sp.sem_clear(N.range)

                @block.tensor
                def _(pe):
                    def scores(j):
                        q0, loc, n, h = jobs[j]
                        nl = len(loc)
                        hs = half(h)
                        q = qT[hs, h % 4, q0:q0 + P]
                        if j >= 2:
                            pe.wait_ge(S.probs, j - 1)
                        r = region(j)
                        if nl:
                            nc.tensor.matmul(r[:, L - P * nl:L], q, kT[hs, loc[0] * P:(loc[-1] + 1) * P],
                                             start=True, stop=False)
                            edges = [m for m in loc if m != n]
                            for m in edges:
                                a = L - P * nl + (m - loc[0]) * P
                                nc.tensor.matmul(r[:, a:a + P], constb("ident"), constb("low" if m < n else "up"),
                                                 start=False, stop=(m == edges[-1]))
                        nc.tensor.matmul(r[:, L:L + LC], q, kT[hs, L:T], start=True, stop=True)\
                            .then_inc(S.scores, 1)

                    def flip(j):
                        pe.wait_ge(S.normed, j + 1)
                        if j >= 1:
                            pe.wait_ge(S.copied, j)
                        for i in range(len(jobs[j][1]) + 2):
                            last = nc.tensor.transpose(flips[:, i * P:(i + 1) * P],
                                                       pr[:, j % 3, i * P:(i + 1) * P], ident)
                        last.then_inc(S.flipped, 1)

                    def mix(j):
                        q0, loc, n, h = jobs[j]
                        hs = half(h)
                        pe.wait_ge(S.copied, j + 1)
                        if j >= 2:
                            pe.wait_ge(S.dve_out, j - 1)
                        keys = loc + [4, 5]
                        for i, m in enumerate(keys):
                            last = nc.tensor.matmul(PS[hs, 6 + j % 2, 0:P], vtok[:, m, hs],
                                                    pt[:, j % 2, i * P:(i + 1) * P], start=(i == 0),
                                                    stop=(i == len(keys) - 1))
                        last.then_inc(S.mixed, 1)

                    for s in range(NJ + 3):
                        if s < NJ:
                            scores(s)
                        if 2 <= s < NJ + 2:
                            flip(s - 2)
                        if s >= 3:
                            mix(s - 3)

                @block.scalar
                def _(act):
                    def exps(j):
                        nl = len(jobs[j][1])
                        act.wait_ge(S.shift, j + 1)
                        if j >= 3:
                            act.wait_ge(S.flipped, j - 2)
                        b = st[:, j % 3, :]
                        nc.scalar.activation(b[:, 3:4], b[:, 6:7], A.Exp)
                        nc.scalar.activation(pr[:, j % 3, 0:P * (nl + 2)], region(j)[:, L - P * nl:L + LC], A.Exp,
                                             bias=b[:, 1:2], scale=ASCALE, accum_out=b[:, 2:3]).then_inc(S.probs, 1)

                    def copy(j):
                        nk = len(jobs[j][1]) + 2
                        act.wait_ge(S.flipped, j + 1)
                        if j >= 2:
                            act.wait_ge(S.mixed, j - 1)
                        nc.scalar.activation(pt[:, j % 2, 0:nk * P], flips[:, 0:nk * P], A.Copy)\
                            .then_inc(S.copied, 1)

                    for s in range(NJ + 2):
                        if s < NJ:
                            exps(s)
                        if s >= 2:
                            copy(s - 2)

                @block.vector
                def _(dve):
                    steps = [0]

                    def link(ins):
                        steps[0] += 1
                        ins.then_inc(S.dve_step, 1)
                        dve.wait_ge(S.dve_step, steps[0])

                    def shift(j):
                        h, nl = jobs[j][3], len(jobs[j][1])
                        dve.wait_ge(S.scores, j + 1)
                        if j >= 3:
                            dve.wait_ge(S.normed, j - 2)
                        b = st[:, j % 3, :]
                        link(nc.vector.tensor_reduce(b[:, 0:1], region(j)[:, L - P * nl:L + LC], AX, O.max))
                        link(nc.vector.tensor_scalar(b[:, 1:2], b[:, 0:1], -ASCALE, esink[:, 8 + h:9 + h],
                                                     O.mult, O.min))
                        nc.vector.tensor_tensor(b[:, 6:7], b[:, 1:2], nsink[:, h:h + 1], O.add).then_inc(S.shift, 1)

                    def norm(j):
                        nk = len(jobs[j][1]) + 2
                        dve.wait_ge(S.probs, j + 1)
                        b = st[:, j % 3, :]
                        link(nc.vector.tensor_tensor(b[:, 4:5], b[:, 2:3], b[:, 3:4], O.add))
                        link(nc.vector.reciprocal(b[:, 5:6], b[:, 4:5]))
                        p_ = pr[:, j % 3, 0:nk * P]
                        nc.vector.tensor_scalar(p_, p_, b[:, 5:6], None, O.mult).then_inc(S.normed, 1)

                    def out(j):
                        q0, loc, n, h = jobs[j]
                        hs = half(h)
                        dve.wait_ge(S.mixed, j + 1)
                        y = yin[hs, h % 4, q0:q0 + P]
                        nc.vector.tensor_tensor(y, y, PS[hs, 6 + j % 2, 0:P], O.mult)\
                            .then_inc(S.dve_out, 1)

                    link(nc.vector.tensor_scalar(esink[:, 8:16], nsink, -1.0, None, O.mult))
                    for s in range(NJ + 3):
                        if s < NJ:
                            shift(s)
                        if 1 <= s < NJ + 1:
                            norm(s - 1)
                        if s >= 3:
                            out(s - 3)

        def stage_out1(l, u0, y, W, stream, src, per, xh, xl):
            S, N = stage_sems()
            tiles_in = SplitTiles(S, [y[:, k, 0:W] for k in range(KT)], xh, xl)
            units, ahead = KT // per, 2 // per

            def wide(i):
                return PS[:, 2 * (i % 4):2 * (i % 4) + 2, :].rearrange("p b n -> p (b n)")

            parts = [(0, L)] + ([(L, T)] if W > L else [])
            with nc.Block() as block:
                @block.sync
                def _(sp):
                    sp.sem_clear(N.range)
                    stream.load(sp, src, u0 + ahead - 1, u0 + units + ahead - 1)

                @block.gpsimd
                def _(pool):
                    tiles_in.on_pool(pool)

                @block.scalar
                def _(act):
                    tiles_in.on_act(act)
                    for u in range(units):
                        stream.split_high(act, S, u0, u0 + u + ahead, per)

                @block.tensor
                def _(pe):
                    for i in range(KT):
                        if i >= 4:
                            pe.wait_ge(S.dve_out, i - 3)
                        u, cols = u0 + i // per, slice((i % per) * P, (i % per + 1) * P)
                        pe.wait_ge(w_split, u + 1)
                        wh, wl = [w.rearrange("p (k n) -> p k n", k=KT)[:, :, cols]
                                  for w in (stream.high(u), stream.low(u))]
                        for a, b in parts:
                            for k in range(KT):
                                if i + a == 0:
                                    tiles_in.tile(pe, k)
                                last = product3(wide(i)[:, a:b], wh[:, k, :], wl[:, k, :], xh[k][:, a:b],
                                                xl[k][:, a:b], k == 0, k == KT - 1)
                        last.then_inc(S.pe_tile, 1)

                @block.vector
                def _(dve):
                    tiles_in.on_dve(dve)
                    for i in range(KT):
                        if i % per == 0:
                            stream.split_low(dve, u0 + i // per + ahead)
                        dve.wait_ge(S.pe_tile, i + 1)
                        for who, (a, b) in enumerate(parts):
                            last = nc.vector.scalar_tensor_tensor(X[:, i, a:b], wide(i)[:, a:b], modv(l, 2, who, i),
                                                                  X[:, i, a:b], O.mult, O.add)
                        last.then_inc(S.dve_out, 1)

        def stage_layer_norm(l, W, sq, tmp):
            S, N = stage_sems()
            parts = [(0, L)] + ([(L, T)] if W > L else [])
            mean = PS[:, 0:2, :].rearrange("p b n -> p (b n)")
            var = PS[:, 2:4, :].rearrange("p b n -> p (b n)")
            with nc.Block() as block:
                @block.sync
                def _(sp):
                    sp.sem_clear(N.range)

                @block.tensor
                def _(pe):
                    for a, b in parts:
                        for k in range(KT):
                            last = nc.tensor.matmul(mean[:, a:b], ones, X[:, k, a:b], start=(k == 0),
                                                    stop=(k == KT - 1))
                    last.then_inc(S.sums, 1)
                    for k in range(KT):
                        pe.wait_ge(S.squares, k + 1)
                        for a, b in parts:
                            last = nc.tensor.matmul(var[:, a:b], ones, sq[:, k, a:b], start=(k == 0),
                                                    stop=(k == KT - 1))
                    last.then_inc(S.sums, 1)

                @block.scalar
                def _(act):
                    for k in range(KT):
                        act.wait_ge(S.dve_out, k + 1)
                        nc.scalar.activation(sq[:, k, 0:W], X[:, k, 0:W], A.Square).then_inc(S.squares, 1)
                    act.wait_ge(S.sums, 2)
                    nc.scalar.activation(tmp[:, 0:W], var[:, 0:W], A.Sqrt, bias=const("eps")[:, 0:1], scale=1.0 / D)\
                        .then_inc(S.act_out, 1)
                    for k in range(KT):
                        act.wait_ge(S.normed, k + 1)
                        nc.scalar.activation(X[:, k, 0:W], X[:, k, 0:W], A.Identity, bias=vec1(f"ln_b{l}", k),
                                             scale=vec1(f"ln_g{l}", k))

                @block.vector
                def _(dve):
                    dve.wait_ge(S.sums, 1)
                    for k in range(KT):
                        nc.vector.scalar_tensor_tensor(X[:, k, 0:W], mean[:, 0:W], -1.0 / D, X[:, k, 0:W],
                                                       O.mult, O.add).then_inc(S.dve_out, 1)
                    dve.wait_ge(S.act_out, 1)
                    dve.wait_ge(S.dve_out, KT)
                    nc.vector.reciprocal(tmp[:, 0:W], tmp[:, 0:W]).then_inc(S.dve_step, 1)
                    dve.wait_ge(S.dve_step, 1)
                    dve.wait_ge(S.squares, KT)
                    for k in range(KT):
                        nc.vector.tensor_tensor(X[:, k, 0:W], X[:, k, 0:W], tmp[:, 0:W], O.mult)\
                            .then_inc(S.normed, 1)

        stage_modulate(0, yin, lambda sp: ab_stream.start(sp, src_ab))
        stage_ab_in()
        cos1, sin1 = ca[:, CA["cos1"][0]:CA["cos1"][1]], ca[:, CA["sin1"][0]:CA["sin1"][1]]
        stage_rope([(qT[:, j, 0:L], cos1, sin1, L) for j in range(NT4)] + [(kT[:, 0:L], cos1, sin1, L)],
                   const("r1"), xbt[:, 0, 0:L])
        stage_ab_attention()
        stage_out1(0, U1["ab_out"], yin, T, ab_stream, src_ab, 2, xh, xl)
        c = Carve(0, arena1)
        sq1, tmp1 = c(KT * T).rearrange("p (k t) -> p k t", k=KT), c(T + 1)
        stage_layer_norm(0, T, sq1, tmp1)
        ab.close()

        hgrn = ExitStack()

        def csb(name, cols, dt=f32):
            return hgrn.enter_context(nc.sbuf_tensor(name, [P, cols], dt))

        c_stream = SplitStream(NUC, NUC, csb("c_raw", RAW * HALF), csb("c_w_high", SLOTS * HALF, f32r),
                               csb("c_w_low", SLOTS * HALF, f32r), HALF)
        c_high, c_low = csb("c_high", KT * T, f32r), csb("c_low", KT * T, f32r)
        ch = [c_high[:, k * T:(k + 1) * T] for k in range(KT)]
        cl = [c_low[:, k * T:(k + 1) * T] for k in range(KT)]
        arena3 = csb("arena3", 25600)

        def src_c(n):
            return d["wc"][n]

        modulated = arena3[:, 0:KT * T].rearrange("p (k t) -> p k t", k=KT)
        c = Carve(0, arena3)
        yh = c(CH * L).rearrange("p (j t) -> p j t", j=CH)
        hq = [c(2 * L).rearrange("p (j t) -> p j t", j=2) for _ in range(2)]
        hz = c(4 * T).rearrange("p (d j t) -> p d j t", d=2, j=2)
        hi = [c(6 * 256).rearrange("p (i n) -> p i n", i=6), X[:, 0:6, L:T]]
        buf_t1 = [c(T), c(T)]
        buf_k = [c(T), c(T)]
        buf_b = [c(T), c(T)]
        b_at = c.at - 2 * T
        buf_eb = [c(L), c(L)]
        buf_x = [c(LEV * L), c(LEV * L)]
        prod = c(1024)
        prods = [prod, arena3[:, b_at:b_at + 1024]]
        buf_kt = prod[:, 0:5 * P]
        buf_s = [[X[:, 6 + i // 2, L + (i % 2) * P:L + (i % 2 + 1) * P] for i in range(NB)],
                 [c(P) for _ in range(NB)]]
        am = [c(P), c(P)]

        C_TILES = [("q", 0, [0]), ("q", 1, [1]), ("i", 0, [2, 3]), ("i", 1, [2, 3]), ("z", 0, [4]), ("z", 2, [5]),
                   ("g", 0, [6]), ("g", 1, [7]), ("z", 1, [8]), ("z", 3, [9])]
        UNIT_DONE = [1, 2, 4, 4, 5, 6, 7, 8, 9, 10]
        SPLIT_AFTER = [[2], [3], [], [4, 5], [6], [7], [8], [9], [10], [11]]

        def stage_c(step):
            S, N = stage_sems()
            u0 = UC["c_in"] + 10 * step
            projects, scans = step < CH // 2, step > 0
            qn, zn, iv = hq[step % 2], hz, hi[step % 2]
            q_, z_, i_ = hq[(step + 1) % 2], hz, hi[(step + 1) % 2]
            pair = step - 1

            def rev(ap):
                return ap[:, ::-1]

            def levels(v, lev):
                w = v.rearrange("p (n s b) -> p n s b", s=2, b=1 << lev)
                return w[:, :, 0, :], w[:, :, 1, :]

            def bank2(b):
                return PS[:, b:b + 2, :].rearrange("p b n -> p (b n)")

            def order(dr):
                return list(range(NB)) if dr == 0 else list(range(NB))[::-1]

            def exponents(eng, dr):
                b = buf_b[dr]
                for lev in range(LEV):
                    B = 1 << lev
                    left, right = levels(b[:, 0:L], lev)
                    xl, xr = levels(buf_x[dr][:, lev * L:(lev + 1) * L], lev)
                    n = L // (2 * B)
                    if dr == 0:
                        ref = left[:, :, B - 1:B].to_broadcast([P, n, B])
                        eng.tensor_tensor(xr, right, ref, O.subtract)
                        last = eng.tensor_tensor(xl, ref, left, O.subtract)
                    else:
                        ref = right[:, :, 0:1].to_broadcast([P, n, B])
                        eng.tensor_tensor(xl, left, ref, O.subtract)
                        last = eng.tensor_tensor(xr, ref, right, O.subtract)
                return last

            with nc.Block() as block:
                @block.sync
                def _(sp):
                    sp.sem_clear(N.range)
                    if projects:
                        c_stream.load(sp, src_c, u0 + 1 if step else u0 - 1, u0 + 11)

                @block.gpsimd
                def _(pool):
                    def low(units):
                        for n in units:
                            if projects and step:
                                c_stream.split_low(pool, u0 + n, by_pool=True)

                    for j in range(2):
                        low([[2, 3], [7]][j])
                        if scans:
                            pool.wait_ge(S.decays, j + 1)
                            exponents(nc.gpsimd, 1).then_inc(S.ready, 1)
                        low([[4, 5, 6], [8, 9, 10, 11]][j])
                        for i in range(NB * j, NB * (j + 1) if scans else 0):
                            pool.wait_ge(S.masked, 2 * i + 1)
                            p0 = prods[0]
                            for n, half in enumerate((4 * P, 2 * P)):
                                nc.gpsimd.tensor_tensor(p0[:, 0:half], p0[:, 0:half], p0[:, half:2 * half], O.add)\
                                    .then_inc(S.tree, 1)
                                pool.wait_ge(S.tree, 2 * i + n + 1)
                            if i:
                                pool.wait_ge(S.chunk_out, i)
                            nc.gpsimd.tensor_tensor(am[0], p0[:, 0:P], p0[:, P:2 * P], O.add)\
                                .then_inc(S.forward_sum, 1)

                @block.vector
                def _(dve):
                    steps = [0]

                    def link(ins):
                        steps[0] += 1
                        ins.then_inc(S.dve_step, 1)
                        dve.wait_ge(S.dve_step, steps[0])

                    def gate_sum(j, dr):
                        u = 2 * j + dr
                        z = z_[:, dr, j, :]
                        t1, lf, b = buf_t1[dr], z, buf_b[dr]
                        dve.wait_ge(S.absolute, u + 1)
                        if j >= 1:
                            dve.wait_ge(S.head_root, j)
                        nc.vector.scalar_tensor_tensor(buf_k[dr], z, 0.0, t1, O.max, O.add).then_inc(S.log_k, 1)
                        link(nc.vector.scalar_tensor_tensor(lf, z, 0.0, t1, O.min, O.subtract))
                        if dr == 0:
                            nc.vector.tensor_tensor_scan(b[:, 0:L], const("reset"), lf[:, 0:L], 0.0, O.mult, O.add)
                            link(nc.vector.tensor_tensor_scan(b[:, L:T], const("one"), lf[:, L:T], 0.0,
                                                              O.mult, O.add))
                        else:
                            nc.vector.tensor_tensor_scan(rev(b[:, 0:L]), const("reset"), rev(lf[:, 0:L]), 0.0,
                                                         O.mult, O.add)
                            nc.vector.tensor_tensor_scan(rev(b[:, L:T]), const("one"), rev(lf[:, L:T]), 0.0,
                                                         O.mult, O.add).then_inc(S.decays, 1)
                            dve.wait_ge(S.decays, j + 1)
                        end = P - 1 if dr == 0 else 0
                        b4 = b[:, 0:L].rearrange("p (n c) -> p n c", c=P)
                        nc.vector.tensor_tensor(lf[:, 0:L].rearrange("p (n c) -> p n c", c=P),
                                                b4[:, :, end:end + 1].to_broadcast([P, NB, P]), b4, O.subtract)
                        cend = T - 1 if dr == 0 else L
                        last = nc.vector.tensor_tensor(lf[:, L:T], b[:, cend:cend + 1].to_broadcast([P, LC]),
                                                       b[:, L:T], O.subtract)
                        if dr == 0:
                            last = exponents(nc.vector, 0)
                        last.then_inc(S.exponents, 1)

                    def weigh(j, dr):
                        q, k_ = q_[:, j, :], buf_k[dr]
                        dve.wait_ge(S.weights, 2 * j + dr + 1)
                        nc.vector.tensor_tensor(buf_t1[dr][:, 0:L], q, buf_eb[dr], O.mult)
                        nc.vector.tensor_tensor(z_[:, dr, j, :], z_[:, dr, j, :], k_, O.mult).then_inc(S.state_keys, 1)
                        for lev in range(LEV):
                            xl, xr = levels(buf_x[dr][:, lev * L:(lev + 1) * L], lev)
                            ql, qr = levels(q, lev)
                            kl, kr = levels(k_[:, 0:L], lev)
                            if dr == 0:
                                nc.vector.tensor_tensor(xr, xr, qr, O.mult)
                                last = nc.vector.tensor_tensor(xl, xl, kl, O.mult)
                            else:
                                nc.vector.tensor_tensor(xl, xl, ql, O.mult)
                                last = nc.vector.tensor_tensor(xr, xr, kr, O.mult)
                        last.then_inc(S.levelled, 1)

                    def states(j, dr):
                        u = 2 * j + dr
                        s, eb = buf_s[dr], buf_eb[dr]
                        dve.wait_ge(S.flipped, u + 1)
                        nc.vector.tensor_copy(buf_kt, bank2(2 * dr)[:, 0:5 * P]).then_inc(S.copied, 1)
                        dve.wait_ge(S.own, u + 1)
                        end = P - 1 if dr == 0 else 0
                        for i in range(NB):
                            o = s[i]
                            if i == 0:
                                link(nc.vector.tensor_copy(o, PS[:, 4, 0:P]))
                            else:
                                dec = order(dr)[i - 1] * P + end
                                link(nc.vector.scalar_tensor_tensor(o, s[i - 1], eb[:, dec:dec + 1],
                                                                    PS[:, 4, i * P:(i + 1) * P], O.mult, O.add))

                    def masks(j, n):
                        i = j * NB + n
                        for dr in range(2):
                            dve.wait_ge(S.products, 2 * i + dr + 1)
                            m = constb("scan")[:, dr * 1024:(dr + 1) * 1024]
                            nc.vector.tensor_tensor(prods[dr], bank2(2 * dr), m, O.mult).then_inc(S.masked, 1)
                        dve.wait_ge(S.masked, 2 * i + 2)
                        link(nc.vector.tensor_reduce(am[1], prods[1].rearrange("p (l c) -> p c l", l=8), AX, O.add))
                        dve.wait_ge(S.forward_sum, i + 1)
                        nc.vector.tensor_tensor(am[0], am[0], am[1], O.add).then_inc(S.summed, 1)

                    if step == 0:
                        for n in range(12):
                            c_stream.split_low(dve, u0 + n)
                    if scans:
                        link(nc.vector.tensor_scalar(q_, q_, KSCALE, None, O.mult))
                        for j in range(2):
                            gate_sum(j, 0)
                            gate_sum(j, 1)
                            for dr in range(2):
                                weigh(j, dr)
                                states(j, dr)
                            for n in range(NB):
                                masks(j, n)
                            o = buf_b[0][:, 0:L]
                            dve.wait_ge(S.chunk_out, NB * (j + 1))
                            nc.vector.tensor_copy(o, PS[:, 5, :]).then_inc(S.head_copied, 1)
                            dve.wait_ge(S.head_root, j + 1)
                            link(nc.vector.reciprocal(buf_eb[0], buf_eb[0]))
                            link(nc.vector.scalar_tensor_tensor(o, o, vec1("gnorm"), buf_eb[0], O.mult, O.mult))
                            y = yh[:, 2 * pair + j, :]
                            nc.vector.tensor_tensor(y, y, o, O.mult).then_inc(S.normed, 1)

                @block.scalar
                def _(act):
                    def empty(i):
                        if not projects:
                            return
                        kind, j, u = C_TILES[i]
                        act.wait_ge(S.pe_tile, i + 1)
                        if kind == "q":
                            ins = nc.scalar.activation(qn[:, j, :], bank2(6)[:, 0:L], A.Silu)
                        elif kind == "z":
                            ins = nc.scalar.activation(zn[:, j // 2, j % 2, :], bank2(6)[:, 0:T], A.Copy)
                        elif kind == "g":
                            ins = nc.scalar.activation(yh[:, 2 * step + j, :], bank2(6)[:, 0:L], A.Silu)
                        else:
                            n = 4 if j == 0 else 2
                            ins = nc.scalar.activation(iv[:, 4 * j:4 * j + n, :],
                                                       bank2(6)[:, 0:n * 256].rearrange("p (i n) -> p i n", i=n),
                                                       A.Copy)
                        ins.then_inc(S.act_out, 1)
                        high(SPLIT_AFTER[i])

                    def high(units):
                        for n in units:
                            c_stream.split_high(act, S, u0, u0 + n, done=UNIT_DONE)

                    steps = [0]

                    def link(ins):
                        steps[0] += 1
                        ins.then_inc(S.act_step, 1)
                        act.wait_ge(S.act_step, steps[0])

                    def weights(j, dr):
                        u = 2 * j + dr
                        act.wait_ge(S.log_k, u + 1)
                        nc.scalar.activation(buf_k[dr], buf_k[dr], A.Exp, scale=-1.0)
                        act.wait_ge(S.exponents, u + 1)
                        nc.scalar.activation(buf_eb[dr], buf_b[dr][:, 0:L], A.Exp)
                        link(nc.scalar.activation(z_[:, dr, j, :], z_[:, dr, j, :], A.Exp))
                        if dr == 1:
                            act.wait_ge(S.ready, j + 1)
                        nc.scalar.activation(buf_x[dr], buf_x[dr], A.Exp).then_inc(S.weights, 1)

                    if step == 0:
                        high([0, 1])
                    for j in range(2):
                        if scans:
                            for dr in range(2):
                                link(nc.scalar.activation(buf_t1[dr], z_[:, dr, j, :], A.Abs))
                            for t1 in buf_t1:
                                link(nc.scalar.activation(t1, t1, A.Exp, scale=-1.0))
                            for t1 in buf_t1:
                                nc.scalar.activation(t1, t1, A.Ln, bias=1.0).then_inc(S.absolute, 1)
                        empty(5 * j)
                        if j == 0:
                            empty(1)
                        if scans:
                            weights(j, 0)
                        if j:
                            empty(6)
                        if scans:
                            weights(j, 1)
                        for i in range(2, 5):
                            empty(5 * j + i)
                        if scans:
                            act.wait_ge(S.head_copied, j + 1)
                            nc.scalar.activation(buf_k[0][:, 0:L], buf_b[0][:, 0:L], A.Square)\
                                .then_inc(S.head_squared, 1)
                            act.wait_ge(S.head_sum, j + 1)
                            nc.scalar.activation(buf_eb[0], PS[:, 5, :], A.Sqrt, bias=const("eps")[:, 1:2],
                                                 scale=1.0 / P).then_inc(S.head_root, 1)

                @block.tensor
                def _(pe):
                    def tile(i):
                        if not projects:
                            return
                        kind, j, units = C_TILES[i]
                        pe.wait_ge(w_split, u0 + units[-1] + 1)
                        if i >= 1:
                            pe.wait_ge(S.act_out, i)
                        ps = bank2(6)
                        if kind == "i":
                            wh, wl = [w[:, :].rearrange("p (s k n) -> p k s n", s=2, k=KT)
                                      for w in (c_stream.w_high, c_stream.w_low)]
                            for m in (range(4) if j == 0 else range(4, 6)):
                                ts = slice(m * P, (m + 1) * P)
                                for k in range(KT):
                                    last = product3(ps[:, (m % 4) * 256:(m % 4 + 1) * 256], ch[k][:, ts],
                                                    cl[k][:, ts], wh[:, k, :, :], wl[:, k, :, :], k == 0,
                                                    k == KT - 1)
                        else:
                            wh, wl = [w(u0 + units[0]).rearrange("p (k n) -> p k n", k=KT)
                                      for w in (c_stream.high, c_stream.low)]
                            for a, b in ((0, L), (L, T)) if kind == "z" else ((0, L),):
                                for k in range(KT):
                                    last = product3(ps[:, a:b], wh[:, k, :], wl[:, k, :], ch[k][:, a:b],
                                                    cl[k][:, a:b], k == 0, k == KT - 1)
                        last.then_inc(S.pe_tile, 1)

                    def own_states(j, dr):
                        if not scans:
                            return
                        u = 2 * j + dr
                        od = order(dr)
                        pe.wait_ge(S.state_keys, u + 1)
                        if dr == 0 and j >= 1:
                            pe.wait_ge(S.summed, NB * j)
                        for i in range(5):
                            a = L + i * P if i < 2 else od[i - 2] * P
                            last = nc.tensor.transpose(bank2(2 * dr)[:, i * P:(i + 1) * P], z_[:, dr, j, a:a + P], ident)
                        last.then_inc(S.flipped, 1)
                        pe.wait_ge(S.copied, u + 1)
                        v = i_[:, :, j * P:(j + 1) * P]
                        for i in range(2):
                            nc.tensor.matmul(PS[:, 4, 0:P], buf_kt[:, i * P:(i + 1) * P], v[:, 4 + i, :],
                                             start=(i == 0), stop=(i == 1))
                        for i in range(3):
                            last = nc.tensor.matmul(PS[:, 4, (i + 1) * P:(i + 2) * P],
                                                    buf_kt[:, (2 + i) * P:(3 + i) * P], v[:, od[i], :],
                                                    start=True, stop=True)
                        last.then_inc(S.own, 1)

                    def products(j, n, dr):
                        i = 2 * (j * NB + n) + dr
                        cs = slice(n * P, (n + 1) * P)
                        pe.wait_ge(S.levelled, 2 * j + dr + 1)
                        if n > 0:
                            pe.wait_ge(S.masked, i - 1)
                        for lev in range(LEV):
                            xv = buf_x[dr][:, lev * L + n * P:lev * L + (n + 1) * P]
                            nc.tensor.matmul(bank2(2 * dr)[:, lev * P:(lev + 1) * P], xv, xv, start=True, stop=True)
                        nc.tensor.matmul(bank2(2 * dr)[:, LEV * P:(LEV + 1) * P], buf_k[dr][:, cs], q_[:, j, cs],
                                         start=True, stop=True).then_inc(S.products, 1)

                    def chunk(j, n):
                        i = j * NB + n
                        cs = slice(n * P, (n + 1) * P)
                        if n == 0 and j >= 1:
                            pe.wait_ge(S.head_root, j)
                        pe.wait_ge(S.summed, i + 1)
                        o = PS[:, 5, cs]
                        nc.tensor.matmul(o, buf_s[0][n], buf_t1[0][:, cs], start=True, stop=False)
                        r = NB - 1 - n
                        nc.tensor.matmul(o, buf_s[1][r], buf_t1[1][:, cs], start=False, stop=False)
                        nc.tensor.matmul(o, i_[:, n, j * P:(j + 1) * P], am[0], start=False, stop=True)\
                            .then_inc(S.chunk_out, 1)

                    for j in range(2):
                        for i in range(3):
                            tile(5 * j + i)
                        own_states(j, 0)
                        tile(5 * j + 3)
                        own_states(j, 1)
                        tile(5 * j + 4)
                        if scans:
                            for n in range(NB):
                                products(j, n, 0)
                                products(j, n, 1)
                                if n >= 1:
                                    chunk(j, n - 1)
                            chunk(j, NB - 1)
                            pe.wait_ge(S.head_squared, j + 1)
                            nc.tensor.matmul(PS[:, 5, :], ones, buf_k[0][:, 0:L], start=True, stop=True)\
                                .then_inc(S.head_sum, 1)

        stage_modulate(1, modulated, lambda sp: c_stream.start(sp, src_c), ch, cl)
        for step in range(CH // 2 + 1):
            stage_c(step)
        stage_out1(1, UC["c_out"], yh, L, c_stream, src_c, 1, [v[:, 0:L] for v in ch], [v[:, 0:L] for v in cl])
        c = Carve(0, arena3)
        sq1, tmp1 = c(KT * T).rearrange("p (k t) -> p k t", k=KT), c(T + 1)
        stage_layer_norm(1, L, sq1, tmp1)
        hgrn.close()

        raw_ring = sb("raw_ring", RAW * UNIT)
        w_high, w_low = sb("w_high", SLOTS * UNIT, f32r), sb("w_low", SLOTS * UNIT, f32r)
        a_high, a_low = sb("a_high", KT * L, f32r), sb("a_low", KT * L, f32r)
        gate_high, gate_low = sb("gate_high", KT * 24, f32r), sb("gate_low", KT * 24, f32r)
        v2 = sb("v2", NV2)
        arena2 = sb("arena2", 23019)
        ah = [a_high[:, k * L:(k + 1) * L] for k in range(KT)]
        al = [a_low[:, k * L:(k + 1) * L] for k in range(KT)]
        c = Carve(0, arena2)
        rows = c(NR2)
        wgate = c(KT * 24)
        rstd = c(2 * L).rearrange("p (g t) -> p g t", g=2)
        cg = c(NCG)
        fbuf_at = c.at
        fbuf = c(KT * L).rearrange("p (k t) -> p k t", k=KT)
        sq_at = c.at
        sq = c(KT * L).rearrange("p (k t) -> p k t", k=KT)
        hid_at = sq_at
        scratch_at = fbuf_at
        c = Carve(scratch_at + 5144, arena2)
        q2 = c(NT4 * L).rearrange("p (j t) -> p j t", j=NT4)
        ksw = c(2 * L).rearrange("p (b t) -> p b t", b=2)
        assert c.at > sq_at + KT * L
        y2 = c(KT * L).rearrange("p (k t) -> p k t", k=KT)
        zu = y2[:, NT4:, :]
        after_y2 = c.at
        pcT = c(NB * 2 * P).rearrange("p (i g q) -> p i g q", i=NB, g=2)
        kvc = arena2[:, after_y2:after_y2 + 2 * L].rearrange("p (g t) -> p g t", g=2)
        vt2 = c(NB * 256).rearrange("p (i n) -> p i n", i=NB)
        zv = c(NB * L).rearrange("p (i n) -> p i n", i=NB)
        gates = c(NB * 24).rearrange("p (i n) -> p i n", i=NB)
        wsT = c(NH * P).rearrange("p (g t) -> p g t", g=NH)
        hT = c(4 * 64).rearrange("p (v h n) -> p v h n", v=2, h=2)
        kcT = c(64)
        vcr = c(2 * HD).rearrange("p (g e) -> p g e", g=2)
        c = Carve(scratch_at, arena2)
        blk = c(32 * 64)
        blk4 = blk.rearrange("p (l g n) -> p l g n", l=32, g=2)
        blk3 = blk.rearrange("p (l n) -> p l n", l=32)
        raw_h = c(2 * 256)
        blocks = a_high[:, :].rearrange("p (l s n) -> p l s n", l=32, s=2)
        c = Carve(hid_at, arena2)
        hid = c(FT * L).rearrange("p (j t) -> p j t", j=FT)
        c = Carve(fbuf_at, arena2)
        hc = c(2 * 2 * L).rearrange("p (b s t) -> p b s t", b=2, s=2)
        c = Carve(hid_at + KT * L, arena2)
        pT = c(2 * L).rearrange("p (k t) -> p k t", k=2)
        pg = c(KT * L).rearrange("p (k t) -> p k t", k=KT)

        def const2(name):
            return cg[:, CG[name][0]:CG[name][1]]

        stream2 = SplitStream(NU2, NSPLIT, raw_ring, w_high, w_low)
        raw, high, low = stream2.raw, stream2.high, stream2.low
        stream_raw, split_high, split_low = stream2.load, stream2.split_high, stream2.split_low

        def row(name):
            return rows[:, R2[name][0]:R2[name][1]]

        def bank2(b):
            return PS[:, b:b + 2, :].rearrange("p b n -> p (b n)")

        class Normalise:
            def __init__(self, S, groups, summed=False):
                self.S, self.groups, self.summed = S, groups, summed
                self.flat = [(g, k) for g, (src, _gain) in enumerate(groups) for k in range(len(src))]

            def squares(self, act):
                if self.summed:
                    return
                for i, (g, k) in enumerate(self.flat):
                    nc.scalar.activation(sq[:, i, :], self.groups[g][0][k], A.Square)\
                        .then_inc(self.S.rms_squares, 1)

            def high(self, act):
                for g, (src, _gain) in enumerate(self.groups):
                    if not self.summed:
                        act.wait_ge(self.S.rms_sums, g + 1)
                    nc.scalar.activation(rstd[:, g, :], PS[:, 6 + g, :], A.Sqrt, bias=const("eps")[:, 1:2],
                                         scale=1.0 / (P * len(src))).then_inc(self.S.rms_root, 1)
                for i in range(KT):
                    act.wait_ge(self.S.rms_scaled, i + 1)
                    nc.scalar.activation(ah[i], sq[:, i, :], A.Copy).then_inc(self.S.rms_high, 1)

            def sums(self, pe):
                if self.summed:
                    return
                for i, (g, k) in enumerate(self.flat):
                    pe.wait_ge(self.S.rms_squares, i + 1)
                    n = len(self.groups[g][0])
                    ins = nc.tensor.matmul(PS[:, 6 + g, :], ones, sq[:, i, :], start=(k == 0), stop=(k == n - 1))
                    if k == n - 1:
                        ins.then_inc(self.S.rms_sums, 1)

            def low(self, eng, which, i):
                if i >= 0 and i % 2 == which:
                    eng.wait_ge(self.S.rms_high, i + 1)
                    (nc.vector if which else nc.gpsimd).tensor_tensor(
                        al[i], sq[:, i, :], ah[i].bitcast(f32), O.subtract)\
                        .then_inc(self.S.rms_odd if which else self.S.rms_even, 1)

            def scale(self, dve):
                for g in range(len(self.groups)):
                    dve.wait_ge(self.S.rms_root, g + 1)
                    nc.vector.reciprocal(rstd[:, g, :], rstd[:, g, :]).then_inc(self.S.rms_step, 1)
                    dve.wait_ge(self.S.rms_step, g + 1)
                    for i, (gi, k) in enumerate(self.flat):
                        if gi == g:
                            src, gain = self.groups[g]
                            nc.vector.scalar_tensor_tensor(sq[:, i, :], src[k], gain(k), rstd[:, g, :],
                                                           O.mult, O.mult).then_inc(self.S.rms_scaled, 1)
                            self.low(dve, 1, i - 1)
                self.low(dve, 1, KT - 1)

            def even(self, pool):
                for i in range(KT):
                    self.low(pool, 0, i)

            def tile(self, pe, k):
                if k % 2:
                    pe.wait_ge(self.S.rms_odd, k // 2 + 1)
                else:
                    pe.wait_ge(self.S.rms_even, k // 2 + 1)

        def layer2(layer):
            def src2(n):
                return d["w2"][layer, n, :, :]

            def small_loads(sp, S):
                stream2.start(sp, src2)
                sp.dma_start(v2[:, :], d["v2"][layer, :, :]).then_inc(S.load, 16)
                sp.dma_start(rows, d["r2"][layer, :, :]).then_inc(S.load, 16)
                sp.dma_start(wgate, d["wgate"][layer, :, :]).then_inc(S.load, 16)
                sp.dma_start(wsT.rearrange("p g t -> p (g t)"), d["wsT"][layer, :, :]).then_inc(S.load, 16)
                return 64

            def stage_loads():
                S, N = stage_sems()
                with nc.Block() as block:
                    @block.sync
                    def _(sp):
                        sp.sem_clear(N.range)
                        sp.wait_ge(S.load, small_loads(sp, S))

            xt = [X[:, k, 0:L] for k in range(KT)]

            def stage_in2(groups):
                S, N = stage_sems()
                norm = Normalise(S, groups)
                u0 = U2["in2"]
                with nc.Block() as block:
                    @block.sync
                    def _(sp):
                        sp.sem_clear(N.range)
                        stream_raw(sp, src2, u0 - 1, u0 + 9)

                    @block.gpsimd
                    def _(pool):
                        norm.even(pool)

                    @block.tensor
                    def _(pe):
                        norm.sums(pe)
                        for u in range(10):
                            if u < 9:
                                pe.wait_ge(w_split, u0 + u + 1)
                            else:
                                pe.wait_ge(S.dve_step, 1)
                            if u >= 4:
                                pe.wait_ge(S.act_out, u - 3)
                            ps = bank2(2 * (u % 4))
                            wh, wl = [v.rearrange("p (k n) -> p k n", k=KT) for v in
                                      ((high(u0 + u), low(u0 + u)) if u < 9 else (gate_high[:, :], gate_low[:, :]))]
                            if u in (4, 7, 8, 9):
                                n = 24 if u == 9 else 256
                                for m in range(NB):
                                    ts = slice(m * P, (m + 1) * P)
                                    for k in range(KT):
                                        last = product3(ps[:, m * n:(m + 1) * n], ah[k][:, ts], al[k][:, ts],
                                                        wh[:, k, :], wl[:, k, :], k == 0, k == KT - 1)
                            else:
                                for h in range(2):
                                    hs = slice(h * P, (h + 1) * P)
                                    for k in range(KT):
                                        if u + h == 0:
                                            norm.tile(pe, k)
                                        last = product3(ps[:, h * L:(h + 1) * L], wh[:, k, hs], wl[:, k, hs],
                                                        ah[k], al[k], k == 0, k == KT - 1)
                            last.then_inc(S.pe_tile, 1)

                    @block.scalar
                    def _(act):
                        norm.squares(act)
                        split_high(act, S, u0, u0)
                        nc.scalar.activation(gate_high[:, :], wgate, A.Copy).then_inc(S.act_step, 1)
                        norm.high(act)
                        for u in range(10):
                            if u < 9:
                                split_high(act, S, u0, u0 + u + 1)
                            act.wait_ge(S.pe_tile, u + 1)
                            ps = bank2(2 * (u % 4))
                            if u < 2:
                                ins = nc.scalar.activation(q2[:, 2 * u:2 * u + 2, :], ps.rearrange(
                                    "p (j t) -> p j t", j=2), A.Copy)
                            elif u == 2:
                                ins = nc.scalar.activation(kvc, ps.rearrange("p (j t) -> p j t", j=2), A.Copy)
                            elif u == 3:
                                ins = nc.scalar.activation(ksw, ps.rearrange("p (j t) -> p j t", j=2), A.Copy)
                            elif u == 4:
                                ins = nc.scalar.activation(vt2, ps.rearrange("p (j t) -> p j t", j=4), A.Copy)
                            elif u < 7:
                                ins = nc.scalar.activation(zu[:, 2 * (u - 5):2 * (u - 5) + 2, :], ps.rearrange(
                                    "p (j t) -> p j t", j=2), A.Gelu_apprx_tanh)
                            elif u < 9:
                                ins = nc.scalar.activation(zv[:, :, 256 * (u - 7):256 * (u - 6)], ps.rearrange(
                                    "p (j t) -> p j t", j=4), A.Gelu_apprx_tanh)
                            else:
                                ins = nc.scalar.activation(gates, ps[:, 0:96].rearrange("p (i n) -> p i n", i=NB),
                                                           A.Sigmoid)
                            ins.then_inc(S.act_out, 1)

                    @block.vector
                    def _(dve):
                        split_low(dve, u0)
                        dve.wait_ge(S.act_step, 1)
                        nc.vector.tensor_tensor(gate_low[:, :], wgate, gate_high[:, :].bitcast(f32), O.subtract)\
                            .then_inc(S.dve_step, 1)
                        norm.scale(dve)
                        for u in range(9):
                            split_low(dve, u0 + u + 1)

            def stage_compress():
                S, N = stage_sems()
                u0 = U2["cmp1"]
                with nc.Block() as block:
                    @block.sync
                    def _(sp):
                        sp.sem_clear(N.range)
                        stream_raw(sp, src2, u0, u0 + 4)

                    @block.gpsimd
                    def _(pool):
                        src = blk4[:, :, :, NCMP:32]
                        nc.gpsimd.memset(src, 0.0).then_inc(S.ready, 1)

                    @block.vector
                    def _(dve):
                        pe_ = v2[:, V2["pe"][0]:V2["pe"][1]]
                        for a in range(2):
                            for g in range(2):
                                src = kvc[:, g, 16 * a:16 * a + 16 * NCMP].rearrange("p (n b) -> p b n", b=16)
                                last = nc.vector.tensor_tensor(
                                    blk4[:, 16 * a:16 * a + 16, g, 0:NCMP], src,
                                    pe_[:, 16 * a:16 * a + 16].unsqueeze(2).to_broadcast([P, 16, NCMP]), O.add)
                            last.then_inc(S.dve_step, 1)
                        for a in range(2):
                            ls = slice(16 * a, 16 * a + 16)
                            dve.wait_ge(S.copied, a + 1)
                            nc.vector.tensor_tensor(blocks[:, ls, 1, :], blk3[:, ls, :],
                                                    blocks[:, ls, 0, :].bitcast(f32), O.subtract)\
                                .then_inc(S.normed, 1)
                        for u in range(4):
                            split_low(dve, u0 + u + 1)
                        dve.wait_ge(S.pe_tile, 6)
                        nc.vector.tensor_tensor(vcr, PS[:, 5, 0:P].rearrange("p (g e) -> p g e", g=2),
                                                row("b2v").unsqueeze(1).to_broadcast([P, 2, HD]), O.add)

                    @block.tensor
                    def _(pe):
                        for u in range(4):
                            pe.wait_ge(w_split, u0 + u + 1)
                            wh, wl = [v.rearrange("p (l n) -> p l n", l=8) for v in (high(u0 + u), low(u0 + u))]
                            if u in (0, 2):
                                pe.wait_ge(S.normed, u // 2 + 1)
                            for l8 in range(8):
                                l_ = 8 * u + l8
                                for w in (wh, wl):
                                    for kv in range(2):
                                        hs = slice(HD * kv, HD * kv + HD)
                                        last = nc.tensor.matmul(
                                            PS[:, kv, 0:256], blocks[hs, l_, :, :].rearrange("p s n -> p (s n)"),
                                            w[hs, l8, :], start=(l_ == 0 and w is wh), stop=(l_ == 31 and w is wl))
                            last.then_inc(S.pe_tile, 1)
                        pe.wait_ge(S.act_out, 1)
                        for i in range(4):
                            last = nc.tensor.matmul(PS[:, 2, 64 * i:64 * i + 64], raw_h[:, i * P:(i + 1) * P],
                                                    const2("fold"), start=True, stop=True)
                        last.then_inc(S.flipped, 1)
                        pe.wait_ge(S.act_out, 5)
                        w2k = row("w2k").rearrange("p (h n) -> p h n", h=2)
                        w2v = row("w2v").rearrange("p (h n) -> p h n", h=2)
                        for h in range(2):
                            last = nc.tensor.matmul(PS[:, 4, 0:64], w2k[:, h, :], hT[:, 0, h, :], start=(h == 0),
                                                    stop=(h == 1))
                        last.then_inc(S.pe_tile, 1)
                        for r in range(4):
                            for g in range(2):
                                for h in range(2):
                                    last = nc.tensor.matmul(PS[32 * r:32 * r + 32, 5, g * HD:(g + 1) * HD],
                                                            hT[:, 1, h, 32 * g:32 * g + 32], w2v[:, h, :],
                                                            start=(h == 0), stop=(h == 1))
                        last.then_inc(S.pe_tile, 1)

                    @block.scalar
                    def _(act):
                        act.wait_ge(S.ready, 1)
                        for a in range(2):
                            ls = slice(16 * a, 16 * a + 16)
                            act.wait_ge(S.dve_step, a + 1)
                            nc.scalar.activation(blocks[:, ls, 0, :], blk3[:, ls, :], A.Copy).then_inc(S.copied, 1)
                        for u in range(4):
                            split_high(act, S, u0, u0 + u + 1)
                        act.wait_ge(S.pe_tile, 4)
                        nc.scalar.activation(raw_h.rearrange("p (v n) -> p v n", v=2), PS[:, 0:2, 0:256], A.Copy)\
                            .then_inc(S.act_out, 1)
                        act.wait_ge(S.flipped, 1)
                        for kv in range(2):
                            for h in range(2):
                                i = 2 * kv + h
                                nc.scalar.activation(hT[:, kv, h, :], PS[:, 2, 64 * i:64 * i + 64],
                                                     A.Gelu_apprx_tanh, bias=vec2("b1", i)).then_inc(S.act_out, 1)
                        act.wait_ge(S.pe_tile, 5)
                        nc.scalar.activation(kcT, PS[:, 4, 0:64], A.Identity, bias=vec2("b2k"))

            def stage_gmlp_and_cmp_attention():
                S, N = stage_sems()
                cc = Carve(scratch_at, arena2)
                e = cc(NB * 256).rearrange("p (i n) -> p i n", i=NB)
                st = cc(NB * 32).rearrange("p (i n) -> p i n", i=NB)
                gst = cc(NB * 16).rearrange("p (i n) -> p i n", i=NB)
                vm = cc(NT4 * L).rearrange("p (j t) -> p j t", j=NT4)
                with nc.Block() as block:
                    @block.sync
                    def _(sp):
                        sp.sem_clear(N.range)

                    @block.tensor
                    def _(pe):
                        for n in range(NB):
                            m = constb("cmp")[:, n * 32:(n + 1) * 32].unsqueeze(1).to_broadcast([P, 4, 32])
                            for g in range(2):
                                hs = slice(HD * g, HD * g + HD)
                                nc.tensor.matmul(PS[:, n + 4 * g, 0:P], constb("ident"), m, start=True, stop=False)
                                for h in range(4):
                                    last = nc.tensor.matmul(PS[:, n + 4 * g, 32 * h:32 * h + 32],
                                                            q2[hs, h, n * P:(n + 1) * P],
                                                            kcT[hs, 32 * g:32 * g + 32], start=False, stop=(h == 3))
                            last.then_inc(S.scores, 1)
                        pe.wait_ge(S.rms_scaled, NB)
                        for j in range(NT4):
                            for h in range(2):
                                g = 2 * j + h
                                for ck in range(NB):
                                    last = nc.tensor.matmul(PS[HD * h:HD * h + HD, 4 + j, ck * P:(ck + 1) * P],
                                                            zv[:, ck, g * HD:(g + 1) * HD], wsT[:, g, :],
                                                            start=True, stop=True)
                            last.then_inc(S.pe_tile, 1)
                        for n in range(NB):
                            pe.wait_ge(S.normed, n + 1)
                            for g in range(2):
                                last = nc.tensor.transpose(PS[:, n, g * P:(g + 1) * P],
                                                           e[:, n, g * P:(g + 1) * P], ident)
                            last.then_inc(S.flipped, 1)

                    @block.scalar
                    def _(act):
                        act.wait_ge(S.ready, 1)
                        nc.scalar.activation(gst[:, :, 8:9], gst[:, :, 7:8], A.Sqrt, bias=const("eps")[:, 1:2])\
                            .then_inc(S.rms_root, 1)
                        for n in range(NB):
                            act.wait_ge(S.shift, n + 1)
                            nc.scalar.activation(e[:, n, :], e[:, n, :], A.Exp).then_inc(S.probs, 1)
                        for n in range(NB):
                            act.wait_ge(S.flipped, n + 1)
                            nc.scalar.activation(pcT[:, n, :, :].rearrange("p g q -> p (g q)"), PS[:, n, 0:256],
                                                 A.Copy)

                    @block.vector
                    def _(dve):
                        steps = [0]

                        def link(ins):
                            steps[0] += 1
                            ins.then_inc(S.dve_step, 1)
                            dve.wait_ge(S.dve_step, steps[0])

                        def heads(v):
                            return v.rearrange("p (h n) -> p h n", h=NH)

                        nc.vector.tensor_tensor(wsT, wsT, const2("tri").unsqueeze(1).to_broadcast([P, NH, P]),
                                                O.mult)
                        for i in range(NB):
                            last = nc.vector.bn_stats(gst[:, i, 0:6], zv[:, i, :])
                        link(last)
                        for i in range(NB):
                            last = nc.vector.bn_aggr(gst[:, i, 6:8], gst[:, i, 0:6])
                        last.then_inc(S.ready, 1)
                        for n in range(NB):
                            dve.wait_ge(S.scores, n + 1)
                            b = st[:, n, :]
                            ps = [PS[:, n + 4 * g, 0:P].rearrange("p (h n) -> p h n", h=4) for g in range(2)]
                            for g in range(2):
                                last = nc.vector.tensor_reduce(b[:, 4 * g:4 * g + 4], ps[g], AX, O.max)
                            link(last)
                            link(nc.vector.tensor_scalar(b[:, 8:16], b[:, 0:8], NEG / 10, -ASCALE, O.max, O.mult))
                            for g in range(2):
                                last = nc.vector.scalar_tensor_tensor(
                                    heads(e[:, n, :])[:, 4 * g:4 * g + 4, :], ps[g], ASCALE,
                                    b[:, 8 + 4 * g:12 + 4 * g].unsqueeze(2).to_broadcast([P, 4, 32]), O.mult, O.add)
                            last.then_inc(S.shift, 1)
                        dve.wait_ge(S.rms_root, 1)
                        link(nc.vector.reciprocal(gst[:, :, 9:10], gst[:, :, 8:9]))
                        for i in range(NB):
                            last = nc.vector.tensor_scalar(zv[:, i, :], zv[:, i, :], gst[:, i, 6:7], gst[:, i, 9:10],
                                                           O.subtract, O.mult)
                        link(last)
                        link(nc.vector.tensor_tensor(zv, zv, row("ln_g").unsqueeze(1).to_broadcast([P, NB, L]),
                                                     O.mult))
                        for i in range(NB):
                            nc.vector.tensor_tensor(zv[:, i, :], zv[:, i, :], row("ln_b"), O.add)\
                                .then_inc(S.rms_scaled, 1)
                        for n in range(NB):
                            dve.wait_ge(S.probs, n + 1)
                            b = st[:, n, :]
                            ev = heads(e[:, n, :])
                            link(nc.vector.tensor_reduce(b[:, 16:24], ev, AX, O.add))
                            link(nc.vector.tensor_scalar(b[:, 16:24], b[:, 16:24], 1e-30, None, O.max))
                            link(nc.vector.reciprocal(b[:, 24:32], b[:, 16:24]))
                            g = gates[:, n, :].rearrange("p (h c) -> p c h", c=3)[:, 0, :]
                            link(nc.vector.tensor_tensor(b[:, 24:32], b[:, 24:32], g, O.mult))
                            nc.vector.tensor_tensor(ev, ev, b[:, 24:32].unsqueeze(2).to_broadcast([P, NH, 32]),
                                                    O.mult).then_inc(S.normed, 1)
                        for j in range(NT4):
                            dve.wait_ge(S.pe_tile, j + 1)
                            b = row("bs").rearrange("p (j t) -> p j t", j=NT4)[:, j, :]
                            nc.vector.tensor_tensor(vm[:, j, :].rearrange("p (c t) -> p c t", c=NB),
                                                    PS[:, 4 + j, :].rearrange("p (c t) -> p c t", c=NB),
                                                    b.unsqueeze(1).to_broadcast([P, NB, P]), O.add)\
                                .then_inc(S.dve_out, 1)
                            dve.wait_ge(S.dve_out, j + 1)
                            nc.vector.tensor_tensor(y2[:, 4 + j, :], zu[:, j, :], vm[:, j, :], O.mult)

            def stage_attention():
                S, N = stage_sems()
                cc = Carve(scratch_at, arena2)
                pr = cc(3 * 2 * L).rearrange("p (b s t) -> p b s t", b=3, s=2)
                pt = cc(2 * 2 * L).rearrange("p (b s t) -> p b s t", b=2, s=2)
                st = cc(3 * 8).rearrange("p (b n) -> p b n", b=3)
                jobs = [(n, h) for n in range(NB) for h in range(NH)]
                NJ = len(jobs)

                def half(h):
                    g = h // 4
                    return slice(HD * g, HD * g + HD)

                def region(j):
                    return PS[:, 2 * (j % 2):2 * (j % 2) + 2, :]

                with nc.Block() as block:
                    @block.sync
                    def _(sp):
                        sp.sem_clear(N.range)

                    @block.tensor
                    def _(pe):
                        def scores(j):
                            n, h = jobs[j]
                            hs = half(h)
                            if j >= 2:
                                pe.wait_ge(S.probs, j - 1)
                            for s in range(2):
                                nc.tensor.matmul(region(j)[:, s, 0:(n + 1) * P], q2[hs, h % 4, n * P:(n + 1) * P],
                                                 ksw[hs, s, 0:(n + 1) * P], start=True, stop=False)
                                last = nc.tensor.matmul(region(j)[:, s, n * P:(n + 1) * P], constb("ident"),
                                                        constb("up"), start=False, stop=True)
                            last.then_inc(S.scores, 1)

                        def flip(j):
                            n, h = jobs[j]
                            pe.wait_ge(S.normed, j + 1)
                            if j >= 1:
                                pe.wait_ge(S.copied, j)
                            for s in range(2):
                                for i in range(n + 1):
                                    last = nc.tensor.transpose(PS[:, 4 + s, i * P:(i + 1) * P],
                                                               pr[:, j % 3, s, i * P:(i + 1) * P], ident)
                            last.then_inc(S.flipped, 1)

                        def mix(j):
                            n, h = jobs[j]
                            hs = half(h)
                            g, r = h // 4, h % 4
                            pe.wait_ge(S.copied, j + 1)
                            if j >= 2:
                                pe.wait_ge(S.dve_out, j - 1)
                            o = PS[hs, 6 + j % 2, 0:P]
                            for s in range(2):
                                for i in range(n + 1):
                                    nc.tensor.matmul(o, vt2[:, i, s * P + HD * g:s * P + HD * g + HD],
                                                     pt[:, j % 2, s, i * P:(i + 1) * P], start=(s + i == 0),
                                                     stop=False)
                            rs = slice(32 * r, 32 * r + 32)
                            nc.tensor.matmul(o, vcr[rs, g, :], pcT[rs, n, g, :], start=False, stop=True)\
                                .then_inc(S.mixed, 1)

                        for s in range(NJ + 3):
                            if s < NJ:
                                scores(s)
                            if 2 <= s < NJ + 2:
                                flip(s - 2)
                            if s >= 3:
                                mix(s - 3)

                    @block.scalar
                    def _(act):
                        def exps(j):
                            n = jobs[j][0]
                            w = (n + 1) * P
                            act.wait_ge(S.shift, j + 1)
                            if j >= 3:
                                act.wait_ge(S.flipped, j - 2)
                            b = st[:, j % 3, :]
                            for s in range(2):
                                last = nc.scalar.activation(pr[:, j % 3, s, 0:w], region(j)[:, s, 0:w], A.Exp,
                                                            bias=b[:, 2 + s:3 + s], scale=ASCALE,
                                                            accum_out=b[:, 4 + s:5 + s])
                            last.then_inc(S.probs, 1)

                        def copy(j):
                            w = (jobs[j][0] + 1) * P
                            act.wait_ge(S.flipped, j + 1)
                            if j >= 2:
                                act.wait_ge(S.mixed, j - 1)
                            nc.scalar.activation(pt[:, j % 2, :, 0:w], PS[:, 4:6, 0:w], A.Copy)\
                                .then_inc(S.copied, 1)

                        for s in range(NJ + 2):
                            if s < NJ:
                                exps(s)
                            if s >= 2:
                                copy(s - 2)

                    @block.vector
                    def _(dve):
                        steps = [0]

                        def link(ins):
                            steps[0] += 1
                            ins.then_inc(S.dve_step, 1)
                            dve.wait_ge(S.dve_step, steps[0])

                        def shift(j):
                            w = (jobs[j][0] + 1) * P
                            dve.wait_ge(S.scores, j + 1)
                            if j >= 3:
                                dve.wait_ge(S.normed, j - 2)
                            b = st[:, j % 3, :]
                            link(nc.vector.tensor_reduce(b[:, 0:2], region(j)[:, :, 0:w], AX, O.max))
                            nc.vector.tensor_scalar(b[:, 2:4], b[:, 0:2], -ASCALE, None, O.mult)\
                                .then_inc(S.shift, 1)

                        def norm(j):
                            n, h = jobs[j]
                            w = (n + 1) * P
                            dve.wait_ge(S.probs, j + 1)
                            b = st[:, j % 3, :]
                            link(nc.vector.reciprocal(b[:, 6:8], b[:, 4:6]))
                            link(nc.vector.tensor_tensor(b[:, 6:8], b[:, 6:8], gates[:, n, 3 * h + 1:3 * h + 3],
                                                         O.mult))
                            for s in range(2):
                                p_ = pr[:, j % 3, s, 0:w]
                                last = nc.vector.tensor_scalar(p_, p_, b[:, 6 + s:7 + s], None, O.mult)
                            last.then_inc(S.normed, 1)

                        def out(j):
                            n, h = jobs[j]
                            hs = half(h)
                            dve.wait_ge(S.mixed, j + 1)
                            nc.vector.tensor_copy(y2[hs, h % 4, n * P:(n + 1) * P], PS[hs, 6 + j % 2, 0:P])\
                                .then_inc(S.dve_out, 1)

                        for s in range(NJ + 3):
                            if s < NJ:
                                shift(s)
                            if 1 <= s < NJ + 1:
                                norm(s - 1)
                            if s >= 3:
                                out(s - 3)

            def stage_project(name, nk, gain, src=None, groups=None):
                S, N = stage_sems()
                norm = Normalise(S, groups) if groups else None
                u0 = U2[name]
                chunks = [range(8 * v, min(8 * v + 8, nk)) for v in range((nk + 7) // 8)]
                NU = 4 * len(chunks)
                with nc.Block() as block:
                    @block.sync
                    def _(sp):
                        sp.sem_clear(N.range)
                        stream_raw(sp, src2, u0, u0 + NU)

                    @block.gpsimd
                    def _(pool):
                        if norm:
                            norm.even(pool)
                        for k in range(0, KT, 2):
                            pool.wait_ge(S.res_scaled, k + 1)
                            nc.gpsimd.tensor_tensor(X[:, k, 0:L], X[:, k, 0:L], sq[:, k, :], O.add)\
                                .then_inc(S.res_even, 1)

                    @block.tensor
                    def _(pe):
                        def square_sum(k):
                            pe.wait_ge(S.res_squares, k + 1)
                            ins = nc.tensor.matmul(PS[:, 0, :], ones, sq[:, k, :], start=(k == 0), stop=(k == KT - 1))
                            if k == KT - 1:
                                ins.then_inc(S.res_sums, 1)

                        if norm:
                            norm.sums(pe)
                        for v, ks in enumerate(chunks):
                            for m in range(4):
                                u = u0 + 4 * v + m
                                pe.wait_ge(w_split, u + 1)
                                wh, wl = [x.rearrange("p (k n) -> p k n", k=8) for x in (high(u), low(u))]
                                for k in ks:
                                    if src and m == 0:
                                        pe.wait_ge(S.normed, k + 1)
                                    if norm and m == 0:
                                        norm.tile(pe, k)
                                    for h in range(2):
                                        hs = slice(h * P, (h + 1) * P)
                                        last = product3(PS[:, 2 * m + h, :], wh[:, k % 8, hs], wl[:, k % 8, hs],
                                                        ah[k % 8], al[k % 8], k == 0, k == nk - 1)
                                    if m == 3 and k < ks[-1]:
                                        last.then_inc(S.mixed, 1)
                                last.then_inc(S.pe_tile, 1)
                                if v == len(chunks) - 1 and m:
                                    square_sum(2 * m - 2)
                                    square_sum(2 * m - 1)
                        square_sum(6)
                        square_sum(7)
                        for k in range(KT):
                            pe.wait_ge(S.res_next, k + 1)
                            nc.tensor.matmul(PS[:, 6, :], ones, sq[:, k, :], start=(k == 0), stop=(k == KT - 1))

                    @block.scalar
                    def _(act):
                        def split_chunk(v):
                            for k in chunks[v]:
                                if v:
                                    if k % 8 < 7:
                                        act.wait_ge(S.mixed, 7 * (v - 1) + k % 8 + 1)
                                    else:
                                        act.wait_ge(S.pe_tile, 4 * v)
                                nc.scalar.activation(ah[k % 8], src[k], A.Copy).then_inc(S.copied, 1)

                        if norm:
                            norm.squares(act)
                            norm.high(act)
                        if src:
                            split_chunk(0)
                        def empty(m):
                            act.wait_ge(S.pe_tile, NU - 3 + m)
                            nc.scalar.activation(fbuf[:, 2 * m:2 * m + 2, :], PS[:, 2 * m:2 * m + 2, :], A.Copy)\
                                .then_inc(S.act_out, 1)
                            act.wait_ge(S.act_out, m + 1)
                            for k in (2 * m, 2 * m + 1):
                                nc.scalar.activation(sq[:, k, :], fbuf[:, k, :], A.Square).then_inc(S.res_squares, 1)

                        for i in range(NU):
                            split_high(act, S, u0, u0 + i + 1)
                            if src and i % 4 == 3 and i + 1 < NU:
                                split_chunk(i // 4 + 1)
                            if i > NU - 4:
                                empty(i - 1 - (NU - 4))
                        empty(3)
                        act.wait_ge(S.res_sums, 1)
                        nc.scalar.activation(rstd[:, 0, :], PS[:, 0, :], A.Sqrt, bias=const("eps")[:, 1:2],
                                             scale=1.0 / D).then_inc(S.res_root, 1)
                        for k in range(KT):
                            act.wait_ge(S.res_odd if k % 2 else S.res_even, k // 2 + 1)
                            nc.scalar.activation(sq[:, k, :], X[:, k, 0:L], A.Square).then_inc(S.res_next, 1)

                    @block.vector
                    def _(dve):
                        def split_chunk(v):
                            for k in chunks[v]:
                                dve.wait_ge(S.copied, k + 1)
                                nc.vector.tensor_tensor(al[k % 8], src[k], ah[k % 8].bitcast(f32), O.subtract)\
                                    .then_inc(S.normed, 1)

                        if norm:
                            norm.scale(dve)
                        if src:
                            split_chunk(0)
                        for i in range(NU):
                            split_low(dve, u0 + i + 1)
                            if src and i % 4 == 3 and i + 1 < NU:
                                split_chunk(i // 4 + 1)

                        def add(k):
                            if k % 2:
                                dve.wait_ge(S.res_scaled, k + 1)
                                nc.vector.tensor_tensor(X[:, k, 0:L], X[:, k, 0:L], sq[:, k, :], O.add)\
                                    .then_inc(S.res_odd, 1)

                        dve.wait_ge(S.res_root, 1)
                        nc.vector.reciprocal(rstd[:, 0, :], rstd[:, 0, :]).then_inc(S.res_step, 1)
                        dve.wait_ge(S.res_step, 1)
                        for k in range(KT):
                            nc.vector.scalar_tensor_tensor(sq[:, k, :], fbuf[:, k, :], gain(k), rstd[:, 0, :],
                                                           O.mult, O.mult).then_inc(S.res_scaled, 1)
                            if k:
                                add(k - 1)
                        add(KT - 1)

            def stage_up(groups):
                S, N = stage_sems()
                norm = Normalise(S, groups, summed=True)
                u0 = U2["up"]
                with nc.Block() as block:
                    @block.sync
                    def _(sp):
                        sp.sem_clear(N.range)
                        stream_raw(sp, src2, u0, u0 + FT)

                    @block.gpsimd
                    def _(pool):
                        norm.even(pool)

                    @block.tensor
                    def _(pe):
                        norm.sums(pe)
                        for j in range(FT):
                            pe.wait_ge(w_split, u0 + j + 1)
                            if j >= 4:
                                pe.wait_ge(S.dve_out, j - 3)
                            wh, wl = [v.rearrange("p (k n) -> p k n", k=KT) for v in (high(u0 + j), low(u0 + j))]
                            for h in range(2):
                                hs = slice(h * P, (h + 1) * P)
                                for k in range(KT):
                                    if j + h == 0:
                                        norm.tile(pe, k)
                                    last = product3(PS[:, 2 * (j % 4) + h, :], wh[:, k, hs], wl[:, k, hs],
                                                    ah[k], al[k], k == 0, k == KT - 1)
                            last.then_inc(S.pe_tile, 1)

                    @block.scalar
                    def _(act):
                        norm.squares(act)
                        norm.high(act)
                        for j in range(FT):
                            split_high(act, S, u0, u0 + j + 1)
                            act.wait_ge(S.pe_tile, j + 1)
                            if j >= 2:
                                act.wait_ge(S.ready, j - 1)
                            for h in range(2):
                                last = nc.scalar.activation(hc[:, j % 2, h, :], PS[:, 2 * (j % 4) + h, :], A.Identity,
                                                            bias=vec2("cb", 2 * j + h),
                                                            scale=vec2("cw", 3 * (2 * j + h) + 2))
                            last.then_inc(S.act_out, 1)
                            act.wait_ge(S.dve_out, j + 1)
                            nc.scalar.activation(hc[:, j % 2, 0, :], hc[:, j % 2, 0, :], A.Silu)\
                                .then_inc(S.act_step, 1)

                    @block.vector
                    def _(dve):
                        norm.scale(dve)
                        for j in range(FT):
                            split_low(dve, u0 + j + 1)
                            dve.wait_ge(S.act_out, j + 1)
                            for s in (1, 2):
                                for h in range(2):
                                    b = hc[:, j % 2, h, s:L]
                                    last = nc.vector.scalar_tensor_tensor(
                                        b, PS[:, 2 * (j % 4) + h, 0:L - s], vec2("cw", 3 * (2 * j + h) + 2 - s), b,
                                        O.mult, O.add)
                                last.then_inc(S.dve_step if s == 1 else S.dve_out, 1)
                                if s == 1:
                                    dve.wait_ge(S.dve_step, j + 1)
                            dve.wait_ge(S.act_step, j + 1)
                            nc.vector.tensor_tensor(hid[:, j, :], hc[:, j % 2, 0, :], hc[:, j % 2, 1, :], O.mult)\
                                .then_inc(S.ready, 1)

            def stage_ple(groups):
                S, N = stage_sems()
                norm = Normalise(S, groups, summed=True)
                u0 = U2["pleg"]
                with nc.Block() as block:
                    @block.sync
                    def _(sp):
                        sp.sem_clear(N.range)
                        sp.dma_start(pT, d["pT"][layer, :, :].rearrange("p (k t) -> p k t", k=2)).then_inc(S.load, 16)
                        stream_raw(sp, src2, u0, u0 + 5)
                        sp.wait_ge(S.load, 16)

                    @block.gpsimd
                    def _(pool):
                        norm.even(pool)

                    @block.tensor
                    def _(pe):
                        norm.sums(pe)
                        for m in range(4):
                            pe.wait_ge(w_split, u0 + m + 1)
                            wh, wl = [v.rearrange("p (k n) -> p k n", k=8) for v in (high(u0 + m), low(u0 + m))]
                            for h in range(2):
                                hs = slice(h * P, (h + 1) * P)
                                for k in range(KT):
                                    if m + h == 0:
                                        norm.tile(pe, k)
                                    last = product3(PS[:, 2 * m + h, :], wh[:, k, hs], wl[:, k, hs], ah[k], al[k],
                                                    k == 0, k == KT - 1)
                            last.then_inc(S.pe_tile, 1)
                        pe.wait_ge(w_arrived[(u0 + 4) % RAW], 16 * ((u0 + 4) // RAW + 1))
                        pe.wait_ge(S.load, 16)
                        w = raw(u0 + 4).rearrange("p (k n) -> p k n", k=2)
                        for j in range(KT):
                            pe.wait_ge(S.act_out, j // 2 + 1)
                            for k in range(2):
                                last = nc.tensor.matmul(PS[:, j, :], w[:, k, j * P:(j + 1) * P], pT[:, k, :],
                                                        start=(k == 0), stop=(k == 1))
                            last.then_inc(S.mixed, 1)

                    @block.scalar
                    def _(act):
                        norm.squares(act)
                        norm.high(act)
                        for m in range(4):
                            split_high(act, S, u0, u0 + m + 1)
                            act.wait_ge(S.pe_tile, m + 1)
                            nc.scalar.activation(pg[:, 2 * m:2 * m + 2, :], PS[:, 2 * m:2 * m + 2, :], A.Sigmoid)\
                                .then_inc(S.act_out, 1)

                    @block.vector
                    def _(dve):
                        norm.scale(dve)
                        for m in range(4):
                            split_low(dve, u0 + m + 1)
                        for j in range(KT):
                            dve.wait_ge(S.mixed, j + 1)
                            nc.vector.tensor_tensor(pg[:, j, :], pg[:, j, :], PS[:, j, :], O.mult)\
                                .then_inc(S.dve_out, 1)
                            dve.wait_ge(S.dve_out, j + 1)
                            nc.vector.tensor_tensor(xt[j], xt[j], pg[:, j, :], O.add)

            stage_loads()
            stage_in2([(xt, lambda k: vec2("pre_mix", k))])
            stage_compress()
            cos2, sin2 = const2("cos2"), const2("sin2")
            stage_rope([(q2[:, j, :], cos2, sin2, L) for j in range(NT4)]
                       + [(ksw[:, s, :], cos2, sin2, L) for s in range(2)]
                       + [(kcT, const2("cosc"), const2("sinc"), 64)], const("r2"), arena2[:, scratch_at:scratch_at + L])
            stage_gmlp_and_cmp_attention()
            stage_attention()
            yt = [y2[:, k, :] for k in range(KT)]
            stage_project("wo", KT, lambda k: vec2("post_mix", k), groups=[(yt[0:4], lambda k: vec2("attn_g", k)),
                                            (yt[4:8], lambda k: vec2("mlp_g", k))])
            stage_up([(xt, lambda k: vec2("pre_ffn", k))])
            stage_project("down", FT, lambda k: vec2("post_ffn", k), [hid[:, k, :] for k in range(FT)])
            stage_ple([(xt, lambda k: vec2("ple_g", k))])

        S, N = stage_sems()
        with nc.Block() as block:
            @block.sync
            def _(sp):
                sp.sem_clear(N.range)
                sp.dma_start(cg, d["cg"]).then_inc(S.load, 16)
                sp.wait_ge(S.load, 16)
        before = turn[0]
        with nc.Fori(0, 2) as layer:
            layer2(layer)
            if (turn[0] - before) % 2:
                S, N = stage_sems()
                with nc.Block() as block:
                    @block.sync
                    def _(sp):
                        sp.sem_clear(N.range)
        S, N = stage_sems()
        with nc.Block() as block:
            @block.sync
            def _(sp):
                sp.dma_start(d["out"], X[:, :, 0:L]).then_inc(S.store, 16)
                sp.wait_ge(S.store, 16)


HEAD_COLUMNS = np.concatenate([np.arange(HD) + HD * h for t in range(NT4) for h in (t, t + 4)])


def ktiles(w):
    return w.reshape(-1, P, w.shape[1]).transpose(1, 0, 2)


def units_of(w):
    return w.reshape(KT, P, -1, 256).transpose(2, 1, 0, 3).reshape(-1, P, UNIT)


def vec(v):
    return v.reshape(-1, P).T


def partner(halves):
    r = np.zeros((P, P), np.float32)
    for h in range(2):
        for start, half in halves:
            for i in range(half):
                a, b = h * HD + start + i, h * HD + start + half + i
                r[b, a] = -1.0
                r[a, b] = 1.0
    return r


def constants():
    c = np.zeros((P, NCF), np.float32)
    c2 = np.zeros((P, NCG), np.float32)

    def put(name, v):
        if name in CF:
            c[:, CF[name][0]:CF[name][1]] = v
        else:
            c2[:, CG[name][0]:CG[name][1]] = v

    i = np.arange(P)
    put("ident", np.eye(P))
    put("ones", 1.0)
    put("r1", partner([(0, 16), (32, 16)]))
    put("r2", partner([(0, 8)]))
    put("tri", i[:, None] <= i[None, :])
    inv = (np.float32(500000.0) ** (-np.arange(8, dtype=np.float32) / 8)).astype(np.float32)

    def table(pos):
        ang = np.zeros((HD, len(pos)), np.float32)
        ang[0:16] = np.tile(inv, 2)[:, None] * pos.astype(np.float32)[None, :]
        return np.tile(np.cos(ang), (2, 1)), np.tile(np.sin(ang), (2, 1))

    cs, sn = table(np.arange(L))
    put("cos2", cs)
    put("sin2", sn)
    cp = np.arange(32) * 16 + 31
    cs, sn = table(np.concatenate([cp, cp]))
    put("cosc", cs)
    put("sinc", sn)
    put("fold", np.tile(np.eye(64), (2, 1)))
    put("reset", (np.arange(L) % P != 0)[None, :])
    put("one", 1.0)
    put("eps", np.array([LN_EPS, RMS_EPS])[None, :])
    f = (np.float32(10000.0) ** (-np.arange(16, dtype=np.float32) / 16)).astype(np.float32)
    t = np.arange(L)
    ang = np.concatenate([np.tile(f, 2)[:, None] * (t // 64).astype(np.float32)[None, :],
                          np.tile(f, 2)[:, None] * (t % 64).astype(np.float32)[None, :]])
    ca = np.concatenate([np.tile(np.cos(ang), (2, 1)), np.tile(np.sin(ang), (2, 1))], axis=1).astype(np.float32)
    b = np.zeros((P, NCB), np.float32)

    def putb(name, v):
        b[:, CB[name][0]:CB[name][1]] = v

    putb("ident", np.eye(P))
    putb("up", np.where(i[None, :] > i[:, None], NEG, 0))
    putb("low", np.where(i[None, :] < i[:, None], NEG, 0))
    cm = np.zeros((P, NB, 32), np.float32)
    for n in range(NB):
        ok = (cp[None, :] <= n * P + i[:, None]) & (np.arange(32)[None, :] < NCMP)
        cm[:, n] = np.where(ok, 0, NEG)
    putb("cmp", cm.reshape(P, -1))
    m = np.zeros((2, 8, P, P), np.float32)
    for lev in range(LEV):
        B = 1 << lev
        same = (i[:, None] // (2 * B)) == (i[None, :] // (2 * B))
        left, right = (i // B) % 2 == 0, (i // B) % 2 == 1
        m[0, lev] = same & left[:, None] & right[None, :]
        m[1, lev] = same & right[:, None] & left[None, :]
    m[:, 7] = np.eye(P)
    putb("scan", m.transpose(2, 0, 1, 3).reshape(P, -1))
    return c, c2, b, ca


def layout(i):
    f = {k: np.asarray(v) for k, v in i.items()}
    out = {}
    out["xT"] = np.ascontiguousarray(f["x"][0].T.reshape(KT, P, L).transpose(1, 0, 2))
    out["ctxT"] = np.ascontiguousarray(f["ctx"][0].T.reshape(KT, P, LC).transpose(1, 0, 2))
    v = np.zeros((P, NV1), np.float32)
    for name, a in [("c", f["c"][0]), ("cc", f["c_ctx"]), ("b_ada0", f["b_ada"][0]), ("b_ada1", f["b_ada"][1]),
                    ("ln_g0", f["ln_g"][0]), ("ln_b0", f["ln_b"][0]), ("ln_g1", f["ln_g"][1]),
                    ("ln_b1", f["ln_b"][1]), ("conv", f["conv_ab"][0].reshape(-1)), ("gnorm", f["gnorm_c"][0])]:
        v[:, V1[name][0]:V1[name][1]] = vec(a)
    out["v1"] = v
    out["sink"] = np.ascontiguousarray(np.broadcast_to(f["sink_ab"][0][None, :], (P, NH)))
    w = f["w_in_ab"][0]
    q, k, vv, ga, xb, bg, cg, gb = np.split(w, np.cumsum([512, 128, 128, 512, 512, 512, 512]), axis=1)
    ab_in = np.concatenate([q[:, HEAD_COLUMNS], k, vv, ga[:, HEAD_COLUMNS], xb, cg, gb, bg], axis=1)
    wo = f["w_out_ab"][0]
    ab_out = np.concatenate([wo[0:512][HEAD_COLUMNS], wo[512:]], axis=0)
    w = f["w_in_c"][0]
    parts = np.split(w, 5, axis=1)
    tiles = [(0, 0), (0, 1), (3, 0), (3, 1), (1, 0), (2, 0), (4, 0), (4, 1), (1, 1), (2, 1)]
    c_in = np.concatenate([parts[x][:, 256 * p + P * h:256 * p + P * h + P] for p in range(4) for x, h in tiles],
                          axis=1)
    out["wc"] = np.concatenate([w.reshape(KT, P, -1, P).transpose(2, 1, 0, 3).reshape(-1, P, HALF)
                                for w in (c_in, f["w_out_c"][0])])
    out["w1"] = np.concatenate([units_of(x) for x in (f["w_ada"][0], f["w_ada"][1], ab_in, ab_out)])
    seg, v2, r2, wsT, wg, pT = [], [], [], [], [], []
    for l in range(2):
        g = {k[:-2]: v[l] for k, v in f.items() if k.endswith("_2")}
        w = g["w_in"]
        q, kc, vc, ks, vs, kw, vw, zg, zu, zv = np.split(
            w, np.cumsum([512, 128, 128, 128, 128, 128, 128, 24, 512]), axis=1)
        win = np.concatenate([q[:, HEAD_COLUMNS], kc[:, :64], vc[:, :64], kc[:, 64:], vc[:, 64:], ks, kw, vs, vw,
                              zu, zv], axis=1)
        c1 = g["cmp_w1"].reshape(2, 4, 8, HD, 256).transpose(1, 0, 3, 2, 4).reshape(4, P, UNIT)
        wo = np.concatenate([g["w_o"][0:512][HEAD_COLUMNS], g["w_o"][512:]], axis=0)
        up = g["w_up"].reshape(D, 2, FT, P).transpose(0, 2, 1, 3).reshape(D, -1)
        dn = np.concatenate([g["w_down"], np.zeros((24 * P - FF, D), np.float32)])
        dn = dn.reshape(3, 8, P, 4, 256).transpose(0, 3, 2, 1, 4).reshape(12, P, UNIT)
        pj = ktiles(g["w_ple_proj"]).reshape(1, P, UNIT)
        seg.append(np.concatenate([units_of(win), c1, units_of(wo), units_of(up), dn, units_of(g["w_ple_gate"]), pj]))
        a = np.zeros((P, NV2), np.float32)
        for name, x in [("pre_mix", vec(g["pre_mix_g"])), ("b1", vec(g["cmp_b1"].reshape(-1))),
                        ("pe", g["cmp_pe"].transpose(0, 2, 1).reshape(P, 32)),
                        ("b2k", np.tile(g["cmp_b2"][0], 2)[:, None]),
                        ("attn_g", vec(g["attn_out_g"][HEAD_COLUMNS])), ("mlp_g", vec(g["mlp_out_g"])),
                        ("post_mix", vec(g["post_mix_g"])), ("pre_ffn", vec(g["pre_ffn_g"])),
                        ("cw", g["conv_w"].reshape(3, 2, FT, P).transpose(3, 2, 1, 0).reshape(P, -1)),
                        ("cb", g["conv_b"].reshape(2, FT, P).transpose(2, 1, 0).reshape(P, -1)),
                        ("post_ffn", vec(g["post_ffn_g"])), ("ple_g", vec(g["ple_norm_g"]))]:
            a[:, V2[name][0]:V2[name][1]] = x
        v2.append(a)
        r = np.zeros((P, NR2), np.float32)
        for name, x in [("ln_g", g["gmlp_ln_g"][None]), ("ln_b", g["gmlp_ln_b"][None]), ("b2v", g["cmp_b2"][1][None]),
                        ("bs", np.repeat(g["gmlp_bs"].reshape(NT4, 2, P).transpose(1, 0, 2).reshape(2, -1), HD, axis=0)),
                        ("w2k", np.concatenate([ktiles(g["cmp_w2"][0])] * 2, axis=2).reshape(P, -1)),
                        ("w2v", ktiles(g["cmp_w2"][1]).reshape(P, -1))]:
            r[:, R2[name][0]:R2[name][1]] = x
        r2.append(r)
        wsT.append(g["gmlp_ws"].transpose(2, 0, 1).reshape(P, -1))
        wg.append(ktiles(zg).reshape(P, -1))
        pT.append(g["p"][0].T.reshape(2, P, L).transpose(1, 0, 2).reshape(P, -1))
    out["w2"] = np.stack(seg)
    out["v2"], out["r2"], out["wsT"], out["wgate"], out["pT"] = (np.stack(x) for x in (v2, r2, wsT, wg, pT))
    out["cf"], out["cg"], out["cb"], out["ca"] = constants()
    return {k: np.ascontiguousarray(v) for k, v in out.items()}


def kernel(**inputs):
    import numpy as _np
    import concourse.bacc as _bacc
    from concourse import mybir as _mybir
    from concourse.bass_utils import run_bass_kernel_spmd as _run

    nc = _bacc.Bacc("TRN2", target_bir_lowering=False, num_devices=1)
    arrays = layout(inputs)
    d = {n: nc.dram_tensor(n + "_dram", a.shape, _mybir.dt.from_np(a.dtype), kind="ExternalInput").ap()
         for n, a in arrays.items()}
    d["out"] = nc.dram_tensor("out_dram", (P, KT, L), _mybir.dt.float32, kind="ExternalOutput").ap()
    program(nc, d)
    r = _run(nc, [{n + "_dram": a for n, a in arrays.items()}], core_ids=[0])
    o = r.results[0]["out_dram"]
    return _np.ascontiguousarray(o.transpose(2, 1, 0).reshape(1, L, D))
```
